# Optimizing a Trainium2 kernel written in Bass

```python
import jax, jax.numpy as jnp
from jax import lax
import numpy as np
import math

D_MODEL = 1024
BATCH = 1
SEQ = 512
DEPTH = 2

GRID_W = 64
HEAD_DIM = 64
A_HEADS = 8
A_KV_HEADS = 2
A_GROUPS = A_HEADS // A_KV_HEADS
Q_BLOCK = 128
ROPE_THETA = 10000.0
POOL_WINDOWS = (2, 4, 8, 16)
POOL_GROUP = 128
POOL_WIDTH = POOL_GROUP * len(POOL_WINDOWS)
C_HEADS = 8
NA_ROWS = 8
NA_COLS = 16
A_Q = A_HEADS * HEAD_DIM
A_KV = A_KV_HEADS * HEAD_DIM
C_W = C_HEADS * HEAD_DIM
N_BRANCH = 3
BRANCH_WIDTH = 512
IN_WIDTHS = (A_Q, A_KV, A_KV, POOL_WIDTH, C_W, C_W, C_W, N_BRANCH * D_MODEL)
D_IN = sum(IN_WIDTHS)
D_FF = 2816
CONV_W = 3
EPS = 1e-6


def rmsnorm(x, g):
    xf = x.astype(jnp.float32)
    y = xf * lax.rsqrt(jnp.mean(xf * xf, axis=-1, keepdims=True) + EPS)
    return (y * g.astype(jnp.float32)).astype(x.dtype)

def rope_axis(x, pos):
    dim = x.shape[-1]
    half = dim // 2
    freqs = ROPE_THETA ** (-jnp.arange(0, dim, 2, dtype=jnp.float32) / dim)
    ang = pos.astype(jnp.float32)[:, None] * freqs[None, :]
    cos = jnp.cos(ang)[:, None, :]
    sin = jnp.sin(ang)[:, None, :]
    xf = x.astype(jnp.float32)
    x1, x2 = xf[..., :half], xf[..., half:]
    out = jnp.concatenate([x1 * cos - x2 * sin, x1 * sin + x2 * cos], axis=-1)
    return out.astype(x.dtype)

def rope_2d(x, row, col):
    half = x.shape[-1] // 2
    return jnp.concatenate([rope_axis(x[..., :half], row), rope_axis(x[..., half:], col)], axis=-1)

def global_axial_attention(q, k, v, gq, gk):
    B, S = q.shape[0], q.shape[1]
    t = jnp.arange(S)
    row, col = t // GRID_W, t % GRID_W
    q = rmsnorm(q.reshape(B, S, A_HEADS, HEAD_DIM), gq)
    k = rmsnorm(k.reshape(B, S, A_KV_HEADS, HEAD_DIM), gk)
    v = v.reshape(B, S, A_KV_HEADS, HEAD_DIM)
    q = rope_2d(q, row, col) * (HEAD_DIM ** -0.5)
    k = rope_2d(k, row, col)
    nb = S // Q_BLOCK
    qb = q.reshape(B, nb, Q_BLOCK, A_KV_HEADS, A_GROUPS, HEAD_DIM).transpose(1, 0, 2, 3, 4, 5)

    def block(qi):
        s = jnp.einsum('bqkgd,bskd->bkgqs', qi, k).astype(jnp.float32)
        p = jax.nn.softmax(s, axis=-1)
        return jnp.einsum('bkgqs,bskd->bqkgd', p.astype(v.dtype), v)

    o = lax.map(block, qb)
    return o.transpose(1, 0, 2, 3, 4, 5).reshape(B, S, A_Q)

def pool_mixer(u, w_pool, pool_scale):
    B, S = u.shape[0], u.shape[1]
    uf = u.astype(jnp.float32)
    cs = jnp.concatenate([jnp.zeros((B, 1, POOL_WIDTH), jnp.float32), jnp.cumsum(uf, axis=1)], axis=1)
    t = jnp.arange(S)
    outs = []
    for g, w in enumerate(POOL_WINDOWS):
        sl = slice(g * POOL_GROUP, (g + 1) * POOL_GROUP)
        lo = jnp.clip(t - w // 2, 0, S)
        hi = jnp.clip(t + w - w // 2, 0, S)
        csg = cs[..., sl]
        mean = (csg[:, hi] - csg[:, lo]) / (hi - lo).astype(jnp.float32)[None, :, None]
        diff = (mean - uf[..., sl]).astype(u.dtype)
        outs.append(jnp.einsum('bsc,cd->bsd', diff, w_pool[g]))
    return jnp.concatenate(outs, axis=-1) * pool_scale

def neighbourhood_attention(q, k, v, rpb):
    B, S = q.shape[0], q.shape[1]
    rows = S // GRID_W
    win_r = min(NA_ROWS, rows)
    qg = q.reshape(B, rows, GRID_W, C_HEADS, HEAD_DIM) * (HEAD_DIM ** -0.5)
    kg = k.reshape(B, rows, GRID_W, C_HEADS, HEAD_DIM)
    vg = v.reshape(B, rows, GRID_W, C_HEADS, HEAD_DIM)
    col = jnp.arange(GRID_W)
    col_start = jnp.clip(col - NA_COLS // 2, 0, GRID_W - NA_COLS)
    col_idx = col_start[:, None] + jnp.arange(NA_COLS)[None, :]
    dc = col_idx - col[:, None] + (NA_COLS - 1)

    def row_block(args):
        r, q_row = args
        rs = jnp.clip(r - win_r // 2, 0, rows - win_r)
        k_rows = lax.dynamic_slice_in_dim(kg, rs, win_r, axis=1)
        v_rows = lax.dynamic_slice_in_dim(vg, rs, win_r, axis=1)
        k_nb = k_rows[:, :, col_idx]
        v_nb = v_rows[:, :, col_idx]
        dr = rs + jnp.arange(win_r) - r + (NA_ROWS - 1)
        bias = rpb[:, dr[None, :, None], dc[:, None, :]]
        s = jnp.einsum('bqhd,brqjhd->bhqrj', q_row, k_nb).astype(jnp.float32)
        s = s + bias.astype(jnp.float32)[None]
        p = jax.nn.softmax(s.reshape(B, C_HEADS, GRID_W, win_r * NA_COLS), axis=-1)
        p = p.reshape(B, C_HEADS, GRID_W, win_r, NA_COLS).astype(v.dtype)
        return jnp.einsum('bhqrj,brqjhd->bqhd', p, v_nb)

    o = lax.map(row_block, (jnp.arange(rows), qg.transpose(1, 0, 2, 3, 4)))
    return o.transpose(1, 0, 2, 3, 4).reshape(B, S, C_W)

def conv_gated_mlp(h, w_up, conv_w, conv_b, w_down):
    up = jnp.einsum('bsd,df->bsf', h, w_up)
    pad = jnp.pad(up, ((0, 0), (1, 1), (0, 0)))
    up = pad[:, :-2] * conv_w[0] + pad[:, 1:-1] * conv_w[1] + pad[:, 2:] * conv_w[2] + conv_b
    val, gate = up[..., :D_FF], up[..., D_FF:]
    return jnp.einsum('bsf,fd->bsd', jax.nn.gelu(gate, approximate=True) * val, w_down)

def first_inputs(seed: int = 0) -> dict:
    key = jax.random.key(seed)
    ks = jax.random.split(key, 20)
    n = lambda k, shape, s: jax.random.normal(k, shape, jnp.float32) * s
    L, D = DEPTH, D_MODEL
    return {
        "x": n(ks[0], (BATCH, SEQ, D), 1.0),
        "norm_mix_pre": 1.0 + n(ks[1], (L, D), 0.1),
        "norm_mix_post": 1.0 + n(ks[2], (L, D), 0.1),
        "norm_ffn_pre": 1.0 + n(ks[3], (L, D), 0.1),
        "norm_ffn_post": 1.0 + n(ks[4], (L, D), 0.1),
        "w_in": n(ks[5], (L, D, D_IN), D ** -0.5),
        "b_gate": n(ks[6], (L, N_BRANCH * D), 0.1),
        "qk_norm_q": 1.0 + n(ks[7], (L, HEAD_DIM), 0.1),
        "qk_norm_k": 1.0 + n(ks[8], (L, HEAD_DIM), 0.1),
        "w_pool": n(ks[9], (L, len(POOL_WINDOWS), POOL_GROUP, POOL_GROUP), POOL_GROUP ** -0.5),
        "pool_scale": 1.0 + n(ks[10], (L, POOL_WIDTH), 0.1),
        "rpb": n(ks[11], (L, C_HEADS, 2 * NA_ROWS - 1, 2 * NA_COLS - 1), 0.5),
        "w_branch": n(ks[12], (L, N_BRANCH, BRANCH_WIDTH, D), BRANCH_WIDTH ** -0.5),
        "w_out": n(ks[13], (L, D, D), D ** -0.5),
        "w_up": n(ks[14], (L, D, 2 * D_FF), D ** -0.5),
        "conv_w": n(ks[15], (L, CONV_W, 2 * D_FF), CONV_W ** -0.5),
        "conv_b": n(ks[16], (L, 2 * D_FF), 0.01),
        "w_down": n(ks[17], (L, D_FF, D), D_FF ** -0.5),
    }

def first_block(x, norm_mix_pre, norm_mix_post, norm_ffn_pre, norm_ffn_post, w_in, b_gate,
              qk_norm_q, qk_norm_k, w_pool, pool_scale, rpb, w_branch, w_out,
              w_up, conv_w, conv_b, w_down):
    B, S = x.shape[0], x.shape[1]
    splits = [int(s) for s in np.cumsum(IN_WIDTHS)[:-1]]
    for l in range(DEPTH):
        h = rmsnorm(x, norm_mix_pre[l])
        proj = jnp.einsum('bsd,de->bse', h, w_in[l])
        qa, ka, va, pu, qc, kc, vc, gl = jnp.split(proj, splits, axis=-1)
        ya = global_axial_attention(qa, ka, va, qk_norm_q[l], qk_norm_k[l])
        yb = pool_mixer(pu, w_pool[l], pool_scale[l])
        yc = neighbourhood_attention(qc, kc, vc, rpb[l])
        ys = jnp.stack([ya, yb, yc], axis=2)
        z = jnp.einsum('bsnc,ncd->bsnd', ys, w_branch[l])
        gates = jax.nn.sigmoid(gl + b_gate[l]).reshape(B, S, N_BRANCH, D_MODEL)
        merged = jnp.sum(gates * z, axis=2)
        mix = jnp.einsum('bsd,de->bse', merged, w_out[l])
        x = x + rmsnorm(mix, norm_mix_post[l])
        h = rmsnorm(x, norm_ffn_pre[l])
        f = conv_gated_mlp(h, w_up[l], conv_w[l], conv_b[l], w_down[l])
        x = x + rmsnorm(f, norm_ffn_post[l])
    return x


N_A = DEPTH // 2
N_B = DEPTH - N_A
CONV_WIDTH = 31
FFN_CONV_WIDTH = 3
N_HEADS = 8
HEAD_DIM_2 = D_MODEL // N_HEADS
WINDOWS = (128, 512, 2048)
DILATIONS = (1, 4, 16)
N_GROUPS = len(WINDOWS)
Q_WIDTH = N_GROUPS * N_HEADS * HEAD_DIM_2
BLOCK = 128
NEG_INF = -1e30


def rms_norm(x, g):
    xf = x.astype(jnp.float32)
    y = xf * lax.rsqrt(jnp.mean(xf * xf, axis=-1, keepdims=True) + EPS)
    return (y * g.astype(jnp.float32)).astype(x.dtype)

def layer_norm(x, g, b):
    xf = x.astype(jnp.float32)
    mu = jnp.mean(xf, axis=-1, keepdims=True)
    var = jnp.mean(jnp.square(xf - mu), axis=-1, keepdims=True)
    y = (xf - mu) * lax.rsqrt(var + EPS)
    return (y * g.astype(jnp.float32) + b.astype(jnp.float32)).astype(x.dtype)

def causal_dwconv(x, w, b):
    k, c = w.shape
    y = lax.conv_general_dilated(
        x, w[:, None, :].astype(x.dtype), window_strides=(1,), padding=[(k - 1, 0)],
        dimension_numbers=("NWC", "WIO", "NWC"), feature_group_count=c)
    return y + b

def conformer_conv_module(h, w_in, b_in, dw, dw_b, ln_g, ln_b, w_out, b_out):
    u = h @ w_in + b_in
    u = u[..., :D_MODEL] * jax.nn.sigmoid(u[..., D_MODEL:])
    u = causal_dwconv(u, dw, dw_b)
    u = layer_norm(u, ln_g, ln_b)
    u = jax.nn.silu(u)
    return u @ w_out + b_out

def conv_ffn(h, w_in, dw, dw_b, w_out):
    u = causal_dwconv(h @ w_in, dw, dw_b)
    a, g = u[..., :D_FF], u[..., D_FF:]
    return (jax.nn.silu(g) * a) @ w_out

def dilated_branch(q, k, v, window, dil):
    b, s, h, dh = q.shape
    steps = window // dil
    assert steps <= BLOCK and s % dil == 0
    L = s // dil
    nblk = -(-L // BLOCK)
    lp = nblk * BLOCK

    def to_sub(t):
        t = t.reshape(b, L, dil, h, dh).transpose(0, 2, 3, 1, 4)
        return jnp.pad(t, ((0, 0), (0, 0), (0, 0), (0, lp - L), (0, 0)))

    qs, ks, vs = to_sub(q), to_sub(k), to_sub(v)
    q_blk = qs.reshape(b, dil, h, nblk, BLOCK, dh)

    def band(t):
        tp = jnp.pad(t, ((0, 0), (0, 0), (0, 0), (BLOCK, 0), (0, 0)))
        prev = tp[:, :, :, :lp].reshape(b, dil, h, nblk, BLOCK, dh)
        cur = tp[:, :, :, BLOCK:].reshape(b, dil, h, nblk, BLOCK, dh)
        return jnp.concatenate([prev, cur], axis=-2)

    k_band, v_band = band(ks), band(vs)
    scores = jnp.einsum("brhnqc,brhnkc->brhnqk", q_blk, k_band).astype(jnp.float32)
    scores = scores * (1.0 / math.sqrt(dh))

    blk_i = jnp.arange(nblk)[:, None, None]
    qi = jnp.arange(BLOCK)[None, :, None]
    kk = jnp.arange(2 * BLOCK)[None, None, :]
    dist = qi + BLOCK - kk
    key_pos = blk_i * BLOCK + kk - BLOCK
    valid = (dist >= 0) & (dist <= steps) & (key_pos >= 0)
    scores = jnp.where(valid, scores, NEG_INF)

    m = jnp.max(scores, axis=-1, keepdims=True)
    p = jnp.exp(scores - m)
    den = jnp.sum(p, axis=-1, keepdims=True)
    out = jnp.einsum("brhnqk,brhnkc->brhnqc", p.astype(v.dtype), v_band)
    out = out / den.astype(out.dtype)
    lse = (m + jnp.log(den))[..., 0]

    out = out.reshape(b, dil, h, lp, dh)[:, :, :, :L]
    out = out.transpose(0, 3, 1, 2, 4).reshape(b, s, h, dh)
    lse = lse.reshape(b, dil, h, lp)[:, :, :, :L]
    lse = lse.transpose(0, 3, 1, 2).reshape(b, s, h)
    return out, lse

def dilated_mixture_attention(h, w_q, w_o, k, v):
    b, s, _ = h.shape
    q = (h @ w_q).reshape(b, s, N_GROUPS, N_HEADS, HEAD_DIM_2)
    outs, lses = [], []
    for g in range(N_GROUPS):
        o, l = dilated_branch(q[:, :, g], k[:, :, g], v[:, :, g], WINDOWS[g], DILATIONS[g])
        outs.append(o)
        lses.append(l)
    outs = jnp.stack(outs, axis=0)
    wts = jax.nn.softmax(jnp.stack(lses, axis=0), axis=0)
    merged = jnp.sum(wts[..., None].astype(outs.dtype) * outs, axis=0)
    return merged.reshape(b, s, N_HEADS * HEAD_DIM_2) @ w_o

def second_inputs(seed: int = 0) -> dict:
    key = jax.random.key(seed)
    ks = iter(jax.random.split(key, 32))

    def nrm(shape, fan_in):
        return jax.random.normal(next(ks), shape, jnp.float32) * (fan_in ** -0.5)

    def gain(shape):
        return 1.0 + 0.02 * jax.random.normal(next(ks), shape, jnp.float32)

    def bias(shape):
        return 0.01 * jax.random.normal(next(ks), shape, jnp.float32)

    d = D_MODEL
    return {
        "x": jax.random.normal(next(ks), (BATCH, SEQ, d), jnp.float32),
        "mix_pre_g": gain((DEPTH, d)),
        "mix_post_g": gain((DEPTH, d)),
        "ffn_pre_g": gain((DEPTH, d)),
        "ffn_post_g": gain((DEPTH, d)),
        "cm_w_in": nrm((N_A, d, 2 * d), d),
        "cm_b_in": bias((N_A, 2 * d)),
        "cm_dw": nrm((N_A, CONV_WIDTH, d), CONV_WIDTH),
        "cm_dw_b": bias((N_A, d)),
        "cm_ln_g": gain((N_A, d)),
        "cm_ln_b": bias((N_A, d)),
        "cm_w_out": nrm((N_A, d, d), d),
        "cm_b_out": bias((N_A, d)),
        "kv_norm_g": gain((d,)),
        "w_kv": nrm((d, 2 * Q_WIDTH), d),
        "w_q": nrm((N_B, d, Q_WIDTH), d),
        "w_o": nrm((N_B, N_HEADS * HEAD_DIM_2, d), N_HEADS * HEAD_DIM_2),
        "ffn_w_in": nrm((DEPTH, d, 2 * D_FF), d),
        "ffn_dw": nrm((DEPTH, FFN_CONV_WIDTH, 2 * D_FF), FFN_CONV_WIDTH),
        "ffn_dw_b": bias((DEPTH, 2 * D_FF)),
        "ffn_w_out": nrm((DEPTH, D_FF, d), D_FF),
    }

def second_block(x, mix_pre_g, mix_post_g, ffn_pre_g, ffn_post_g,
              cm_w_in, cm_b_in, cm_dw, cm_dw_b, cm_ln_g, cm_ln_b, cm_w_out, cm_b_out,
              kv_norm_g, w_kv, w_q, w_o,
              ffn_w_in, ffn_dw, ffn_dw_b, ffn_w_out):
    b, s, _ = x.shape
    k_sh = v_sh = None
    for i in range(DEPTH):
        h = rms_norm(x, mix_pre_g[i])
        if i < N_A:
            y = conformer_conv_module(h, cm_w_in[i], cm_b_in[i], cm_dw[i], cm_dw_b[i],
                                      cm_ln_g[i], cm_ln_b[i], cm_w_out[i], cm_b_out[i])
        else:
            j = i - N_A
            y = dilated_mixture_attention(h, w_q[j], w_o[j], k_sh, v_sh)
        x = x + rms_norm(y, mix_post_g[i])
        h = rms_norm(x, ffn_pre_g[i])
        y = conv_ffn(h, ffn_w_in[i], ffn_dw[i], ffn_dw_b[i], ffn_w_out[i])
        x = x + rms_norm(y, ffn_post_g[i])
        if i == N_A - 1:
            kv = (rms_norm(x, kv_norm_g) @ w_kv).reshape(b, s, 2, N_GROUPS, N_HEADS, HEAD_DIM_2)
            k_sh, v_sh = kv[:, :, 0], kv[:, :, 1]
    return x


def setup_inputs(seed=0):
    out = dict(first_inputs(seed))
    for name, value in second_inputs(seed + 1).items():
        if name != "x":
            out[name + "_2"] = value
    return out


def reference(
    x, norm_mix_pre, norm_mix_post, norm_ffn_pre, norm_ffn_post, w_in, b_gate, qk_norm_q,
    qk_norm_k, w_pool, pool_scale, rpb, w_branch, w_out, w_up, conv_w, conv_b, w_down,
    mix_pre_g_2, mix_post_g_2, ffn_pre_g_2, ffn_post_g_2, cm_w_in_2, cm_b_in_2, cm_dw_2,
    cm_dw_b_2, cm_ln_g_2, cm_ln_b_2, cm_w_out_2, cm_b_out_2, kv_norm_g_2, w_kv_2, w_q_2, w_o_2,
    ffn_w_in_2, ffn_dw_2, ffn_dw_b_2, ffn_w_out_2,
):
    x = first_block(
        x, norm_mix_pre, norm_mix_post, norm_ffn_pre, norm_ffn_post, w_in, b_gate, qk_norm_q,
        qk_norm_k, w_pool, pool_scale, rpb, w_branch, w_out, w_up, conv_w, conv_b, w_down,
    )
    return second_block(
        x, mix_pre_g_2, mix_post_g_2, ffn_pre_g_2, ffn_post_g_2, cm_w_in_2, cm_b_in_2, cm_dw_2,
        cm_dw_b_2, cm_ln_g_2, cm_ln_b_2, cm_w_out_2, cm_b_out_2, kv_norm_g_2, w_kv_2, w_q_2,
        w_o_2, ffn_w_in_2, ffn_dw_2, ffn_dw_b_2, ffn_w_out_2,
    )


_drawn_inputs = setup_inputs


def setup_inputs(seed=0):
    import zlib

    import numpy as np

    out = dict(_drawn_inputs(seed))
    spreads = {}
    factors = {'qk_norm_q': 4.896,
     'qk_norm_k': 4.763,
     'conv_b': 3.844,
     'mix_pre_g_2': 4.662,
     'mix_post_g_2': 4.447,
     'ffn_pre_g_2': 3.653,
     'ffn_post_g_2': 5.204,
     'cm_b_in_2': 7.487,
     'cm_dw_b_2': 3.821,
     'cm_ln_g_2': 3.93,
     'cm_ln_b_2': 7.927,
     'cm_b_out_2': 4.112,
     'kv_norm_g_2': 5.83,
     'ffn_dw_b_2': 6.951}
    for name, (base, spread) in spreads.items():
        noise = np.random.default_rng([zlib.crc32(name.encode()), seed]).standard_normal(out[name].shape)
        drawn = base * np.exp(spread * noise) if base else spread * noise
        out[name] = __import__('jax').numpy.asarray(drawn.astype(out[name].dtype))
    for name, factor in factors.items():
        out[name] = (out[name] * factor).astype(out[name].dtype)
    return out
```

```python
from contextlib import ExitStack

import numpy as np

import concourse.bass as bass
from concourse import mybir

F32 = mybir.dt.float32
F32R = mybir.dt.float32r
ALU = mybir.AluOpType
ACT = mybir.ActivationFunctionType
AX = mybir.AxisListType

P = 128
T = 512
D = 1024
KT = D // P
D_IN = 5888
FF = 2816
FT = FF // P
EPS = 1e-6
NEG = -1e30
CH = 2048
CW = CH // KT
POOL_WINDOWS = (2, 4, 8, 16)
PAD = 8
TAPS = 31
GRID = 64
NA_COLS = 16
RPB_PAD = 64
E2C = 14 * GRID
SD = 128 ** -0.5

QA, KA, VA, PU, QC, KC, VC, GL = 0, 512, 640, 768, 1280, 1792, 2304, 2816

PLAN = []
for _l in range(2):
    PLAN += [(f"c_qkv{_l}", 6), (f"a_qkv{_l}", 3), (f"pu{_l}", 2), (f"merge{_l}", 18), (f"out{_l}", 4),
             (f"up{_l}", FT), (f"down{_l}", 12)]
PLAN += [("cm_in", 8), ("out2", 4), (f"up2", FT), ("down2", 12), ("d_qkv", 36), ("out3", 4), ("up3", FT), ("down3", 12)]
FIRST, DRAINS = {}, {}
_c = _d = 0
for _name, _n in PLAN:
    FIRST[_name], DRAINS[_name] = _c, _d
    _c += _n
    _d += 0 if _name.startswith("up") else _n
CHUNKS = _c

ROWS = {}
_r = 0
for _name, _n in [("norm_mix_pre", 16), ("norm_mix_post", 16), ("norm_ffn_pre", 16), ("norm_ffn_post", 16),
                  ("b_gate", 48), ("pool_scale", 8), ("qkg", 4), ("conv_w", 264), ("conv_b", 88),
                  ("mix_pre_g_2", 16), ("mix_post_g_2", 16), ("ffn_pre_g_2", 16), ("ffn_post_g_2", 16),
                  ("cm_b_in_2", 16), ("cm_dw_2", 248), ("cm_dw_b_2", 8), ("cm_ln_g_2", 8), ("cm_ln_b_2", 8),
                  ("cm_b_out_2", 8), ("kv_norm_g_2", 8), ("ffn_dw_2", 264), ("ffn_dw_b_2", 88)]:
    ROWS[_name] = (_r, _n)
    _r += _n
ROWS_ALL = _r
ROW_TILES = -(-ROWS_ALL // P)

STEPS = {"C0": 0, "A0": 32, "C1": 64, "A1": 96, "D": 128}
FLUSH = {"C0": 0, "A0": 16, "C1": 20, "A1": 36, "D": 40}
NORMS = ["pre0"]
for _h in range(8):
    if _h == 4:
        NORMS += ["ln_mean", "ln_var"]
    NORMS += [f"post{_h}"] + ([f"pre{_h + 1}"] if _h < 7 else [])
NORM = {n: i for i, n in enumerate(NORMS)}
SQUARES = {n: 8 * i for i, n in enumerate(n for n in NORMS if n != "ln_mean")}
SPLITS = ["pre0", "mg0", "pre1", "pre2", "mg1", "pre3", "pre4", "ln", "pre5", "pre6", "hq", "y", "pre7"]
SPLIT = {n: 8 * i for i, n in enumerate(SPLITS)}
SCALED = {n: 8 * i for i, n in enumerate(n for n in SPLITS if n[0] in "ph")}


def host_constants():
    ident = np.eye(P, dtype=np.float32)
    head = np.kron(np.eye(2), np.full((64, 64), 1 / 64)).astype(np.float32)
    mean = np.full((P, P), 1 / D, np.float32)
    rot = np.zeros((P, P), np.float32)
    for m in range(P):
        rot[m + 16 if m % 32 < 16 else m - 16, m] = -1.0 if m % 32 < 16 else 1.0
    t = np.arange(T)
    freqs = np.float32(10000.0) ** (-np.arange(0, 32, 2, dtype=np.float32) / np.float32(32))
    p = np.arange(P)
    pos = np.where((p % 64 < 32)[:, None], (t // GRID)[None], (t % GRID)[None]).astype(np.float32)
    ang = pos * freqs[p % 16][:, None].astype(np.float32)
    cos, sin = np.cos(ang).astype(np.float32), np.sin(ang).astype(np.float32)
    col = np.arange(GRID)
    start = np.clip(col - NA_COLS // 2, 0, GRID - NA_COLS)
    inside = (col[None] >= start[:, None]) & (col[None] < start[:, None] + NA_COLS)
    cmask = np.tile(np.where(inside, 0, NEG).astype(np.float32)[::-1], (2, 1))
    edge = np.ones((len(POOL_WINDOWS), 2 * PAD), np.float32)
    for g, w in enumerate(POOL_WINDOWS):
        count = np.clip(t + w - w // 2, 0, T) - np.clip(t - w // 2, 0, T)
        edge[g] = np.float32(w) / np.concatenate([count[:PAD], count[-PAD:]]).astype(np.float32)
    edge = np.tile(edge.reshape(1, -1), (P, 1))
    l, m = np.arange(P)[:, None], np.arange(P)[None]
    band = [np.where((4 * (l - m) + d >= 0) & (4 * (l - m) + d <= 128), 0, NEG) for d in range(3, -4, -1)]
    causal = np.where(l >= m, 0, NEG)
    strided = np.where((l >= m) & ((l - m) % 4 == 0), 0, NEG)
    dmask = np.concatenate(band + [causal, strided], axis=1).astype(np.float32)
    return {"c_base": np.concatenate([ident, head, mean, rot, np.roll(ident, 64, axis=1)], axis=1), "c_rope": np.concatenate([cos, sin], axis=1),
            "c_cmask": cmask, "c_edge": edge, "c_dmask": dmask}


class Chain:

    def __init__(self, eng, sem):
        self.eng, self.sem, self.n, self.shift = eng, sem, 0, 0

    def mark(self, ins):
        ins.then_inc(self.sem, 1)
        self.n += 1
        return self.n

    def wait(self, value):
        self.eng.wait_ge(self.sem, value + self.shift)

    def link(self, ins):
        self.wait(self.mark(ins))


def build(nc, A, out):
    with ExitStack() as ctx:
        def sb(name, cols, dt=F32, stack=ctx):
            return stack.enter_context(nc.sbuf_tensor("t_" + name, [P, cols], dt))

        def sem(name):
            return ctx.enter_context(nc.semaphore(name))

        wraw = [sb(f"wraw{s}", CH) for s in range(2)]
        whi = [sb(f"whi{s}", CH, F32R) for s in range(2)]
        wlo = [sb(f"wlo{s}", CH, F32R) for s in range(2)]
        x = sb("x", KT * T)
        base = sb("base", 5 * P)
        pvec = sb("pvec", ROW_TILES * P)
        scratch = sb("scratch", 3 * T)
        small = sb("small", 32)
        ident, headm, meanm, rotm, swapm = (base[:, i * P:(i + 1) * P] for i in range(5))
        tmp = [scratch[:, 0:T], scratch[:, T:2 * T]]
        std = scratch[:, 2 * T:3 * T]
        epsc = small[:, 31:32]
        with ExitStack() as s:
            hh, hl = sb("hh", KT * T, F32R, s), sb("hl", KT * T, F32R, s)
        hbufs = ctx.enter_context(ExitStack())
        mix, sq = sb("mix", KT * T, stack=hbufs), sb("sq", KT * T, stack=hbufs)

        with ExitStack() as s:
            prow, xrow = sb("prow", ROW_TILES * P, stack=s), sb("xrow", 4 * D, stack=s)
        with ExitStack() as s:
            yh, yl = sb("yh", 12 * T, F32R, s), sb("yl", 12 * T, F32R, s)
            with ExitStack() as u:
                qC, kC, vC = sb("qC", 4 * T, stack=u), sb("kC", 4 * T, stack=u), sb("vC", 4 * T, stack=u)
                e2 = [sb(f"e2{i}", 2 * E2C, stack=u) for i in range(2)]
                pC, oC = sb("pC", 2 * T, stack=u), sb("oC", 2 * P, stack=u)
                cmask = sb("cmask", GRID, stack=u)
            with ExitStack() as u:
                qA, kA, vA = sb("qA", 4 * T, stack=u), sb("kA", 2 * T, stack=u), sb("vA", T, stack=u)
                rope = sb("rope", 2 * T, stack=u)
                pA, oA = sb("pA", 2 * T, stack=u), sb("oA", 2 * T, stack=u)
                pw = sb("pw", 4 * P, stack=u)
                pu = sb("pu", 4 * (T + 2 * PAD), stack=u)
                win = [sb(f"win{i}", T + 2 * PAD, stack=u) for i in range(2)]
                edge = sb("edge", len(POOL_WINDOWS) * 2 * PAD, stack=u)
            with ExitStack() as u:
                gates, mg = sb("gates", 4 * T, stack=u), sb("mg", KT * T, stack=u)
        with ExitStack() as s:
            midh, midl = sb("midh", FT * T, F32R, s), sb("midl", FT * T, F32R, s)
            accv, accg = sb("accv", 2 * T, stack=s), sb("accg", 2 * T, stack=s)
        with ExitStack() as s:
            uh, ul = sb("uh", KT * T, F32R, s), sb("ul", KT * T, F32R, s)
            UW = T + TAPS - 1
            ub, vb = sb("ub", KT * UW, stack=s), sb("vb", KT * T, stack=s)
        with ExitStack() as s:
            qh, ql = sb("qh", KT * T, F32R, s), sb("ql", KT * T, F32R, s)
            yD = sb("yD", KT * T, stack=s)
            qD, kD, vD = (sb(n, 6 * T, stack=s) for n in ("qD", "kD", "vD"))
            pD, oD = sb("pD", 2 * 768, stack=s), sb("oD", 2 * P, stack=s)
            dmask = sb("dmask", 9 * P, stack=s)

        ps = ctx.enter_context(nc.psum_tensor("ps", [P, 8 * T], F32))

        def bank(b, n=1):
            return ps[:, b * T:(b + n) * T]

        w_loaded = [sem("w_loaded0"), sem("w_loaded1")]
        w_hi, w_lo, w_used = sem("w_hi"), sem("w_lo"), sem("w_used")
        drained = sem("drained")
        conv_done = sem("conv_done")
        mid_lo = sem("mid_lo")
        affine, acted, product, mid_hi = sem("affine"), sem("acted"), sem("product"), sem("mid_hi")
        init_in, init_turn, init_out = sem("init_in"), sem("init_turn"), sem("init_out")
        stored = sem("stored")
        squared, summed, rooted, x_tmp, x_new = (sem(n) for n in ("squared", "summed", "rooted", "x_tmp", "x_new"))
        h_tmp, h_hi, h_lo = sem("h_tmp"), sem("h_hi"), sem("h_lo")
        gate_sig, head_sq, head_sum, head_std, head_scaled, head_rot = (
            sem(n) for n in ("gate_sig", "head_sq", "head_sum", "head_std", "head_scaled", "head_rot"))
        qk_ready, swapped = sem("qk_ready"), sem("swapped")
        scored, maxed, probs, turned, pt_ready, weighted, o_ready, flushed, y_hi, y_lo = (
            sem(n) for n in ("scored", "maxed", "probs", "turned", "pt_ready", "weighted", "o_ready", "flushed",
                             "y_hi", "y_lo"))
        e2_loaded = [sem("e2_loaded0"), sem("e2_loaded1")]
        e2_ready, tables = sem("e2_ready"), sem("tables")
        pu_in, pooled, pool_out = sem("pu_in"), sem("pooled"), sem("pool_out")
        u_sig, convolved, centred, ln_scaled = sem("u_sig"), sem("convolved"), sem("centred"), sem("ln_scaled")
        pool_hi, pool_lo, merged = sem("pool_hi"), sem("pool_lo"), sem("merged")
        dve_self, act_self, pool_self = sem("dve_self"), sem("act_self"), sem("pool_self")

        def col(name, i=0):
            if isinstance(i, int):
                return pvec[:, ROWS[name][0] + i:ROWS[name][0] + i + 1]
            return pvec[:, bass.ds(i + ROWS[name][0], 1)]

        def tile(buf, t, n=1):
            if isinstance(t, int):
                return buf[:, t * T:(t + n) * T]
            return buf[:, bass.ds(t * T, n * T)]

        def permuted(ap):
            return ap.rearrange("p (l b) -> p b l", b=4)

        def by4(ap):
            return ap.rearrange("p (b l) -> p b l", b=4)

        FFN = [("w_up", "w_down", 0, "conv_w", "conv_b"), ("w_up", "w_down", 1, "conv_w", "conv_b"),
               ("ffn_w_in_2", "ffn_w_out_2", 0, "ffn_dw_2", "ffn_dw_b_2"),
               ("ffn_w_in_2", "ffn_w_out_2", 1, "ffn_dw_2", "ffn_dw_b_2")]
        POST = [("norm_mix_post", 0), ("norm_ffn_post", 0), ("norm_mix_post", 1), ("norm_ffn_post", 1),
                ("mix_post_g_2", 0), ("ffn_post_g_2", 0), ("mix_post_g_2", 1), ("ffn_post_g_2", 1)]
        PRE = [("norm_mix_pre", 0), ("norm_ffn_pre", 0), ("norm_mix_pre", 1), ("norm_ffn_pre", 1),
               ("mix_pre_g_2", 0), ("ffn_pre_g_2", 0), ("kv_norm_g_2", 0), ("ffn_pre_g_2", 1)]

        param_loads = []
        for name, (r0, n) in ROWS.items():
            if name == "qkg":
                for i, a in enumerate((A["qk_norm_q"], A["qk_norm_k"])):
                    for l in range(2):
                        for half in range(2):
                            r, c0 = r0 + 2 * i + l, 64 * half
                            at0 = (r // P) * P + c0
                            param_loads.append((prow[r % P:r % P + 1, at0:at0 + 64], a[l:l + 1, :]))
                continue
            flat = A[name]
            if len(flat.shape) == 3:
                flat = flat.rearrange("a b c -> (a b) c")
            flat = (flat.rearrange("a (n p) -> (a n) p", p=P) if len(flat.shape) == 2 else
                    flat.rearrange("(n p) -> n p", p=P))
            done = 0
            while done < n:
                r = r0 + done
                k = min(n - done, P - r % P)
                param_loads.append((prow[r % P:r % P + k, (r // P) * P:(r // P + 1) * P], flat[done:done + k, :]))
                done += k

        def steps_of(kind):
            if kind[0] == "A":
                return [(h, b) for b in range(4) for h in range(8)]
            if kind[0] == "C":
                return [(2 * hp + s, b) for hp in range(4) for b in range(4) for s in range(2)]
            return [(m, b) for b in range(4) for m in range(2)]

        OUT_TURNS = 3 + 8 + 8
        block = ctx.enter_context(nc.Block())

        def half_layer_tail(sp, load, at, rows, f, w_out):
            c = FIRST[f"out{f}"]
            for j in range(4):
                load(at(c + j), w_out[:, :, CW * j:CW * (j + 1)])
            up, down, l = FFN[f][:3]
            w = rows(A[up], l)
            c = FIRST[f"up{f}"]
            with sp.Fori(0, FT // 2) as i:
                for s in range(2):
                    load(at(c + s, i, 2), w[:, :, bass.ds(i * CW + FF * s, CW)])
            w = rows(A[down], l)
            c = FIRST[f"down{f}"]
            for half in range(2):
                for j in range(6):
                    k = min(4, FT - 4 * j)
                    load(at(c + 6 * half + j), w[:, 4 * j:4 * j + k, 512 * half:512 * half + 512], k * 512)

        @block.sync
        def _(sp):
            def load(c, src, cols=CH):
                c, slot, turn = c
                if not isinstance(c, int) or c >= 2:
                    sp.wait_ge(w_lo, c - 1)
                sp.dma_start(wraw[slot][:, 0:cols].rearrange("p (k n) -> p k n", n=src.shape[-1]),
                             src).then_inc(w_loaded[slot], 16)

            def at(c, i=None, per=0):
                if i is None:
                    return c, c % 2, c // 2
                return i * per + c, c % 2, i * (per // 2) + c // 2

            def rows(w, l):
                return w[l].rearrange("(k p) n -> p k n", p=P)

            for dst, src in param_loads:
                sp.dma_start(dst, src).then_inc(init_in, 16)

            for l in range(2):
                w = rows(A["w_in"], l)
                c = FIRST[f"c_qkv{l}"]
                for j, n0 in enumerate([QC, QC + CW, KC, KC + CW, VC, VC + CW]):
                    load(at(c + j), w[:, :, n0:n0 + CW])
                c = FIRST[f"a_qkv{l}"]
                for j in range(2):
                    load(at(c + j), w[:, :, QA + CW * j:QA + CW * (j + 1)])
                load(at(c + 2), w[:, :, KA:KA + CW])
                c = FIRST[f"pu{l}"]
                for j in range(2):
                    load(at(c + j), w[:, :, PU + CW * j:PU + CW * (j + 1)])
                c = FIRST[f"merge{l}"]
                wb = A["w_branch"][l].rearrange("b (k p) n -> p (b k) n", p=P)
                with sp.Fori(0, 3) as n:
                    for g in range(2):
                        for j in range(2):
                            load(at(c + 3 * g + j, n, 6), w[:, :, bass.ds(n * D + (GL + 512 * g + CW * j), CW)])
                        load(at(c + 3 * g + 2, n, 6), wb[:, bass.ds(n * 4, 4), 512 * g:512 * g + 512])
                half_layer_tail(sp, load, at, rows, l, rows(A["w_out"], l))
            c = FIRST["cm_in"]
            w = rows(A["cm_w_in_2"], 0)
            for j in range(4):
                load(at(c + 2 * j), w[:, :, CW * j:CW * (j + 1)])
                load(at(c + 2 * j + 1), w[:, :, D + CW * j:D + CW * (j + 1)])
            half_layer_tail(sp, load, at, rows, 2, rows(A["cm_w_out_2"], 0))
            c = FIRST["d_qkv"]
            wkv = A["w_kv_2"].rearrange("(k p) n -> p k n", p=P)
            wq = rows(A["w_q_2"], 0)
            for hp in range(4):
                for g in range(3):
                    n0 = D * g + CW * hp
                    load(at(c), wkv[:, :, n0:n0 + CW])
                    load(at(c + 1), wkv[:, :, 3 * D + n0:3 * D + n0 + CW])
                    load(at(c + 2), wq[:, :, n0:n0 + CW])
                    c += 3
            half_layer_tail(sp, load, at, rows, 3, rows(A["w_o_2"], 0))
            sp.wait_ge(init_out, OUT_TURNS)
            for b in range(4):
                sp.dma_start(out[0, b * P:(b + 1) * P, :], xrow[:, b * D:(b + 1) * D]).then_inc(stored, 16)
            sp.wait_ge(stored, 16 * 4)

        @block.gpsimd
        def _(pool):
            ch = Chain(pool, pool_self)
            gp = nc.gpsimd

            def tables_in(pairs, wait):
                for buf, name in pairs:
                    pool.dma_start(buf, A[name]).then_inc(tables, 16)

            nt = [0]

            def const(buf, src):
                pool.dma_start(buf, src).then_inc(tables, 16)
                nt[0] += 16
                return nt[0]

            const(base[:, :], A["c_base"])
            for b in range(4):
                const(xrow[:, b * D:(b + 1) * D], A["x"][0, b * P:(b + 1) * P, :])
            ch.mark(gp.memset(epsc, EPS))

            def post(h):
                for t in range(KT):
                    pool.wait_ge(x_tmp, KT * h + t + 1)
                    gp.tensor_tensor(tile(x, t), tile(x, t), tmp[t % 2], ALU.add).then_inc(x_new, 1)

            for l in range(2):
                if l == 0:
                    pool.wait_ge(init_out, 3 + 8)
                else:
                    pool.wait_ge(w_used, FIRST[f"c_qkv{l}"])
                    pool.wait_ge(mid_lo, 2 + FT * l)
                pool.wait_ge(tables, nt[0])
                pool.wait_ge(tables, const(cmask[:, :], A["c_cmask"]))
                for hp in range(4):
                    if hp >= 2:
                        pool.wait_ge(maxed, STEPS[f"C{l}"] + 8 * (hp - 1))
                    for s in range(2):
                        for half in range(2):
                            src = bass.AP(tensor=A["rpbp"].tensor, ap=[[1, GRID], [31, 14], [1, GRID]],
                                          offset=RPB_PAD + ((l * 8 + 2 * hp + s) * 15 + half) * 31 + 15 - 63)
                            pool.dma_start(e2[hp % 2][64 * half:64 * half + 64, s * E2C:(s + 1) * E2C].rearrange(
                                "p (r k) -> p r k", k=GRID), src).then_inc(e2_loaded[hp % 2], 16)
                    pool.wait_ge(e2_loaded[hp % 2], 64 * (2 * l + hp // 2 + 1))
                    v = e2[hp % 2][:, :].rearrange("p (r k) -> p r k", k=GRID)
                    m = cmask[:, :].rearrange("p (o k) -> p o k", o=1).broadcast_to([P, 28, GRID])
                    gp.tensor_tensor(v, v, m, ALU.add).then_inc(e2_ready, 1)
                pool.wait_ge(y_lo, FLUSH[f"C{l}"] + 16)
                const(rope[:, :], A["c_rope"])
                const(pw[:, :].rearrange("p (g d) -> p g d", g=4), A["w_pool"][l].rearrange("g c d -> c g d"))
                k = const(edge[:, :], A["c_edge"])
                W = T + 2 * PAD
                for g in range(4):
                    for a, b in ((0, PAD), (T + PAD, W)):
                        n = ch.mark(gp.memset(pu[:, g * W + a:g * W + b], 0.0))
                pool.wait_ge(tables, k)
                for g, w in enumerate(POOL_WINDOWS):
                    pool.wait_ge(pu_in, 2 * l + g // 2 + 1)
                    if g:
                        pool.wait_ge(pooled, 4 * l + g)
                    ch.wait(n)
                    u = pu[:, g * W:(g + 1) * W]
                    n = ch.mark(gp.tensor_tensor(win[0][:, 1:W], u[:, 0:W - 1], u[:, 1:W], ALU.add))
                    have, cur, lo = 2, 0, 1
                    while have < w:
                        ch.wait(n)
                        s = have // 2
                        lo += s
                        hi = W - lo + 1
                        n = ch.mark(gp.tensor_tensor(win[1 - cur][:, lo:hi], win[cur][:, lo - s:hi - s],
                                                     win[cur][:, lo + s:hi + s], ALU.add))
                        have, cur = 2 * have, 1 - cur
                    ch.wait(n)
                    e = edge[:, g * 2 * PAD:(g + 1) * 2 * PAD]
                    ch.mark(gp.tensor_tensor(win[cur][:, PAD:2 * PAD], win[cur][:, PAD:2 * PAD], e[:, 0:PAD], ALU.mult))
                    n = ch.mark(gp.tensor_tensor(win[cur][:, T:T + PAD], win[cur][:, T:T + PAD], e[:, PAD:2 * PAD], ALU.mult))
                    ch.wait(n)
                    mean = win[cur][:, PAD:PAD + T]
                    ch.link(gp.tensor_scalar(mean, mean, 1.0 / w, None, ALU.mult))
                    gp.tensor_tensor(u[:, PAD:PAD + T], mean, u[:, PAD:PAD + T], ALU.subtract).then_inc(pooled, 1)
                post(2 * l)
                post(2 * l + 1)
            post(4)
            post(5)
            pool.wait_ge(w_used, FIRST["d_qkv"])
            pool.wait_ge(mid_lo, 2 + 3 * FT)
            const(dmask[:, :], A["c_dmask"])
            post(6)
            post(7)

        @block.scalar
        def _(act):
            ch = Chain(act, act_self)
            sc = nc.scalar

            def hi(c, i=None, per=0):
                cc, slot = (c, c % 2) if i is None else (i * per + c, c % 2)
                act.wait_ge(w_used, cc + 1)
                if isinstance(cc, int) and cc + 2 >= CHUNKS:
                    return
                act.wait_ge(w_loaded[slot], (cc // 2 + 2) * 16 if i is None else i * (per * 8) + (c // 2 + 2) * 16)
                sc.activation(whi[slot][:, :], wraw[slot][:, :], ACT.Copy).then_inc(w_hi, 1)

            def split_hi(name, src, dst, ready, n=KT):
                for t in range(n):
                    ready(t)
                    sc.activation(dst(t), src(t), ACT.Copy).then_inc(h_hi, 1)

            def root(name):
                m = NORM[name]
                act.wait_ge(summed, m + 1)
                if m == 0:
                    act.wait_ge(pool_self, 1)
                sc.activation(std, bank(7 if name[:4] in ("post", "ln_m") else 6), ACT.Sqrt, bias=epsc).then_inc(rooted, 1)

            def h_split(name, dsth, view=lambda a: a):
                for t in range(KT):
                    act.wait_ge(h_tmp, SCALED[name] + t + 1)
                    sc.activation(tile(dsth, t), tmp[t % 2], ACT.Copy).then_inc(h_hi, 1)

            def squares_of_x(name):
                for t in range(KT):
                    if name == "pre0":
                        act.wait_ge(init_out, 3 + t + 1)
                    else:
                        act.wait_ge(x_new, KT * (int(name[3:]) - 1) + t + 1)
                    sc.activation(tile(sq, t), tile(x, t), ACT.Square).then_inc(squared, 1)

            def pre(h, second=None):
                name = f"pre{h}"
                squares_of_x(name)
                root(name)
                h_split(name, hh)
                if second:
                    h_split("hq", qh)

            def attention(kind, n0, f0, count, width, pbuf, from_psum, flush):
                for n in range(count + 4):
                    if n < count:
                        s = (n0 + n) % 2
                        act.wait_ge(maxed, n0 + n + 1)
                        if n >= 2:
                            act.wait_ge(turned, n0 + n - 1)
                        q = (n0 + n) % 4
                        src = from_psum(s) if from_psum else pbuf[:, s * width:(s + 1) * width]
                        sc.activation(pbuf[:, s * width:(s + 1) * width], src, ACT.Exp, bias=small[:, q:q + 1],
                                      scale={"A": 0.125, "C": 1.0, "D": SD}[kind],
                                      accum_out=small[:, 8 + q:9 + q]).then_inc(probs, 1)
                    if 1 <= n <= count:
                        m = n0 + n - 1
                        act.wait_ge(turned, m + 1)
                        if n >= 3:
                            act.wait_ge(weighted, m - 1)
                        src = bank(4, 2)[:, 0:768] if kind == "D" else bank(2 + m % 2)
                        sc.activation(scratch[:, (m % 2) * width:(m % 2) * width + width], src,
                                      ACT.Copy).then_inc(pt_ready, 1)
                    flush(n)

            def out_rows(f, extra_bias=None, view=lambda a: a):
                c = FIRST[f"out{f}"]
                for j in range(4):
                    hi(c + j)
                    for m in range(2):
                        t = 2 * j + m
                        b = {"bias": col(extra_bias, t)} if extra_bias else {}
                        sc.activation(view(tile(sq, t)), by4(bank(2 * (j % 2) + m)) if f == 3 else bank(2 * (j % 2) + m),
                                      ACT.Square, **b).then_inc(squared, 1)
                root(f"post{2 * f}")

            def ffn(f):
                fn = ACT.Gelu_apprx_tanh if f < 2 else ACT.Silu
                _, _, l, cw, cb = FFN[f]
                centre = 1 if f < 2 else 2
                c = FIRST[f"up{f}"]
                m0 = FT * f
                with act.Fori(0, FT // 2) as i:
                    for s, acc in enumerate((accv, accg)):
                        hi(c + s, i, 2)
                        for m in range(2):
                            if s == 0:
                                act.wait_ge(mid_lo, i * 2 + (m0 + m + 1))
                            r = i * 2 + (s * FT + m)
                            sc.activation(tile(acc, m), bank(2 * s + m), ACT.Identity,
                                          bias=col(cb, r + 2 * FT * l),
                                          scale=col(cw, r + 2 * FT * (3 * l + centre))).then_inc(affine, 1)
                    for m in range(2):
                        act.wait_ge(conv_done, i * 4 + (4 + 2 * m0 + 2 + m + 1))
                        sc.activation(tile(accg, m), tile(accg, m), fn).then_inc(acted, 1)
                    for m in range(2):
                        act.wait_ge(product, i * 2 + (m0 + m + 1))
                        sc.activation(tile(midh, i * 2 + m), tile(accv, m), ACT.Copy).then_inc(mid_hi, 1)
                c = FIRST[f"down{f}"]
                for half in range(2):
                    for j in range(6):
                        hi(c + 6 * half + j)
                    for t in range(4):
                        sc.activation(tile(sq, 4 * half + t), bank(4 * (1 - half) + t), ACT.Square).then_inc(squared, 1)
                root(f"post{2 * f + 1}")

            for c in range(2):
                act.wait_ge(w_loaded[c], 16)
                sc.activation(whi[c][:, :], wraw[c][:, :], ACT.Copy).then_inc(w_hi, 1)
            pre(0)
            for l in range(2):
                c = FIRST[f"c_qkv{l}"]
                for j in range(6):
                    hi(c + j)

                def flush_c(n, l=l):
                    if n >= 5 and (n - 5) % 2 == 0:
                        g = (n - 5) // 2
                        yh_flush(8 + g // 4, g % 4, FLUSH[f"C{l}"] + g)

                def yh_flush(t, b, f):
                    act.wait_ge(flushed, f + 1)
                    sc.activation(yh[:, t * T + b * P:t * T + b * P + P], bank(6 + f % 2)[:, 0:P], ACT.Copy).then_inc(y_hi, 1)

                attention("C", STEPS[f"C{l}"], 0, 32, T, pC, None, flush_c)
                c = FIRST[f"a_qkv{l}"]
                for j in range(3):
                    hi(c + j)
                    for m in range(2 if j < 2 else 1):
                        t = 5 * l + 2 * j + m
                        if t >= 2:
                            act.wait_ge(head_sum, t - 1)
                        sc.activation(tmp[t % 2], bank(2 * ((c + j) % 2) + m), ACT.Square).then_inc(head_sq, 1)
                    for m in range(2 if j < 2 else 1):
                        t = 5 * l + 2 * j + m
                        act.wait_ge(head_sum, t + 1)
                        if t >= 1:
                            act.wait_ge(head_scaled, t)
                        sc.activation(std, bank(6), ACT.Sqrt, bias=epsc).then_inc(head_std, 1)
                c = FIRST[f"pu{l}"]
                W = T + 2 * PAD
                for j in range(2):
                    hi(c + j)
                    sc.activation(pu[:, 2 * j * W:2 * (j + 1) * W].rearrange("p (m w) -> p m w", m=2)[:, :, PAD:PAD + T],
                                  bank(2 * ((c + j) % 2), 2).rearrange("p (m w) -> p m w", m=2), ACT.Copy).then_inc(pu_in, 1)

                def flush_a(n, l=l):
                    if n >= 11 and (n - 11) % 8 == 0:
                        b = (n - 11) // 8
                        f = FLUSH[f"A{l}"] + b
                        act.wait_ge(flushed, f + 1)
                        sc.activation(yh[:, 0:4 * T].rearrange("p (t q) -> p t q", t=4)[:, :, b * P:(b + 1) * P],
                                      bank(6 + f % 2).rearrange("p (t q) -> p t q", t=4), ACT.Copy).then_inc(y_hi, 1)

                attention("A", STEPS[f"A{l}"], 0, 32, T, pA, lambda s: bank(s), flush_a)
                for g in range(4):
                    act.wait_ge(pool_out, 4 * l + g + 1)
                    sc.activation(tile(yh, 4 + g), bank(2 + g), ACT.Copy, scale=col("pool_scale", 4 * l + g)).then_inc(pool_hi, 1)
                c = FIRST[f"merge{l}"]
                d = DRAINS[f"merge{l}"]
                with act.Fori(0, 3) as n:
                    for g in range(2):
                        for j in range(2):
                            hi(c + 3 * g + j, n, 6)
                            act.wait_ge(drained, n * 6 + (2 + d + 3 * g + j + 1))
                            sc.activation(tile(gates, 2 * j, 2), tile(gates, 2 * j, 2), ACT.Sigmoid).then_inc(gate_sig, 1)
                        hi(c + 3 * g + 2, n, 6)
                for t in range(KT):
                    act.wait_ge(merged, 6 * (l + 1))
                    sc.activation(tile(yh, t), tile(mg, t), ACT.Copy).then_inc(h_hi, 1)
                out_rows(l)
                pre(2 * l + 1)
                ffn(l)
                pre(2 * l + 2)
            c = FIRST["cm_in"]
            for j in range(4):
                hi(c + 2 * j)
                hi(c + 2 * j + 1)
                for m in range(2):
                    act.wait_ge(drained, 2 + DRAINS["cm_in"] + 2 * j)
                    sc.activation(tmp[m], bank(2 * ((c + 1) % 2) + m), ACT.Sigmoid, bias=col("cm_b_in_2", 8 + 2 * j + m)).then_inc(u_sig, 1)
            for t in range(KT):
                act.wait_ge(centred, t + 1)
                sc.activation(tile(sq, t), tile(vb, t), ACT.Square).then_inc(squared, 1)
            root("ln_var")
            for t in range(KT):
                act.wait_ge(ln_scaled, t + 1)
                ch.link(sc.activation(tile(vb, t), tile(vb, t), ACT.Silu, scale=col("cm_ln_g_2", t), bias=col("cm_ln_b_2", t)))
                sc.activation(tile(uh, t), tile(vb, t), ACT.Copy).then_inc(h_hi, 1)
            out_rows(2, "cm_b_out_2")
            pre(5)
            ffn(2)
            pre(6, second=True)
            c = FIRST["d_qkv"]
            for hp in range(4):
                for j in range(9):
                    hi(c + 9 * hp + j)
                attention("D", STEPS["D"] + 8 * hp, 0, 8, 768, pD, None, lambda n: None)
            for t in range(KT):
                act.wait_ge(y_lo, FLUSH["D"] + 32)
                sc.activation(tile(qh, t), tile(yD, t), ACT.Copy).then_inc(h_hi, 1)
            out_rows(3, view=permuted)
            pre(7)
            ffn(3)

        @block.vector
        def _(dve):
            ch = Chain(dve, dve_self)
            v = nc.vector

            def lo(c, i=None, per=0):
                cc, slot = (c, c % 2) if i is None else (i * per + c, c % 2)
                dve.wait_ge(w_used, cc + 1)
                if isinstance(cc, int) and cc + 2 >= CHUNKS:
                    return
                dve.wait_ge(w_hi, cc + 3)
                v.tensor_tensor(wlo[slot][:, :], wraw[slot][:, :], whi[slot][:, :].bitcast(F32), ALU.subtract).then_inc(w_lo, 1)

            def split_lo(name, src, dsth, dstl):
                for t in range(KT):
                    dve.wait_ge(h_hi, SPLIT[name] + t + 1)
                    v.tensor_tensor(tile(dstl, t), tile(src, t), tile(dsth, t).bitcast(F32), ALU.subtract).then_inc(h_lo, 1)

            def rstd(name):
                dve.wait_ge(rooted, SQUARES[name] // 8 + 1)
                ch.link(v.reciprocal(std, std))

            def post(h):
                rstd(f"post{h}")
                name, l = POST[h]
                for t in range(KT):
                    if t >= 2:
                        dve.wait_ge(x_new, KT * h + t - 1)
                    v.scalar_tensor_tensor(out=tmp[t % 2], in0=tile(mix, t), scalar=col(name, KT * l + t), in1=std,
                                           op0=ALU.mult, op1=ALU.mult).then_inc(x_tmp, 1)

            def h_split(name, gain, l, dsth, dstl, permute):
                for t in range(KT + 1):
                    if t < KT:
                        if t >= 2 or name == "hq":
                            dve.wait_ge(h_lo, SPLIT[name] + t - 1)
                        a, r, o = tile(x, t), std, tmp[t % 2]
                        if permute:
                            a, r, o = permuted(a), permuted(r), by4(o)
                        v.scalar_tensor_tensor(out=o, in0=a, scalar=col(gain, KT * l + t), in1=r,
                                               op0=ALU.mult, op1=ALU.mult).then_inc(h_tmp, 1)
                    if t >= 1:
                        dve.wait_ge(h_hi, SPLIT[name] + t)
                        v.tensor_tensor(tile(dstl, t - 1), tmp[(t - 1) % 2], tile(dsth, t - 1).bitcast(F32),
                                        ALU.subtract).then_inc(h_lo, 1)

            def pre(h):
                rstd(f"pre{h}")
                h_split(f"pre{h}", *PRE[h], hh, hl, h == 6)
                if h == 6:
                    h_split("hq", "mix_pre_g_2", 1, qh, ql, True)

            def attention(kind, n0, count, width, obuf, group, flush_lag, flush, scores_in):
                for n in range(count + flush_lag + 2):
                    if n < count:
                        g, q, s = n0 + n, (n0 + n) % 4, (n0 + n) % 2
                        dve.wait_ge(scored, g + 1)
                        m = ch.mark(scores_in(n, s, q))
                        ch.wait(m)
                        v.tensor_scalar(small[:, q:q + 1], small[:, 4 + q:5 + q], {"A": -0.125, "C": -1.0, "D": -SD}[kind],
                                        None, ALU.mult).then_inc(maxed, 1)
                    if 2 <= n < count + 2:
                        g = n0 + n - 2
                        q = g % 4
                        dve.wait_ge(weighted, g + 1)
                        ch.link(v.reciprocal(small[:, 12 + q:13 + q], small[:, 8 + q:9 + q]))
                        group(n - 2, g, small[:, 12 + q:13 + q])
                    flush(n)

            def ffn(f):
                c = FIRST[f"up{f}"]
                m0 = FT * f
                _, _, l, cw, cb = FFN[f]
                taps = [(0, (1, T), (0, T - 1)), (2, (0, T - 1), (1, T))] if f < 2 else \
                       [(1, (1, T), (0, T - 1)), (0, (2, T), (0, T - 2))]
                per = 4
                with dve.Fori(0, FT // 2) as i:
                    start = ch.n
                    ch.shift = i * per
                    for s, acc in enumerate((accv, accg)):
                        lo(c + s, i, 2)
                        first = []
                        for n, (k, (o0, o1), (i0, i1)) in enumerate(taps):
                            for m in range(2):
                                r = i * 2 + (s * FT + m + 2 * FT * (3 * l + k))
                                if n == 0:
                                    dve.wait_ge(affine, i * 4 + (2 * m0 + 2 * s + m + 1))
                                else:
                                    ch.wait(first[m])
                                ins = v.scalar_tensor_tensor(
                                    out=tile(acc, m)[:, o0:o1], in0=bank(2 * s + m)[:, i0:i1], scalar=col(cw, r),
                                    in1=tile(acc, m)[:, o0:o1], op0=ALU.mult, op1=ALU.add)
                                if n == 0:
                                    first.append(ch.mark(ins))
                                else:
                                    ins.then_inc(conv_done, 1)
                    for m in range(2):
                        dve.wait_ge(acted, i * 2 + (m0 + m + 1))
                        v.tensor_tensor(tile(accv, m), tile(accg, m), tile(accv, m), ALU.mult).then_inc(product, 1)
                    for m in range(2):
                        dve.wait_ge(mid_hi, i * 2 + (m0 + m + 1))
                        v.tensor_tensor(tile(midl, i * 2 + m), tile(accv, m), tile(midh, i * 2 + m).bitcast(F32),
                                        ALU.subtract).then_inc(mid_lo, 1)
                    assert ch.n - start == per
                ch.shift = 0
                ch.n += per * (FT // 2 - 1)
                c = FIRST[f"down{f}"]
                for half in range(2):
                    for j in range(6):
                        lo(c + 6 * half + j)
                    for t in range(4):
                        dve.wait_ge(squared, SQUARES[f"post{2 * f + 1}"] + 4 * half + t + 1)
                        ins = v.tensor_copy(tile(mix, 4 * half + t), bank(4 * (1 - half) + t))
                    ins.then_inc(drained, 6)
                post(2 * f + 1)

            def out_rows(f):
                c = FIRST[f"out{f}"]
                for j in range(4):
                    lo(c + j)
                    for m in range(2):
                        t, b = 2 * j + m, bank(2 * (j % 2) + m)
                        dve.wait_ge(squared, SQUARES[f"post{2 * f}"] + t + 1)
                        if f == 2:
                            ins = v.tensor_scalar(tile(mix, t), b, col("cm_b_out_2", t), None, ALU.add)
                        elif f == 3:
                            ins = v.tensor_copy(permuted(tile(mix, t)), by4(b))
                        else:
                            ins = v.tensor_copy(tile(mix, t), b)
                    ins.then_inc(drained, 1)
                post(2 * f)

            v.memset(small[:, 16:17], 0.0).then_inc(drained, 2)
            v.memset(small[:, 17:18], 0.0).then_inc(conv_done, 4)
            v.memset(small[:, 18:19], 0.0).then_inc(mid_lo, 2)
            for c in range(2):
                dve.wait_ge(w_hi, c + 1)
                v.tensor_tensor(wlo[c][:, :], wraw[c][:, :], whi[c][:, :].bitcast(F32), ALU.subtract).then_inc(w_lo, 1)
            for r in range(3):
                n = min(4 * P, ROWS_ALL - 4 * r * P)
                dve.wait_ge(init_turn, r + 1)
                v.tensor_copy(pvec[:, 4 * r * P:4 * r * P + n], bank(r)[:, 0:n]).then_inc(init_out, 1)
            for t in range(KT):
                dve.wait_ge(init_turn, 3 + t + 1)
                v.tensor_copy(tile(x, t), bank(3 + t % 3)).then_inc(init_out, 1)
            pre(0)
            for l in range(2):
                c = FIRST[f"c_qkv{l}"]
                for j in range(6):
                    lo(c + j)
                    src = bank(2 * ((c + j) % 2), 2)
                    if j < 2:
                        ins = v.tensor_scalar(tile(qC, 2 * j, 2).rearrange("p (b q) -> p b q", q=P),
                                              src.rearrange("p (b q) -> p b q", q=P)[:, :, ::-1], 0.125, None, ALU.mult)
                    elif j < 4:
                        ins = v.tensor_copy(tile(kC, 2 * j - 4, 2), src)
                    else:
                        ins = v.tensor_copy(vC[:, :].rearrange("p (b n) -> p b n", b=4)[:, :, CW * (j - 4):CW * (j - 3)],
                                            src.rearrange("p (b n) -> p b n", b=4))
                    ins.then_inc(drained, 1)

                def scores_c(n, s, q, l=l):
                    h, b = steps_of("C")[n]
                    hp = h // 2
                    dve.wait_ge(e2_ready, 4 * l + hp + 1)
                    if n >= 2:
                        dve.wait_ge(turned, STEPS[f"C{l}"] + n - 1)
                    off = (h % 2) * E2C + (6 - 2 * b) * GRID
                    return v.tensor_tensor_reduce(pC[:, s * T:(s + 1) * T], bank(s), e2[hp % 2][:, off:off + T], 1.0,
                                                  2 * NEG, ALU.add, ALU.max, small[:, 4 + q:5 + q])

                def group_c(n, g, r, l=l):
                    k = n // 2
                    if k >= 2:
                        dve.wait_ge(flushed, FLUSH[f"C{l}"] + k - 1)
                    v.tensor_scalar(oC[:, (k % 2) * P + (n % 2) * 64:(k % 2) * P + (n % 2) * 64 + 64], bank(4 + g % 2)[:, 0:64],
                                    r, None, ALU.mult).then_inc(o_ready, 1)

                def flush_c(n, l=l):
                    if n >= 6 and (n - 6) % 2 == 0 and n < 38:
                        k = (n - 6) // 2
                        f = FLUSH[f"C{l}"] + k
                        dve.wait_ge(y_hi, f + 1)
                        at = (8 + k // 4) * T + (k % 4) * P
                        v.tensor_tensor(yl[:, at:at + P], bank(6 + f % 2)[:, 0:P], yh[:, at:at + P].bitcast(F32),
                                        ALU.subtract).then_inc(y_lo, 1)

                attention("C", STEPS[f"C{l}"], 32, T, oC, group_c, 4, flush_c, scores_c)

                def rotate(t):
                    dst = tile(qA, t) if t < 4 else tile(kA, t - 4)
                    n = 5 * l + t
                    dve.wait_ge(head_rot, n + 1)
                    dve.wait_ge(tables, 16 * (5 + 4 * (l + 1)))
                    o = oA[:, (n % 2) * T:(n % 2) * T + T]
                    v.tensor_tensor(o, bank(5 + 2 * (n % 2)), rope[:, T:2 * T], ALU.mult)
                    ch.link(v.tensor_tensor(dst, dst, rope[:, 0:T], ALU.mult))
                    v.tensor_tensor(dst, dst, o, ALU.add).then_inc(qk_ready, 1)

                c = FIRST[f"a_qkv{l}"]
                for j in range(3):
                    lo(c + j)
                    s = (c + j) % 2
                    dve.wait_ge(head_sq, 5 * l + min(2 * j + 2, 5))
                    if j < 2:
                        ins = v.tensor_copy(tile(qA, 2 * j, 2), bank(2 * s, 2))
                    else:
                        v.tensor_copy(tile(kA, 0), bank(2 * s))
                        ins = v.tensor_copy(vA[:, :], bank(4))
                    ins.then_inc(drained, 1)
                    for m in range(2 if j < 2 else 1):
                        t = 2 * j + m
                        n = 5 * l + t
                        dst = tile(qA, t) if t < 4 else tile(kA, t - 4)
                        dve.wait_ge(head_std, n + 1)
                        ch.link(v.reciprocal(std, std))
                        v.scalar_tensor_tensor(out=dst, in0=dst, scalar=col("qkg", l if t < 4 else 2 + l), in1=std,
                                               op0=ALU.mult, op1=ALU.mult).then_inc(head_scaled, 1)
                rotate(0)
                rotate(1)
                c = FIRST[f"pu{l}"]
                lo(c)
                dve.wait_ge(pu_in, 2 * l + 1)
                v.memset(small[:, 16:17], 0.0).then_inc(drained, 1)
                rotate(2)
                rotate(3)
                lo(c + 1)
                dve.wait_ge(pu_in, 2 * l + 2)
                v.memset(small[:, 16:17], 0.0).then_inc(drained, 1)
                rotate(4)
                dve.wait_ge(swapped, l + 1)
                v.tensor_copy(tile(kA, 1), bank(4)).then_inc(qk_ready, 1)

                def scores_a(n, s, q):
                    return v.tensor_reduce(small[:, 4 + q:5 + q], bank(s), AX.X, ALU.max)

                def group_a(n, g, r, l=l):
                    h, b = steps_of("A")[n]
                    if b >= 2:
                        dve.wait_ge(flushed, FLUSH[f"A{l}"] + b - 1)
                    v.tensor_scalar(oA[:, (b % 2) * T + h * 64:(b % 2) * T + h * 64 + 64], bank(4 + g % 2)[:, 0:64],
                                    r, None, ALU.mult).then_inc(o_ready, 1)

                def flush_a(n, l=l):
                    if n >= 12 and (n - 12) % 8 == 0:
                        b = (n - 12) // 8
                        f = FLUSH[f"A{l}"] + b
                        dve.wait_ge(y_hi, f + 1)
                        dst, src = (u[:, 0:4 * T].rearrange("p (t q) -> p t q", t=4)[:, :, b * P:(b + 1) * P] for u in (yl, yh))
                        v.tensor_tensor(dst, bank(6 + f % 2).rearrange("p (t q) -> p t q", t=4), src.bitcast(F32),
                                        ALU.subtract).then_inc(y_lo, 1)

                attention("A", STEPS[f"A{l}"], 32, T, oA, group_a, 4, flush_a, scores_a)
                for g in range(4):
                    dve.wait_ge(pool_hi, 4 * l + g + 1)
                    v.scalar_tensor_tensor(out=tile(yl, 4 + g), in0=bank(2 + g), scalar=col("pool_scale", 4 * l + g),
                                           in1=tile(yh, 4 + g).bitcast(F32), op0=ALU.mult, op1=ALU.subtract).then_inc(pool_lo, 1)
                cleared = ch.mark(v.memset(mg[:, :], 0.0))
                c = FIRST[f"merge{l}"]
                d = DRAINS[f"merge{l}"]
                with dve.Fori(0, 3) as n:
                    for g in range(2):
                        for j in range(2):
                            lo(c + 3 * g + j, n, 6)
                            if g or j:
                                pass
                            for m in range(2):
                                ins = v.tensor_scalar(tile(gates, 2 * j + m), bank(4 + 2 * j + m),
                                                      col("b_gate", n * 8 + (24 * l + 4 * g + 2 * j + m)), None, ALU.add)
                            ins.then_inc(drained, 1)
                        lo(c + 3 * g + 2, n, 6)
                        dve.wait_ge(gate_sig, n * 4 + (12 * l + 2 * g + 2))
                        v.tensor_tensor(gates[:, :], gates[:, :], bank(0, 4), ALU.mult).then_inc(drained, 1)
                        dve.wait_ge(drained, n * 6 + (2 + d + 3 * g + 3))
                        ch.wait(cleared)
                        v.tensor_tensor(tile(mg, 4 * g, 4), tile(mg, 4 * g, 4), gates[:, :], ALU.add).then_inc(merged, 1)
                        dve.wait_ge(merged, n * 2 + (6 * l + g + 1))
                split_lo(f"mg{l}", mg, yh, yl)
                out_rows(l)
                pre(2 * l + 1)
                ffn(l)
                pre(2 * l + 2)
            c = FIRST["cm_in"]
            v.memset(ub[:, :].rearrange("p (t w) -> p t w", t=KT)[:, :, 0:TAPS - 1], 0.0)
            for j in range(4):
                lo(c + 2 * j)
                for m in range(2):
                    t = 2 * j + m
                    ins = v.tensor_scalar(ub[:, t * UW + TAPS - 1:(t + 1) * UW], bank(2 * (c % 2) + m), col("cm_b_in_2", t), None,
                                          ALU.add)
                ins.then_inc(drained, 1)
                lo(c + 2 * j + 1)
                dve.wait_ge(drained, 2 + DRAINS["cm_in"] + 2 * j + 1)
                for m in range(2):
                    t = 2 * j + m
                    dve.wait_ge(u_sig, t + 1)
                    u = ub[:, t * UW + TAPS - 1:(t + 1) * UW]
                    ins = v.tensor_tensor(u, u, tmp[m], ALU.mult)
                ins.then_inc(drained, 1)
                dve.wait_ge(drained, 2 + DRAINS["cm_in"] + 2 * j + 2)
                last = [0, 0]
                for k in range(TAPS):
                    for m in range(2):
                        t = 2 * j + m
                        u = ub[:, t * UW + k:t * UW + k + T]
                        if k == 0:
                            last[m] = ch.mark(v.tensor_scalar(tile(vb, t), u, col("cm_dw_2", 8 * k + t), col("cm_dw_b_2", t),
                                                              ALU.mult, ALU.add))
                            continue
                        ch.wait(last[m])
                        ins = v.scalar_tensor_tensor(out=tile(vb, t), in0=u, scalar=col("cm_dw_2", 8 * k + t), in1=tile(vb, t),
                                                     op0=ALU.mult, op1=ALU.add)
                        if k < TAPS - 1:
                            last[m] = ch.mark(ins)
                        else:
                            ins.then_inc(convolved, 1)
            dve.wait_ge(summed, NORM["ln_mean"] + 1)
            for t in range(KT):
                v.tensor_tensor(tile(vb, t), tile(vb, t), bank(7), ALU.subtract).then_inc(centred, 1)
            rstd("ln_var")
            for t in range(KT):
                v.tensor_tensor(tile(vb, t), tile(vb, t), std, ALU.mult).then_inc(ln_scaled, 1)
            split_lo("ln", vb, uh, ul)
            out_rows(2)
            pre(5)
            ffn(2)
            pre(6)
            c = FIRST["d_qkv"]
            for hp in range(4):
                for g in range(3):
                    for j, dst in enumerate((kD, vD, qD)):
                        lo(c)
                        src = bank(2 * (c % 2), 2)
                        if j == 1:
                            ins = v.tensor_copy(vD[:, :].rearrange("p (b g n) -> p b g n", b=4, g=3)[:, :, g, :],
                                                src.rearrange("p (b n) -> p b n", b=4))
                        else:
                            ins = v.tensor_copy(tile(dst, 2 * g, 2), src)
                        ins.then_inc(drained, 1)
                        c += 1
                n0 = STEPS["D"] + 8 * hp

                def scores_d(n, s, q, n0=n0):
                    m, b = steps_of("D")[n]
                    if n >= 2:
                        dve.wait_ge(turned, n0 + n - 1)
                    ch.link(v.tensor_tensor(pD[:, s * 768:s * 768 + T], bank(2 * s), dmask[:, (3 - b) * P:(7 - b) * P], ALU.add))
                    ch.link(v.tensor_tensor(pD[:, s * 768 + T:s * 768 + 768], bank(2 * s + 1)[:, 0:256], dmask[:, 7 * P:9 * P], ALU.add))
                    return v.tensor_reduce(small[:, 4 + q:5 + q], pD[:, s * 768:s * 768 + 768], AX.X, ALU.max)

                def group_d(n, g, r, n0=n0):
                    if n >= 2:
                        dve.wait_ge(flushed, FLUSH["D"] + g - STEPS["D"] - 1)
                    v.tensor_scalar(oD[:, (g % 2) * P:(g % 2) * P + P], bank(6)[:, 0:P], r, None, ALU.mult).then_inc(o_ready, 1)

                def flush_d(n, hp=hp):
                    if 4 <= n < 12:
                        m, b = steps_of("D")[n - 4]
                        dve.wait_ge(flushed, FLUSH["D"] + 8 * hp + n - 4 + 1)
                        at = (2 * hp + m) * T + b * P
                        v.tensor_copy(yD[:, at:at + P], bank(7)[:, 0:P]).then_inc(y_lo, 1)

                dve.wait_ge(tables, 16 * (5 + 8 + 1))
                attention("D", n0, 8, 768, oD, group_d, 4, flush_d, scores_d)
            split_lo("y", yD, qh, ql)
            out_rows(3)
            pre(7)
            ffn(3)
            for n in range(8):
                dve.wait_ge(init_turn, 11 + n + 1)
                v.tensor_copy(xrow[:, n * T:(n + 1) * T], bank(n % 4)).then_inc(init_out, 1)

        @block.tensor
        def _(pe):
            te = nc.tensor

            def mm3(out, wh, wl, xh, xl, first, last):
                te.matmul(out, wh, xh, start=first, stop=False)
                te.matmul(out, wh, xl, start=False, stop=False)
                return te.matmul(out, wl, xh, start=False, stop=last)

            def start(c, i=None, per=0, d=None):
                if i is None:
                    pe.wait_ge(w_lo, c + 1)
                    pe.wait_ge(drained, d + 1)
                else:
                    pe.wait_ge(w_lo, i * per + (c + 1))
                    pe.wait_ge(drained, i * per + (d + 1))

            def rows_out(c, bufs, split, bank0=None, tiles=2):
                s = c % 2
                b0 = 2 * s if bank0 is None else bank0
                for m in range(tiles):
                    for k in range(KT):
                        if split is not None and m == 0:
                            pe.wait_ge(h_lo, SPLIT[split] + k + 1)
                        wh, wl = (w[s][:, k * CW + m * P:k * CW + (m + 1) * P] for w in (whi, wlo))
                        ins = mm3(bank(b0 + m), wh, wl, tile(bufs[0], k), tile(bufs[1], k), k == 0, k == KT - 1)
                return ins

            def tokens_out(c, bufs, c0, n, at):
                s = c % 2
                for b in range(4):
                    o = ps[:, at * T + b * n:at * T + (b + 1) * n]
                    for k in range(KT):
                        xs = [u[:, k * T + b * P:k * T + (b + 1) * P] for u in bufs]
                        wh, wl = (w[s][:, k * CW + c0:k * CW + c0 + n] for w in (whi, wlo))
                        te.matmul(o, xs[0], wh, start=k == 0, stop=False)
                        te.matmul(o, xs[0], wl, start=False, stop=False)
                        ins = te.matmul(o, xs[1], wh, start=False, stop=k == KT - 1)
                return ins

            def mean_of(name, t, bank_no, src=None):
                if src is None:
                    pe.wait_ge(squared, SQUARES[name] + t + 1)
                ins = te.matmul(bank(bank_no), meanm, tile(sq if src is None else src, t), start=t == 0, stop=t == KT - 1)
                if t == KT - 1:
                    ins.then_inc(summed, 1)

            def out_product(f, bufs, split):
                c, d = FIRST[f"out{f}"], DRAINS[f"out{f}"]
                for j in range(4):
                    start(c + j, d=d + j)
                    rows_out(c + j, bufs, split if j == 0 else None, bank0=2 * (j % 2)).then_inc(w_used, 1)
                    if j:
                        mean_of(f"post{2 * f}", 2 * j - 2, 7)
                        mean_of(f"post{2 * f}", 2 * j - 1, 7)
                mean_of(f"post{2 * f}", 6, 7)
                mean_of(f"post{2 * f}", 7, 7)

            def pre(h):
                for t in range(KT):
                    mean_of(f"pre{h}", t, 6)

            def ffn(f):
                c, m0 = FIRST[f"up{f}"], FT * f
                pe.wait_ge(drained, 2 + DRAINS[f"up{f}"])
                with pe.Fori(0, FT // 2) as i:
                    for s in range(2):
                        pe.wait_ge(w_lo, i * 2 + (c + s + 1))
                        pe.wait_ge(conv_done, i * 4 + (2 * m0 + 2 * s + 2))
                        rows_out(c + s, (hh, hl), f"pre{2 * f + 1}", bank0=2 * s).then_inc(w_used, 1)
                pe.wait_ge(conv_done, 4 + 2 * m0 + 2 * FT)
                c = FIRST[f"down{f}"]
                for half in range(2):
                    for j in range(6):
                        cc = c + 6 * half + j
                        pe.wait_ge(w_lo, cc + 1)
                        for k in range(min(4, FT - 4 * j)):
                            n = 4 * j + k
                            if half == 0:
                                pe.wait_ge(mid_lo, 2 + m0 + n + 1)
                            for t in range(4):
                                at = k * 512 + t * P
                                ins = mm3(bank(4 * (1 - half) + t), whi[cc % 2][:, at:at + P], wlo[cc % 2][:, at:at + P],
                                          tile(midh, n), tile(midl, n), n == 0, n == FT - 1)
                        ins.then_inc(w_used, 1)
                        if half == 1 and 1 <= j < 5:
                            if j == 1:
                                pe.wait_ge(drained, 2 + DRAINS[f"down{f}"] + 6)
                            mean_of(f"post{2 * f + 1}", j - 1, 7)
                for t in range(4, KT):
                    mean_of(f"post{2 * f + 1}", t, 7)

            def attention(kind, n0, count, scores, turn, weigh, flush):
                scores(0, n0)
                scores(1, n0 + 1)
                for n in range(count + 4):
                    if n < count:
                        pe.wait_ge(probs, n0 + n + 1)
                        if n + 2 < count:
                            scores(n + 2, n0 + n + 2)
                        turn(n, n0 + n)
                    if 1 <= n <= count:
                        pe.wait_ge(pt_ready, n0 + n)
                        weigh(n - 1, n0 + n - 1)
                    flush(n)

            def turn4(pbuf):
                def turn(n, g):
                    if n >= 2:
                        pe.wait_ge(pt_ready, g - 1)
                    for j in range(4):
                        ins = te.transpose(bank(2 + g % 2)[:, j * P:(j + 1) * P],
                                           pbuf[:, (g % 2) * T + j * P:(g % 2) * T + (j + 1) * P], ident)
                    ins.then_inc(turned, 1)
                return turn

            pe.wait_ge(init_in, 16 * len(param_loads))
            pe.wait_ge(tables, 16 * 5)
            for r in range(3):
                for j in range(min(4, ROW_TILES - 4 * r)):
                    n = 4 * r + j
                    k = min(P, ROWS_ALL - n * P)
                    ins = te.transpose(bank(r)[:, j * P:j * P + k], prow[0:k, n * P:(n + 1) * P], ident[0:k, 0:k])
                ins.then_inc(init_turn, 1)
            for t in range(KT):
                if t >= 3:
                    pe.wait_ge(init_out, 3 + t - 3 + 1)
                for b in range(4):
                    ins = te.transpose(bank(3 + t % 3)[:, b * P:(b + 1) * P], xrow[:, b * D + t * P:b * D + (t + 1) * P], ident)
                ins.then_inc(init_turn, 1)
            pre(0)
            for l in range(2):
                c, d = FIRST[f"c_qkv{l}"], DRAINS[f"c_qkv{l}"]
                for j in range(6):
                    start(c + j, d=d + j)
                    if j == 0:
                        pe.wait_ge(drained, 2 + d)
                    if j < 4:
                        rows_out(c + j, (hh, hl), f"pre{2 * l}" if j == 0 else None).then_inc(w_used, 1)
                    else:
                        tokens_out(c + j, (hh, hl), 0, CW, 2 * ((c + j) % 2)).then_inc(w_used, 1)
                pe.wait_ge(drained, 2 + d + 6)

                def scores_c(n, g):
                    h, b = steps_of("C")[n]
                    r, t = 64 * (h % 2), h // 2
                    te.matmul(bank(g % 2), qC[r:r + 64, t * T + b * P:t * T + (b + 1) * P], kC[r:r + 64, t * T:(t + 1) * T],
                              start=True, stop=True).then_inc(scored, 1)

                def weigh_c(n, g):
                    h, b = steps_of("C")[n]
                    if n >= 2:
                        pe.wait_ge(o_ready, g - 1)
                    for k in range(4):
                        ins = te.matmul(bank(4 + g % 2)[:, 0:64], scratch[:, (g % 2) * T + k * P:(g % 2) * T + (k + 1) * P],
                                        vC[:, k * 512 + h * 64:k * 512 + h * 64 + 64], start=k == 0, stop=k == 3)
                    ins.then_inc(weighted, 1)

                def flush_c(n, l=l):
                    if n >= 4 and n % 2 == 0:
                        k = (n - 4) // 2
                        f = FLUSH[f"C{l}"] + k
                        pe.wait_ge(o_ready, STEPS[f"C{l}"] + 2 * k + 2)
                        if k >= 2:
                            pe.wait_ge(y_lo, f - 1)
                        te.matmul(bank(6 + f % 2)[:, 0:P], oC[:, (k % 2) * P:(k % 2) * P + P], ident[:, ::-1], start=True,
                                  stop=True).then_inc(flushed, 1)

                attention("C", STEPS[f"C{l}"], 32, scores_c, turn4(pC), weigh_c, flush_c)

                def head_mean(t, l=l):
                    n = 5 * l + t
                    pe.wait_ge(head_sq, n + 1)
                    if t:
                        pe.wait_ge(head_std, n)
                    te.matmul(bank(6), headm, tmp[n % 2], start=True, stop=True).then_inc(head_sum, 1)

                def rotate(t, l=l):
                    n = 5 * l + t
                    pe.wait_ge(head_scaled, n + 1)
                    if t >= 2:
                        pe.wait_ge(qk_ready, 6 * l + t - 1)
                    te.matmul(bank(5 + 2 * (n % 2)), rotm, tile(qA, t) if t < 4 else tile(kA, t - 4), start=True,
                              stop=True).then_inc(head_rot, 1)

                pe.wait_ge(y_lo, FLUSH[f"C{l}"] + 16)
                c, d = FIRST[f"a_qkv{l}"], DRAINS[f"a_qkv{l}"]
                for j in range(3):
                    start(c + j, d=d + j)
                    if j < 2:
                        rows_out(c + j, (hh, hl), None).then_inc(w_used, 1)
                    else:
                        rows_out(c + j, (hh, hl), None, tiles=1)
                        tokens_out(c + j, (hh, hl), P, P, 4).then_inc(w_used, 1)
                    if j == 1:
                        head_mean(0)
                        head_mean(1)
                for t in range(2, 5):
                    head_mean(t)
                rotate(0)
                rotate(1)
                c, d = FIRST[f"pu{l}"], DRAINS[f"pu{l}"]
                start(c, d=d)
                rows_out(c, (hh, hl), None).then_inc(w_used, 1)
                rotate(2)
                rotate(3)
                start(c + 1, d=d + 1)
                rows_out(c + 1, (hh, hl), None).then_inc(w_used, 1)
                rotate(4)
                pe.wait_ge(qk_ready, 6 * l + 5)
                te.matmul(bank(4), swapm, tile(kA, 0), start=True, stop=True).then_inc(swapped, 1)
                pe.wait_ge(qk_ready, 6 * l + 6)
                pe.wait_ge(drained, 2 + d + 2)

                def scores_a(n, g):
                    h, b = steps_of("A")[n]
                    r, t, kv = 64 * (h % 2), h // 2, int(h % 2 != h // 4)
                    te.matmul(bank(g % 2), qA[r:r + 64, t * T + b * P:t * T + (b + 1) * P], kA[r:r + 64, kv * T:(kv + 1) * T],
                              start=True, stop=True).then_inc(scored, 1)

                def weigh_a(n, g):
                    h, b = steps_of("A")[n]
                    if n >= 2:
                        pe.wait_ge(o_ready, g - 1)
                    for k in range(4):
                        at = k * P + 64 * (h // 4)
                        ins = te.matmul(bank(4 + g % 2)[:, 0:64], scratch[:, (g % 2) * T + k * P:(g % 2) * T + (k + 1) * P],
                                        vA[:, at:at + 64], start=k == 0, stop=k == 3)
                    ins.then_inc(weighted, 1)

                def flush_a(n, l=l):
                    if n >= 10 and (n - 10) % 8 == 0:
                        b = (n - 10) // 8
                        f = FLUSH[f"A{l}"] + b
                        pe.wait_ge(o_ready, STEPS[f"A{l}"] + 8 * b + 8)
                        if b >= 2:
                            pe.wait_ge(y_lo, f - 1)
                        for j in range(4):
                            ins = te.transpose(bank(6 + f % 2)[:, j * P:(j + 1) * P],
                                               oA[:, (b % 2) * T + j * P:(b % 2) * T + (j + 1) * P], ident)
                        ins.then_inc(flushed, 1)

                attention("A", STEPS[f"A{l}"], 32, scores_a, turn4(pA), weigh_a, flush_a)
                pe.wait_ge(y_lo, FLUSH[f"A{l}"] + 4)
                W = T + 2 * PAD
                for g in range(4):
                    pe.wait_ge(pooled, 4 * l + g + 1)
                    te.matmul(bank(2 + g), pw[:, g * P:(g + 1) * P], pu[:, g * W + PAD:g * W + PAD + T], start=True,
                              stop=True).then_inc(pool_out, 1)
                pe.wait_ge(pool_lo, 4 * l + 4)
                c, d = FIRST[f"merge{l}"], DRAINS[f"merge{l}"]
                with pe.Fori(0, 3) as n:
                    for g in range(2):
                        for j in range(2):
                            start(c + 3 * g + j, n, 6, d + 3 * g + j)
                            rows_out(c + 3 * g + j, (hh, hl), None, bank0=4 + 2 * j).then_inc(w_used, 1)
                        cc = c + 3 * g + 2
                        start(cc, n, 6, d + 3 * g + 2)
                        for t in range(4):
                            for k in range(4):
                                at = k * 512 + t * P
                                ins = mm3(bank(t), whi[cc % 2][:, at:at + P], wlo[cc % 2][:, at:at + P],
                                          tile(yh, n * 4 + k), tile(yl, n * 4 + k), k == 0, k == 3)
                        ins.then_inc(w_used, 1)
                out_product(l, (yh, yl), f"mg{l}")
                pre(2 * l + 1)
                ffn(l)
                pre(2 * l + 2)
            c, d = FIRST["cm_in"], DRAINS["cm_in"]
            for j in range(8):
                start(c + j, d=d + j)
                if j == 0:
                    pe.wait_ge(drained, 2 + d)
                rows_out(c + j, (hh, hl), "pre4" if j == 0 else None).then_inc(w_used, 1)
            for t in range(KT):
                pe.wait_ge(convolved, t + 1)
                mean_of("ln_mean", t, 7, vb)
            for t in range(KT):
                mean_of("ln_var", t, 6)
            pe.wait_ge(drained, 2 + d + 8)
            out_product(2, (uh, ul), "ln")
            pre(5)
            ffn(2)
            pre(6)
            c, d = FIRST["d_qkv"], DRAINS["d_qkv"]
            for hp in range(4):
                for g in range(3):
                    for j in range(3):
                        start(c, d=d)
                        if hp == g == j == 0:
                            pe.wait_ge(drained, 2 + d)
                        if j == 1:
                            tokens_out(c, (hh, hl), 0, CW, 2 * (c % 2)).then_inc(w_used, 1)
                        else:
                            bufs, split = ((hh, hl), "pre6") if j == 0 else ((qh, ql), "hq")
                            rows_out(c, bufs, split if hp == g == 0 else None).then_inc(w_used, 1)
                        c, d = c + 1, d + 1
                pe.wait_ge(drained, 2 + d)

                def scores_d(n, g, hp=hp):
                    m, b = steps_of("D")[n]

                    def at(buf, i):
                        return buf[:, (2 * i + m) * T + b * P:(2 * i + m) * T + (b + 1) * P]
                    te.matmul(bank(2 * (g % 2)), at(qD, 0), kD[:, m * T:(m + 1) * T], start=True, stop=True)
                    te.matmul(bank(2 * (g % 2) + 1)[:, 0:P], at(qD, 1), at(kD, 1), start=True, stop=True)
                    te.matmul(bank(2 * (g % 2) + 1)[:, P:2 * P], at(qD, 2), at(kD, 2), start=True, stop=True).then_inc(scored, 1)

                def turn_d(n, g):
                    if n >= 1:
                        pe.wait_ge(pt_ready, g)
                    for j in range(6):
                        ins = te.transpose(bank(4, 2)[:, j * P:(j + 1) * P],
                                           pD[:, (g % 2) * 768 + j * P:(g % 2) * 768 + (j + 1) * P], ident)
                    ins.then_inc(turned, 1)

                def weigh_d(n, g):
                    m, b = steps_of("D")[n]
                    if n >= 1:
                        pe.wait_ge(o_ready, g)
                    keys = [(k, 0) for k in range(4)] + [(b, 1), (b, 2)]
                    for j, (k, i) in enumerate(keys):
                        at = k * 768 + i * CW + m * P
                        ins = te.matmul(bank(6)[:, 0:P], scratch[:, (g % 2) * 768 + j * P:(g % 2) * 768 + (j + 1) * P],
                                        vD[:, at:at + P], start=j == 0, stop=j == 5)
                    ins.then_inc(weighted, 1)

                def flush_d(n, hp=hp):
                    if 3 <= n < 11:
                        f = 8 * hp + n - 3
                        pe.wait_ge(o_ready, STEPS["D"] + f + 1)
                        if n >= 4:
                            pe.wait_ge(y_lo, FLUSH["D"] + f)
                        te.transpose(bank(7)[:, 0:P], oD[:, (f % 2) * P:(f % 2) * P + P], ident).then_inc(flushed, 1)

                attention("D", STEPS["D"] + 8 * hp, 8, scores_d, turn_d, weigh_d, flush_d)
            out_product(3, (qh, ql), "y")
            pre(7)
            ffn(3)
            pe.wait_ge(x_new, 8 * KT)
            for n in range(8):
                b, half = n // 2, n % 2
                if n >= 4:
                    pe.wait_ge(init_out, 11 + n - 3)
                for j in range(4):
                    t = 4 * half + j
                    ins = te.transpose(bank(n % 4)[:, j * P:(j + 1) * P], x[:, t * T + b * P:t * T + (b + 1) * P], ident)
                ins.then_inc(init_turn, 1)


def kernel(**inputs):
    import numpy as _np
    import concourse.bacc as _bacc
    from concourse import mybir as _mybir
    from concourse.bass_utils import run_bass_kernel_spmd as _run

    nc = _bacc.Bacc("TRN2", target_bir_lowering=False, num_devices=1)
    arrays = {n: _np.ascontiguousarray(a) for n, a in inputs.items() if n != "rpb"}
    arrays["rpbp"] = _np.pad(_np.ascontiguousarray(inputs["rpb"]).reshape(1, -1), ((0, 0), (RPB_PAD, RPB_PAD)))
    arrays.update(host_constants())
    maps, aps = {}, {}
    for n, a in arrays.items():
        maps[f"in_{n}_dram"] = a
        aps[n] = nc.dram_tensor(f"in_{n}_dram", a.shape, _mybir.dt.from_np(a.dtype), kind="ExternalInput").ap()
    out = nc.dram_tensor("out_0_dram", (1, T, D), F32, kind="ExternalOutput").ap()
    build(nc, aps, out)
    r = _run(nc, [maps], core_ids=[0])
    return r.results[0]["out_0_dram"]
```

```python
from contextlib import ExitStack

import numpy as np

import concourse.bass as bass
from concourse import mybir

F32 = mybir.dt.float32
F32R = mybir.dt.float32r
ALU = mybir.AluOpType
ACT = mybir.ActivationFunctionType
AX = mybir.AxisListType

P = 128
T = 512
D = 1024
KT = D // P
D_IN = 5888
FF = 2816
FT = FF // P
EPS = 1e-6
NEG = -1e30
CH = 2048
CW = CH // KT
POOL_WINDOWS = (2, 4, 8, 16)
PAD = 8
TAPS = 31
PE_TAPS = 10
GRID = 64
NA_COLS = 16
RPB_PAD = 64
E2C = 14 * GRID
SD = 128 ** -0.5

QA, KA, VA, PU, QC, KC, VC, GL = 0, 512, 640, 768, 1280, 1792, 2304, 2816

PLAN = []
for _l in range(2):
    PLAN += [(f"c_qkv{_l}", 6), (f"a_qkv{_l}", 3), (f"pu{_l}", 2), (f"merge{_l}", 18), (f"out{_l}", 4),
             (f"up{_l}", FT), (f"down{_l}", 12)]
PLAN += [("cm_in", 8), ("out2", 4), (f"up2", FT), ("down2", 12), ("d_qkv", 36), ("out3", 4), ("up3", FT), ("down3", 12)]
FIRST, DRAINS = {}, {}
_c = _d = 0
for _name, _n in PLAN:
    FIRST[_name], DRAINS[_name] = _c, _d
    _c += _n
    _d += 0 if _name.startswith("up") else _n
CHUNKS = _c

ROWS = {}
_r = 0
for _name, _n in [("norm_mix_pre", 16), ("norm_mix_post", 16), ("norm_ffn_pre", 16), ("norm_ffn_post", 16),
                  ("b_gate", 48), ("pool_scale", 8), ("qkg", 4), ("conv_w", 264), ("conv_b", 88),
                  ("mix_pre_g_2", 16), ("mix_post_g_2", 16), ("ffn_pre_g_2", 16), ("ffn_post_g_2", 16),
                  ("cm_b_in_2", 16), ("cm_dw_2", 248), ("cm_dw_b_2", 8), ("cm_ln_g_2", 8), ("cm_ln_b_2", 8),
                  ("cm_b_out_2", 8), ("kv_norm_g_2", 8), ("ffn_dw_2", 264), ("ffn_dw_b_2", 88)]:
    ROWS[_name] = (_r, _n)
    _r += _n
ROWS_ALL = _r
ROW_TILES = -(-ROWS_ALL // P)

STEPS = {"C0": 0, "A0": 32, "C1": 64, "A1": 96, "D": 128}
SLOTS = 3
PAIRS = {"C0": 0, "A0": 4, "C1": 8, "A1": 12, "D": 16}
NORMS = ["pre0"]
for _h in range(8):
    if _h == 4:
        NORMS += ["ln_mean", "ln_var"]
    NORMS += [f"post{_h}"] + ([f"pre{_h + 1}"] if _h < 7 else [])
NORM = {n: i for i, n in enumerate(NORMS)}
SQUARES = {n: 8 * i for i, n in enumerate(n for n in NORMS if n != "ln_mean")}
SPLITS = ["pre0", "mg0", "pre1", "pre2", "mg1", "pre3", "pre4", "ln", "pre5", "pre6", "hq", "y", "pre7"]
SPLIT = {n: 8 * i for i, n in enumerate(SPLITS)}
SCALED = {n: 8 * i for i, n in enumerate(n for n in SPLITS if n[0] in "ph")}


def host_constants():
    ident = np.eye(P, dtype=np.float32)
    head = np.kron(np.eye(2), np.full((64, 64), 1 / 64)).astype(np.float32)
    mean = np.full((P, P), 1 / D, np.float32)
    rot = np.zeros((P, P), np.float32)
    for m in range(P):
        rot[m + 16 if m % 32 < 16 else m - 16, m] = -1.0 if m % 32 < 16 else 1.0
    t = np.arange(T)
    freqs = np.float32(10000.0) ** (-np.arange(0, 32, 2, dtype=np.float32) / np.float32(32))
    p = np.arange(P)
    pos = np.where((p % 64 < 32)[:, None], (t // GRID)[None], (t % GRID)[None]).astype(np.float32)
    ang = pos * freqs[p % 16][:, None].astype(np.float32)
    cos, sin = np.cos(ang).astype(np.float32), np.sin(ang).astype(np.float32)
    col = np.arange(GRID)
    start = np.clip(col - NA_COLS // 2, 0, GRID - NA_COLS)
    inside = (col[None] >= start[:, None]) & (col[None] < start[:, None] + NA_COLS)
    cmask = np.tile(np.where(inside, 0, NEG).astype(np.float32)[::-1], (2, 1))
    edge = np.ones((len(POOL_WINDOWS), 2 * PAD), np.float32)
    for g, w in enumerate(POOL_WINDOWS):
        count = np.clip(t + w - w // 2, 0, T) - np.clip(t - w // 2, 0, T)
        edge[g] = np.float32(w) / np.concatenate([count[:PAD], count[-PAD:]]).astype(np.float32)
    edge = np.tile(edge.reshape(1, -1), (P, 1))
    l, m = np.arange(P)[:, None], np.arange(P)[None]
    band = [np.where((4 * (l - m) + d >= 0) & (4 * (l - m) + d <= 128), 0, NEG) for d in range(3, -4, -1)]
    causal = np.where(l >= m, 0, NEG)
    strided = np.where((l >= m) & ((l - m) % 4 == 0), 0, NEG)
    dmask = np.concatenate(band + [causal, strided], axis=1).astype(np.float32)
    return {"c_base": np.concatenate([ident, head, mean, rot, np.roll(ident, 64, axis=1)], axis=1), "c_rope": np.concatenate([cos, sin], axis=1),
            "c_cmask": cmask, "c_edge": edge, "c_dmask": dmask}


class Chain:

    def __init__(self, eng, sem):
        self.eng, self.sem, self.n, self.shift = eng, sem, 0, 0

    def mark(self, ins):
        ins.then_inc(self.sem, 1)
        self.n += 1
        return self.n

    def wait(self, value):
        self.eng.wait_ge(self.sem, value + self.shift)

    def link(self, ins):
        self.wait(self.mark(ins))


def build(nc, A, out):
    with ExitStack() as ctx:
        def sb(name, cols, dt=F32, stack=ctx):
            return stack.enter_context(nc.sbuf_tensor("t_" + name, [P, cols], dt))

        def sem(name):
            return ctx.enter_context(nc.semaphore(name))

        wraw = [sb(f"wraw{s}", CH) for s in range(2)]
        whi = [sb(f"whi{s}", CH, F32R) for s in range(2)]
        wlo = [sb(f"wlo{s}", CH, F32R) for s in range(2)]
        x = sb("x", KT * T)
        base = sb("base", 5 * P)
        pvec = sb("pvec", ROW_TILES * P)
        scratch = sb("scratch", 3 * T)
        small = sb("small", 32)
        ident, headm, meanm, rotm, swapm = (base[:, i * P:(i + 1) * P] for i in range(5))
        tmp = [scratch[:, 0:T], scratch[:, T:2 * T]]
        std = scratch[:, 2 * T:3 * T]
        roots, rroots = small[:, 20:24], small[:, 24:28]
        epsc = small[:, 31:32]
        with ExitStack() as s:
            hh, hl = sb("hh", KT * T, F32R, s), sb("hl", KT * T, F32R, s)
        hbufs = ctx.enter_context(ExitStack())
        mix, sq = sb("mix", KT * T, stack=hbufs), sb("sq", KT * T, stack=hbufs)

        with ExitStack() as s:
            prow, xrow = sb("prow", ROW_TILES * P, stack=s), sb("xrow", 4 * D, stack=s)
        with ExitStack() as s:
            yh, yl = sb("yh", 12 * T, F32R, s), sb("yl", 12 * T, F32R, s)
            with ExitStack() as u:
                qC, kC, vC = sb("qC", 4 * T, stack=u), sb("kC", 4 * T, stack=u), sb("vC", 4 * T, stack=u)
                e2 = [sb(f"e2{i}", 2 * E2C, stack=u) for i in range(2)]
                pC = sb("pC", SLOTS * T, stack=u)
                cmask = sb("cmask", GRID, stack=u)
            with ExitStack() as u:
                qA, kA, vA = sb("qA", 4 * T, stack=u), sb("kA", 2 * T, stack=u), sb("vA", T, stack=u)
                rope = sb("rope", 2 * T, stack=u)
                pA = sb("pA", SLOTS * T, stack=u)
                pw = sb("pw", 4 * P, stack=u)
                pu = sb("pu", 4 * (T + 2 * PAD), stack=u)
                win = [sb(f"win{i}", T + 2 * PAD, stack=u) for i in range(2)]
                edge = sb("edge", len(POOL_WINDOWS) * 2 * PAD, stack=u)
            with ExitStack() as u:
                gates, mg = sb("gates", 4 * T, stack=u), sb("mg", KT * T, stack=u)
        with ExitStack() as s:
            midh, midl = sb("midh", FT * T, F32R, s), sb("midl", FT * T, F32R, s)
            accv, accg = sb("accv", 2 * T, stack=s), sb("accg", 2 * T, stack=s)
        with ExitStack() as s:
            uh, ul = sb("uh", KT * T, F32R, s), sb("ul", KT * T, F32R, s)
            UW = T + TAPS - 1
            ub, vb = sb("ub", KT * UW, stack=s), sb("vb", KT * T, stack=s)
            tapd = sb("tapd", 4 * PE_TAPS * P, stack=s)
        with ExitStack() as s:
            qh, ql = sb("qh", KT * T, F32R, s), sb("ql", KT * T, F32R, s)
            yD = sb("yD", KT * T, stack=s)
            qD, kD, vD = (sb(n, 6 * T, stack=s) for n in ("qD", "kD", "vD"))
            pD = sb("pD", SLOTS * 768, stack=s)
            dmask = sb("dmask", 9 * P, stack=s)

        ps = ctx.enter_context(nc.psum_tensor("ps", [P, 8 * T], F32))

        def bank(b, n=1):
            return ps[:, b * T:(b + n) * T]

        w_loaded = [sem("w_loaded0"), sem("w_loaded1")]
        w_hi, w_lo, w_used = sem("w_hi"), sem("w_lo"), sem("w_used")
        drained = sem("drained")
        conv_done = sem("conv_done")
        mid_lo = sem("mid_lo")
        affine, acted, product, mid_hi = sem("affine"), sem("acted"), sem("product"), sem("mid_hi")
        init_in, init_turn, init_out = sem("init_in"), sem("init_turn"), sem("init_out")
        stored = sem("stored")
        squared, summed, rooted, x_tmp, x_new = (sem(n) for n in ("squared", "summed", "rooted", "x_tmp", "x_new"))
        diagonal, spread, sq_added = sem("diagonal"), sem("spread"), sem("sq_added")
        h_tmp, h_hi, h_lo = sem("h_tmp"), sem("h_hi"), sem("h_lo")
        gate_sig, head_sq, head_sum, head_std, head_scaled, head_rot = (
            sem(n) for n in ("gate_sig", "head_sq", "head_sum", "head_std", "head_scaled", "head_rot"))
        qk_ready, swapped = sem("qk_ready"), sem("swapped")
        scored, maxed, probs, scaled, turned, pt_ready, weighted, y_hi, y_lo = (
            sem(n) for n in ("scored", "maxed", "probs", "scaled", "turned", "pt_ready", "weighted", "y_hi", "y_lo"))
        e2_loaded = [sem("e2_loaded0"), sem("e2_loaded1")]
        e2_ready, tables = sem("e2_ready"), sem("tables")
        pu_in, pooled, pool_out = sem("pu_in"), sem("pooled"), sem("pool_out")
        u_ready, taps_in, tapped, u_sig, convolved, centred, ln_scaled = sem("u_ready"), sem("taps_in"), sem("tapped"), sem("u_sig"), sem("convolved"), sem("centred"), sem("ln_scaled")
        pool_hi, pool_lo, merged = sem("pool_hi"), sem("pool_lo"), sem("merged")
        dve_self, act_self, pool_self = sem("dve_self"), sem("act_self"), sem("pool_self")

        def col(name, i=0):
            if isinstance(i, int):
                return pvec[:, ROWS[name][0] + i:ROWS[name][0] + i + 1]
            return pvec[:, bass.ds(i + ROWS[name][0], 1)]

        def tile(buf, t, n=1):
            if isinstance(t, int):
                return buf[:, t * T:(t + n) * T]
            return buf[:, bass.ds(t * T, n * T)]

        def MEAN_BANK(name):
            return 7 if name[:4] == "post" else 6

        def permuted(ap):
            return ap.rearrange("p (l b) -> p b l", b=4)

        def by4(ap):
            return ap.rearrange("p (b l) -> p b l", b=4)

        def backward(ap):
            return by4(ap)[:, :, ::-1]

        FFN = [("w_up", "w_down", 0, "conv_w", "conv_b"), ("w_up", "w_down", 1, "conv_w", "conv_b"),
               ("ffn_w_in_2", "ffn_w_out_2", 0, "ffn_dw_2", "ffn_dw_b_2"),
               ("ffn_w_in_2", "ffn_w_out_2", 1, "ffn_dw_2", "ffn_dw_b_2")]
        POST = [("norm_mix_post", 0), ("norm_ffn_post", 0), ("norm_mix_post", 1), ("norm_ffn_post", 1),
                ("mix_post_g_2", 0), ("ffn_post_g_2", 0), ("mix_post_g_2", 1), ("ffn_post_g_2", 1)]
        PRE = [("norm_mix_pre", 0), ("norm_ffn_pre", 0), ("norm_mix_pre", 1), ("norm_ffn_pre", 1),
               ("mix_pre_g_2", 0), ("ffn_pre_g_2", 0), ("kv_norm_g_2", 0), ("ffn_pre_g_2", 1)]

        param_loads = []
        for name, (r0, n) in ROWS.items():
            if name == "qkg":
                for i, a in enumerate((A["qk_norm_q"], A["qk_norm_k"])):
                    for l in range(2):
                        for half in range(2):
                            r, c0 = r0 + 2 * i + l, 64 * half
                            at0 = (r // P) * P + c0
                            param_loads.append((prow[r % P:r % P + 1, at0:at0 + 64], a[l:l + 1, :]))
                continue
            flat = A[name]
            if len(flat.shape) == 3:
                flat = flat.rearrange("a b c -> (a b) c")
            flat = (flat.rearrange("a (n p) -> (a n) p", p=P) if len(flat.shape) == 2 else
                    flat.rearrange("(n p) -> n p", p=P))
            done = 0
            while done < n:
                r = r0 + done
                k = min(n - done, P - r % P)
                param_loads.append((prow[r % P:r % P + k, (r // P) * P:(r // P + 1) * P], flat[done:done + k, :]))
                done += k

        def steps_of(kind):
            if kind[0] == "D":
                return [(m, b) for m in range(2) for b in range(4)]
            return [(2 * hp + s, b) for hp in range(4) for s in range(2) for b in range(4)]

        OUT_TURNS = 3 + 8 + 8
        block = ctx.enter_context(nc.Block())

        def half_layer_tail(sp, load, at, rows, f, w_out):
            c = FIRST[f"out{f}"]
            for j in range(4):
                load(at(c + j), w_out[:, :, CW * j:CW * (j + 1)])
            up, down, l = FFN[f][:3]
            w = rows(A[up], l)
            c = FIRST[f"up{f}"]
            with sp.Fori(0, FT // 2) as i:
                for s in range(2):
                    load(at(c + s, i, 2), w[:, :, bass.ds(i * CW + FF * s, CW)])
            w = rows(A[down], l)
            c = FIRST[f"down{f}"]
            for half in range(2):
                for j in range(6):
                    k = min(4, FT - 4 * j)
                    load(at(c + 6 * half + j), w[:, 4 * j:4 * j + k, 512 * half:512 * half + 512], k * 512)

        @block.sync
        def _(sp):
            def load(c, src, cols=CH):
                c, slot, turn = c
                if not isinstance(c, int) or c >= 2:
                    sp.wait_ge(w_lo, c - 1)
                sp.dma_start(wraw[slot][:, 0:cols].rearrange("p (k n) -> p k n", n=src.shape[-1]),
                             src).then_inc(w_loaded[slot], 16)

            def at(c, i=None, per=0):
                if i is None:
                    return c, c % 2, c // 2
                return i * per + c, c % 2, i * (per // 2) + c // 2

            def rows(w, l):
                return w[l].rearrange("(k p) n -> p k n", p=P)

            for dst, src in param_loads:
                sp.dma_start(dst, src).then_inc(init_in, 16)

            for l in range(2):
                w = rows(A["w_in"], l)
                c = FIRST[f"c_qkv{l}"]
                for j, n0 in enumerate([QC, QC + CW, KC, KC + CW, VC, VC + CW]):
                    load(at(c + j), w[:, :, n0:n0 + CW])
                c = FIRST[f"a_qkv{l}"]
                for j in range(2):
                    load(at(c + j), w[:, :, QA + CW * j:QA + CW * (j + 1)])
                load(at(c + 2), w[:, :, KA:KA + CW])
                c = FIRST[f"pu{l}"]
                for j in range(2):
                    load(at(c + j), w[:, :, PU + CW * j:PU + CW * (j + 1)])
                c = FIRST[f"merge{l}"]
                wb = A["w_branch"][l].rearrange("b (k p) n -> p (b k) n", p=P)
                with sp.Fori(0, 3) as n:
                    for g in range(2):
                        for j in range(2):
                            load(at(c + 3 * g + j, n, 6), w[:, :, bass.ds(n * D + (GL + 512 * g + CW * j), CW)])
                        load(at(c + 3 * g + 2, n, 6), wb[:, bass.ds(n * 4, 4), 512 * g:512 * g + 512])
                half_layer_tail(sp, load, at, rows, l, rows(A["w_out"], l))
            c = FIRST["cm_in"]
            w = rows(A["cm_w_in_2"], 0)
            for j in range(4):
                load(at(c + 2 * j), w[:, :, CW * j:CW * (j + 1)])
                load(at(c + 2 * j + 1), w[:, :, D + CW * j:D + CW * (j + 1)])
            half_layer_tail(sp, load, at, rows, 2, rows(A["cm_w_out_2"], 0))
            c = FIRST["d_qkv"]
            wkv = A["w_kv_2"].rearrange("(k p) n -> p k n", p=P)
            wq = rows(A["w_q_2"], 0)
            for hp in range(4):
                for g in range(3):
                    n0 = D * g + CW * hp
                    load(at(c), wkv[:, :, n0:n0 + CW])
                    load(at(c + 1), wkv[:, :, 3 * D + n0:3 * D + n0 + CW])
                    load(at(c + 2), wq[:, :, n0:n0 + CW])
                    c += 3
            half_layer_tail(sp, load, at, rows, 3, rows(A["w_o_2"], 0))
            sp.wait_ge(init_out, OUT_TURNS)
            for b in range(4):
                sp.dma_start(out[0, b * P:(b + 1) * P, :], xrow[:, b * D:(b + 1) * D]).then_inc(stored, 16)
            sp.wait_ge(stored, 16 * 4)

        @block.gpsimd
        def _(pool):
            ch = Chain(pool, pool_self)
            gp = nc.gpsimd

            def tables_in(pairs, wait):
                for buf, name in pairs:
                    pool.dma_start(buf, A[name]).then_inc(tables, 16)

            nt = [0]

            def const(buf, src):
                pool.dma_start(buf, src).then_inc(tables, 16)
                nt[0] += 16
                return nt[0]

            const(base[:, :], A["c_base"])
            for b in range(4):
                const(xrow[:, b * D:(b + 1) * D], A["x"][0, b * P:(b + 1) * P, :])
            ch.mark(gp.memset(epsc, EPS))

            def add_squares(name):
                n = None
                for t in range(1, KT):
                    pool.wait_ge(squared, SQUARES[name] + t + 1)
                    if n:
                        ch.wait(n)
                    ins = gp.tensor_tensor(tile(sq, 0), tile(sq, 0), tile(sq, t), ALU.add)
                    if t < KT - 1:
                        n = ch.mark(ins)
                ins.then_inc(sq_added, 1)

            add_squares("pre0")
            for l in range(2):
                if l == 0:
                    pool.wait_ge(init_out, 3 + 8)
                else:
                    pool.wait_ge(w_used, FIRST[f"c_qkv{l}"])
                    pool.wait_ge(mid_lo, 2 + FT * l)
                pool.wait_ge(tables, nt[0])
                pool.wait_ge(tables, const(cmask[:, :], A["c_cmask"]))
                for hp in range(4):
                    if hp >= 2:
                        pool.wait_ge(maxed, STEPS[f"C{l}"] + 8 * (hp - 1))
                    for s in range(2):
                        for half in range(2):
                            src = bass.AP(tensor=A["rpbp"].tensor, ap=[[1, GRID], [31, 14], [1, GRID]],
                                          offset=RPB_PAD + ((l * 8 + 2 * hp + s) * 15 + half) * 31 + 15 - 63)
                            pool.dma_start(e2[hp % 2][64 * half:64 * half + 64, s * E2C:(s + 1) * E2C].rearrange(
                                "p (r k) -> p r k", k=GRID), src).then_inc(e2_loaded[hp % 2], 16)
                    pool.wait_ge(e2_loaded[hp % 2], 64 * (2 * l + hp // 2 + 1))
                    v = e2[hp % 2][:, :].rearrange("p (r k) -> p r k", k=GRID)
                    m = cmask[:, :].rearrange("p (o k) -> p o k", o=1).broadcast_to([P, 28, GRID])
                    gp.tensor_tensor(v, v, m, ALU.add).then_inc(e2_ready, 1)
                pool.wait_ge(y_lo, PAIRS[f"C{l}"] + 4)
                const(rope[:, :], A["c_rope"])
                const(pw[:, :].rearrange("p (g d) -> p g d", g=4), A["w_pool"][l].rearrange("g c d -> c g d"))
                k = const(edge[:, :], A["c_edge"])
                W = T + 2 * PAD
                for g in range(4):
                    for a, b in ((0, PAD), (T + PAD, W)):
                        n = ch.mark(gp.memset(pu[:, g * W + a:g * W + b], 0.0))
                pool.wait_ge(tables, k)
                for g, w in enumerate(POOL_WINDOWS):
                    pool.wait_ge(pu_in, 2 * l + g // 2 + 1)
                    if g:
                        pool.wait_ge(pooled, 4 * l + g)
                    ch.wait(n)
                    u = pu[:, g * W:(g + 1) * W]
                    n = ch.mark(gp.tensor_tensor(win[0][:, 1:W], u[:, 0:W - 1], u[:, 1:W], ALU.add))
                    have, cur, lo = 2, 0, 1
                    while have < w:
                        ch.wait(n)
                        s = have // 2
                        lo += s
                        hi = W - lo + 1
                        n = ch.mark(gp.tensor_tensor(win[1 - cur][:, lo:hi], win[cur][:, lo - s:hi - s],
                                                     win[cur][:, lo + s:hi + s], ALU.add))
                        have, cur = 2 * have, 1 - cur
                    ch.wait(n)
                    e = edge[:, g * 2 * PAD:(g + 1) * 2 * PAD]
                    ch.mark(gp.tensor_tensor(win[cur][:, PAD:2 * PAD], win[cur][:, PAD:2 * PAD], e[:, 0:PAD], ALU.mult))
                    n = ch.mark(gp.tensor_tensor(win[cur][:, T:T + PAD], win[cur][:, T:T + PAD], e[:, PAD:2 * PAD], ALU.mult))
                    ch.wait(n)
                    mean = win[cur][:, PAD:PAD + T]
                    ch.link(gp.tensor_scalar(mean, mean, 1.0 / w, None, ALU.mult))
                    gp.tensor_tensor(u[:, PAD:PAD + T], mean, u[:, PAD:PAD + T], ALU.subtract).then_inc(pooled, 1)
                for name in (f"post{2 * l}", f"pre{2 * l + 1}", f"post{2 * l + 1}", f"pre{2 * l + 2}"):
                    add_squares(name)
            for name in ("ln_var", "post4", "pre5", "post5", "pre6"):
                add_squares(name)
            pool.wait_ge(w_used, FIRST["d_qkv"])
            pool.wait_ge(mid_lo, 2 + 3 * FT)
            const(dmask[:, :], A["c_dmask"])
            for name in ("post6", "pre7", "post7"):
                add_squares(name)

        @block.scalar
        def _(act):
            ch = Chain(act, act_self)
            sc = nc.scalar

            def hi(c, i=None, per=0):
                cc, slot = (c, c % 2) if i is None else (i * per + c, c % 2)
                act.wait_ge(w_used, cc + 1)
                if isinstance(cc, int) and cc + 2 >= CHUNKS:
                    return
                act.wait_ge(w_loaded[slot], (cc // 2 + 2) * 16 if i is None else i * (per * 8) + (c // 2 + 2) * 16)
                sc.activation(whi[slot][:, :], wraw[slot][:, :], ACT.Copy).then_inc(w_hi, 1)

            def split_hi(name, src, dst, ready, n=KT):
                for t in range(n):
                    ready(t)
                    sc.activation(dst(t), src(t), ACT.Copy).then_inc(h_hi, 1)

            def root(name):
                m = NORM[name]
                if m == 0:
                    act.wait_ge(pool_self, 1)
                sc.activation(small[:, 19:20], epsc, ACT.Sqrt)
                act.wait_ge(summed, m + 1)
                sc.activation(roots, bank(MEAN_BANK(name))[:, 0:4], ACT.Sqrt, bias=epsc).then_inc(rooted, 1)

            def h_split(name, dsth, view=lambda a: a):
                for t in range(KT):
                    act.wait_ge(h_tmp, SCALED[name] + t + 1)
                    sc.activation(tile(dsth, t), tmp[t % 2], ACT.Copy).then_inc(h_hi, 1)

            def squares_of_x(name):
                for t in range(KT):
                    if name == "pre0":
                        act.wait_ge(init_out, 3 + t + 1)
                    else:
                        act.wait_ge(x_new, KT * (int(name[3:]) - 1) + t + 1)
                    sc.activation(tile(sq, t), tile(x, t), ACT.Square).then_inc(squared, 1)

            def pre(h, second=None):
                name = f"pre{h}"
                squares_of_x(name)
                root(name)
                h_split(name, hh)
                if second:
                    h_split("hq", qh)

            def attention(kind, n0, count, width, pbuf, from_psum):
                for n in range(count + 3):
                    if n < count:
                        s = (n0 + n) % SLOTS
                        act.wait_ge(maxed, n0 + n + 1)
                        if n >= SLOTS:
                            act.wait_ge(turned, n0 + n - SLOTS + 1)
                        q = (n0 + n) % 4
                        src = from_psum((n0 + n) % 2) if from_psum else pbuf[:, s * width:(s + 1) * width]
                        sc.activation(pbuf[:, s * width:(s + 1) * width], src, ACT.Exp, bias=small[:, q:q + 1],
                                      scale={"A": 0.125, "C": 1.0, "D": SD}[kind],
                                      accum_out=small[:, 8 + q:9 + q]).then_inc(probs, 1)
                    if 1 <= n <= count:
                        m = n0 + n - 1
                        act.wait_ge(turned, m + 1)
                        if n >= 3:
                            act.wait_ge(weighted, m - 1)
                        src = bank(4, 2)[:, 0:768] if kind == "D" else bank(2 + m % 2)
                        sc.activation(scratch[:, (m % 2) * width:(m % 2) * width + width], src,
                                      ACT.Copy).then_inc(pt_ready, 1)
                    if kind != "D" and n >= 10 and (n - 10) % 8 == 0:
                        y_round(n0, (n - 10) // 8, 8 if kind == "C" else 0)

            def y_round(n0, hp, t0):
                act.wait_ge(weighted, n0 + 8 * hp + 8)
                src, dst = bank(4 + hp % 2), tile(yh, t0 + hp)
                if t0:
                    src, dst = backward(src), by4(dst)
                sc.activation(dst, src, ACT.Copy).then_inc(y_hi, 1)

            def out_rows(f, extra_bias=None, view=lambda a: a):
                c = FIRST[f"out{f}"]
                for j in range(4):
                    hi(c + j)
                    for m in range(2):
                        t = 2 * j + m
                        b = {"bias": col(extra_bias, t)} if extra_bias else {}
                        sc.activation(view(tile(sq, t)), by4(bank(2 * (j % 2) + m)) if f == 3 else bank(2 * (j % 2) + m),
                                      ACT.Square, **b).then_inc(squared, 1)
                root(f"post{2 * f}")

            def ffn(f):
                fn = ACT.Gelu_apprx_tanh if f < 2 else ACT.Silu
                _, _, l, cw, cb = FFN[f]
                centre = 1 if f < 2 else 2
                c = FIRST[f"up{f}"]
                m0 = FT * f
                with act.Fori(0, FT // 2) as i:
                    for s, acc in enumerate((accv, accg)):
                        hi(c + s, i, 2)
                        for m in range(2):
                            if s == 0:
                                act.wait_ge(mid_lo, i * 2 + (m0 + m + 1))
                            r = i * 2 + (s * FT + m)
                            sc.activation(tile(acc, m), bank(2 * s + m), ACT.Identity,
                                          bias=col(cb, r + 2 * FT * l),
                                          scale=col(cw, r + 2 * FT * (3 * l + centre))).then_inc(affine, 1)
                    for m in range(2):
                        act.wait_ge(conv_done, i * 4 + (4 + 2 * m0 + 2 + m + 1))
                        sc.activation(tile(accg, m), tile(accg, m), fn).then_inc(acted, 1)
                    for m in range(2):
                        act.wait_ge(product, i * 2 + (m0 + m + 1))
                        sc.activation(tile(midh, i * 2 + m), tile(accv, m), ACT.Copy).then_inc(mid_hi, 1)
                c = FIRST[f"down{f}"]
                for half in range(2):
                    for j in range(6):
                        hi(c + 6 * half + j)
                    for t in range(4):
                        sc.activation(tile(sq, 4 * half + t), bank(4 * (1 - half) + t), ACT.Square).then_inc(squared, 1)
                root(f"post{2 * f + 1}")

            for c in range(2):
                act.wait_ge(w_loaded[c], 16)
                sc.activation(whi[c][:, :], wraw[c][:, :], ACT.Copy).then_inc(w_hi, 1)
            pre(0)
            for l in range(2):
                c = FIRST[f"c_qkv{l}"]
                for j in range(6):
                    hi(c + j)

                attention("C", STEPS[f"C{l}"], 32, T, pC, None)
                c = FIRST[f"a_qkv{l}"]
                for j in range(3):
                    hi(c + j)
                    for m in range(2 if j < 2 else 1):
                        t = 5 * l + 2 * j + m
                        if t >= 2:
                            act.wait_ge(head_sum, t - 1)
                        sc.activation(tmp[t % 2], bank(2 * ((c + j) % 2) + m), ACT.Square).then_inc(head_sq, 1)
                    for m in range(2 if j < 2 else 1):
                        t = 5 * l + 2 * j + m
                        act.wait_ge(head_sum, t + 1)
                        if t >= 1:
                            act.wait_ge(head_scaled, t)
                        sc.activation(std, bank(6), ACT.Sqrt, bias=epsc).then_inc(head_std, 1)
                c = FIRST[f"pu{l}"]
                W = T + 2 * PAD
                for j in range(2):
                    hi(c + j)
                    sc.activation(pu[:, 2 * j * W:2 * (j + 1) * W].rearrange("p (m w) -> p m w", m=2)[:, :, PAD:PAD + T],
                                  bank(2 * ((c + j) % 2), 2).rearrange("p (m w) -> p m w", m=2), ACT.Copy).then_inc(pu_in, 1)

                attention("A", STEPS[f"A{l}"], 32, T, pA, lambda s: bank(s))
                for g in range(4):
                    act.wait_ge(pool_out, 4 * l + g + 1)
                    sc.activation(tile(yh, 4 + g), bank(2 + g), ACT.Copy, scale=col("pool_scale", 4 * l + g)).then_inc(pool_hi, 1)
                c = FIRST[f"merge{l}"]
                d = DRAINS[f"merge{l}"]
                with act.Fori(0, 3) as n:
                    for g in range(2):
                        for j in range(2):
                            hi(c + 3 * g + j, n, 6)
                            act.wait_ge(drained, n * 6 + (2 + d + 3 * g + j + 1))
                            sc.activation(tile(gates, 2 * j, 2), tile(gates, 2 * j, 2), ACT.Sigmoid).then_inc(gate_sig, 1)
                        hi(c + 3 * g + 2, n, 6)
                for t in range(KT):
                    act.wait_ge(merged, 6 * (l + 1))
                    sc.activation(tile(yh, t), tile(mg, t), ACT.Copy).then_inc(h_hi, 1)
                out_rows(l)
                pre(2 * l + 1)
                ffn(l)
                pre(2 * l + 2)
            def tap_diagonals(j):
                if j >= 2:
                    act.wait_ge(tapped, 2 * (j - 1))
                for m in range(2):
                    t = 2 * j + m
                    for i in range(PE_TAPS):
                        at = ((t % 4) * PE_TAPS + i) * P
                        ins = sc.activation(tapd[:, at:at + P], ident, ACT.Copy, scale=col("cm_dw_2", 8 * (TAPS - PE_TAPS + i) + t))
                    ins.then_inc(taps_in, 1)

            c = FIRST["cm_in"]
            for j in range(4):
                hi(c + 2 * j)
                hi(c + 2 * j + 1)
                for m in range(2):
                    act.wait_ge(drained, 2 + DRAINS["cm_in"] + 2 * j)
                    sc.activation(tmp[m], bank(2 * ((c + 1) % 2) + m), ACT.Sigmoid, bias=col("cm_b_in_2", 8 + 2 * j + m)).then_inc(u_sig, 1)
                tap_diagonals(j)
            for t in range(KT):
                act.wait_ge(centred, t + 1)
                sc.activation(tile(sq, t), tile(vb, t), ACT.Square).then_inc(squared, 1)
            root("ln_var")
            for t in range(KT):
                act.wait_ge(ln_scaled, t + 1)
                ch.link(sc.activation(tile(vb, t), tile(vb, t), ACT.Silu, scale=col("cm_ln_g_2", t), bias=col("cm_ln_b_2", t)))
                sc.activation(tile(uh, t), tile(vb, t), ACT.Copy).then_inc(h_hi, 1)
            out_rows(2, "cm_b_out_2")
            pre(5)
            ffn(2)
            pre(6, second=True)
            c = FIRST["d_qkv"]
            for hp in range(4):
                for j in range(9):
                    hi(c + 9 * hp + j)
                attention("D", STEPS["D"] + 8 * hp, 8, 768, pD, None)
            for t in range(KT):
                act.wait_ge(y_lo, PAIRS["D"] + t + 1)
                sc.activation(tile(qh, t), tile(yD, t), ACT.Copy).then_inc(h_hi, 1)
            out_rows(3, view=permuted)
            pre(7)
            ffn(3)

        @block.vector
        def _(dve):
            ch = Chain(dve, dve_self)
            v = nc.vector

            def lo(c, i=None, per=0):
                cc, slot = (c, c % 2) if i is None else (i * per + c, c % 2)
                dve.wait_ge(w_used, cc + 1)
                if isinstance(cc, int) and cc + 2 >= CHUNKS:
                    return
                dve.wait_ge(w_hi, cc + 3)
                v.tensor_tensor(wlo[slot][:, :], wraw[slot][:, :], whi[slot][:, :].bitcast(F32), ALU.subtract).then_inc(w_lo, 1)

            def split_lo(name, src, dsth, dstl):
                for t in range(KT):
                    dve.wait_ge(h_hi, SPLIT[name] + t + 1)
                    v.tensor_tensor(tile(dstl, t), tile(src, t), tile(dsth, t).bitcast(F32), ALU.subtract).then_inc(h_lo, 1)

            def rstd(name):
                n = SQUARES[name] // 8 + 1
                dve.wait_ge(rooted, n)
                ch.link(v.reciprocal(rroots, roots))
                for b in range(4):
                    ins = v.tensor_scalar(std[:, b * P:(b + 1) * P], ident, rroots[:, b:b + 1], float(D), ALU.mult, ALU.mult)
                ins.then_inc(diagonal, 1)
                dve.wait_ge(spread, n)
                return bank(MEAN_BANK(name))

            def post(h):
                rs = rstd(f"post{h}")
                name, l = POST[h]
                for t in range(KT + 1):
                    if t < KT:
                        if t >= 2:
                            dve.wait_ge(x_new, KT * h + t - 1)
                        v.scalar_tensor_tensor(out=tmp[t % 2], in0=tile(mix, t), scalar=col(name, KT * l + t), in1=rs,
                                               op0=ALU.mult, op1=ALU.mult).then_inc(x_tmp, 1)
                    if t:
                        dve.wait_ge(x_tmp, KT * h + t)
                        v.tensor_tensor(tile(x, t - 1), tile(x, t - 1), tmp[(t - 1) % 2], ALU.add).then_inc(x_new, 1)

            def h_split(name, gain, l, rs, dsth, dstl, permute):
                for t in range(KT + 1):
                    if t < KT:
                        if t >= 2 or name == "hq":
                            dve.wait_ge(h_lo, SPLIT[name] + t - 1)
                        a, r, o = tile(x, t), rs, tmp[t % 2]
                        if permute:
                            a, r, o = permuted(a), permuted(r), by4(o)
                        v.scalar_tensor_tensor(out=o, in0=a, scalar=col(gain, KT * l + t), in1=r,
                                               op0=ALU.mult, op1=ALU.mult).then_inc(h_tmp, 1)
                    if t >= 1:
                        dve.wait_ge(h_hi, SPLIT[name] + t)
                        v.tensor_tensor(tile(dstl, t - 1), tmp[(t - 1) % 2], tile(dsth, t - 1).bitcast(F32),
                                        ALU.subtract).then_inc(h_lo, 1)

            def pre(h):
                rs = rstd(f"pre{h}")
                h_split(f"pre{h}", *PRE[h], rs, hh, hl, h == 6)
                if h == 6:
                    h_split("hq", "mix_pre_g_2", 1, rs, qh, ql, True)

            def attention(kind, n0, count, width, pbuf, scores_in, pair_out):
                per = 4 if kind == "D" else 8
                for n in range(count + 4):
                    if n < count:
                        g, q, s = n0 + n, (n0 + n) % 4, (n0 + n) % SLOTS
                        dve.wait_ge(scored, g + 1)
                        m = ch.mark(scores_in(n, s, q))
                        ch.wait(m)
                        v.tensor_scalar(small[:, q:q + 1], small[:, 4 + q:5 + q], {"A": -0.125, "C": -1.0, "D": -SD}[kind],
                                        None, ALU.mult).then_inc(maxed, 1)
                    if 1 <= n < count + 1:
                        g = n0 + n - 1
                        q = g % 4
                        dve.wait_ge(probs, g + 1)
                        ch.link(v.reciprocal(small[:, 12 + q:13 + q], small[:, 8 + q:9 + q]))
                        p = pbuf[:, (g % SLOTS) * width:(g % SLOTS) * width + width]
                        v.tensor_scalar(p, p, small[:, 12 + q:13 + q], None, ALU.mult).then_inc(scaled, 1)
                    if n >= per + 3 and (n - 3) % per == 0:
                        pair_out((n - 3) // per - 1)

            def y_rest(kind, l, t0):
                def rest(hp):
                    dve.wait_ge(y_hi, PAIRS[f"{kind}{l}"] + hp + 1)
                    src, h, dst = bank(4 + hp % 2), tile(yh, t0 + hp).bitcast(F32), tile(yl, t0 + hp)
                    if t0:
                        src, h, dst = backward(src), by4(h), by4(dst)
                    v.tensor_tensor(dst, src, h, ALU.subtract).then_inc(y_lo, 1)
                return rest

            def ffn(f):
                c = FIRST[f"up{f}"]
                m0 = FT * f
                _, _, l, cw, cb = FFN[f]
                taps = [(0, (1, T), (0, T - 1)), (2, (0, T - 1), (1, T))] if f < 2 else \
                       [(1, (1, T), (0, T - 1)), (0, (2, T), (0, T - 2))]
                per = 4
                with dve.Fori(0, FT // 2) as i:
                    start = ch.n
                    ch.shift = i * per
                    for s, acc in enumerate((accv, accg)):
                        lo(c + s, i, 2)
                        first = []
                        for n, (k, (o0, o1), (i0, i1)) in enumerate(taps):
                            for m in range(2):
                                r = i * 2 + (s * FT + m + 2 * FT * (3 * l + k))
                                if n == 0:
                                    dve.wait_ge(affine, i * 4 + (2 * m0 + 2 * s + m + 1))
                                else:
                                    ch.wait(first[m])
                                ins = v.scalar_tensor_tensor(
                                    out=tile(acc, m)[:, o0:o1], in0=bank(2 * s + m)[:, i0:i1], scalar=col(cw, r),
                                    in1=tile(acc, m)[:, o0:o1], op0=ALU.mult, op1=ALU.add)
                                if n == 0:
                                    first.append(ch.mark(ins))
                                else:
                                    ins.then_inc(conv_done, 1)
                    for m in range(2):
                        dve.wait_ge(acted, i * 2 + (m0 + m + 1))
                        v.tensor_tensor(tile(accv, m), tile(accg, m), tile(accv, m), ALU.mult).then_inc(product, 1)
                    for m in range(2):
                        dve.wait_ge(mid_hi, i * 2 + (m0 + m + 1))
                        v.tensor_tensor(tile(midl, i * 2 + m), tile(accv, m), tile(midh, i * 2 + m).bitcast(F32),
                                        ALU.subtract).then_inc(mid_lo, 1)
                    assert ch.n - start == per
                ch.shift = 0
                ch.n += per * (FT // 2 - 1)
                c = FIRST[f"down{f}"]
                for half in range(2):
                    for j in range(6):
                        lo(c + 6 * half + j)
                    for t in range(4):
                        dve.wait_ge(squared, SQUARES[f"post{2 * f + 1}"] + 4 * half + t + 1)
                        ins = v.tensor_copy(tile(mix, 4 * half + t), bank(4 * (1 - half) + t))
                    ins.then_inc(drained, 6)
                post(2 * f + 1)

            def out_rows(f):
                c = FIRST[f"out{f}"]
                for j in range(4):
                    lo(c + j)
                    for m in range(2):
                        t, b = 2 * j + m, bank(2 * (j % 2) + m)
                        dve.wait_ge(squared, SQUARES[f"post{2 * f}"] + t + 1)
                        if f == 2:
                            ins = v.tensor_scalar(tile(mix, t), b, col("cm_b_out_2", t), None, ALU.add)
                        elif f == 3:
                            ins = v.tensor_copy(permuted(tile(mix, t)), by4(b))
                        else:
                            ins = v.tensor_copy(tile(mix, t), b)
                    ins.then_inc(drained, 1)
                post(2 * f)

            v.memset(small[:, 16:17], 0.0).then_inc(drained, 2)
            v.memset(small[:, 17:18], 0.0).then_inc(conv_done, 4)
            v.memset(small[:, 18:19], 0.0).then_inc(mid_lo, 2)
            for c in range(2):
                dve.wait_ge(w_hi, c + 1)
                v.tensor_tensor(wlo[c][:, :], wraw[c][:, :], whi[c][:, :].bitcast(F32), ALU.subtract).then_inc(w_lo, 1)
            for r in range(3):
                n = min(4 * P, ROWS_ALL - 4 * r * P)
                dve.wait_ge(init_turn, r + 1)
                v.tensor_copy(pvec[:, 4 * r * P:4 * r * P + n], bank(r)[:, 0:n]).then_inc(init_out, 1)
            for t in range(KT):
                dve.wait_ge(init_turn, 3 + t + 1)
                v.tensor_copy(tile(x, t), bank(3 + t % 3)).then_inc(init_out, 1)
            pre(0)
            for l in range(2):
                c = FIRST[f"c_qkv{l}"]
                for j in range(6):
                    lo(c + j)
                    src = bank(2 * ((c + j) % 2), 2)
                    if j < 2:
                        ins = v.tensor_scalar(tile(qC, 2 * j, 2).rearrange("p (b q) -> p b q", q=P),
                                              src.rearrange("p (b q) -> p b q", q=P)[:, :, ::-1], 0.125, None, ALU.mult)
                    elif j < 4:
                        ins = v.tensor_copy(tile(kC, 2 * j - 4, 2), src)
                    else:
                        ins = v.tensor_copy(vC[:, :].rearrange("p (b n) -> p b n", b=4)[:, :, CW * (j - 4):CW * (j - 3)],
                                            src.rearrange("p (b n) -> p b n", b=4))
                    ins.then_inc(drained, 1)

                def scores_c(n, s, q, l=l):
                    h, b = steps_of("C")[n]
                    hp = h // 2
                    dve.wait_ge(e2_ready, 4 * l + hp + 1)
                    if n >= SLOTS:
                        dve.wait_ge(turned, STEPS[f"C{l}"] + n - SLOTS + 1)
                    off = (h % 2) * E2C + (6 - 2 * b) * GRID
                    return v.tensor_tensor_reduce(pC[:, s * T:(s + 1) * T], bank(n % 2), e2[hp % 2][:, off:off + T], 1.0,
                                                  2 * NEG, ALU.add, ALU.max, small[:, 4 + q:5 + q])

                attention("C", STEPS[f"C{l}"], 32, T, pC, scores_c, y_rest("C", l, 8))

                def rotate(t):
                    dst = tile(qA, t) if t < 4 else tile(kA, t - 4)
                    n = 5 * l + t
                    dve.wait_ge(head_rot, n + 1)
                    dve.wait_ge(tables, 16 * (5 + 4 * (l + 1)))
                    o = pA[:, (n % 2) * T:(n % 2) * T + T]
                    v.tensor_tensor(o, bank(5 + 2 * (n % 2)), rope[:, T:2 * T], ALU.mult)
                    ch.link(v.tensor_tensor(dst, dst, rope[:, 0:T], ALU.mult))
                    v.tensor_tensor(dst, dst, o, ALU.add).then_inc(qk_ready, 1)

                c = FIRST[f"a_qkv{l}"]
                for j in range(3):
                    lo(c + j)
                    s = (c + j) % 2
                    dve.wait_ge(head_sq, 5 * l + min(2 * j + 2, 5))
                    if j < 2:
                        ins = v.tensor_copy(tile(qA, 2 * j, 2), bank(2 * s, 2))
                    else:
                        v.tensor_copy(tile(kA, 0), bank(2 * s))
                        ins = v.tensor_copy(vA[:, :], bank(4))
                    ins.then_inc(drained, 1)
                    for m in range(2 if j < 2 else 1):
                        t = 2 * j + m
                        n = 5 * l + t
                        dst = tile(qA, t) if t < 4 else tile(kA, t - 4)
                        dve.wait_ge(head_std, n + 1)
                        ch.link(v.reciprocal(std, std))
                        v.scalar_tensor_tensor(out=dst, in0=dst, scalar=col("qkg", l if t < 4 else 2 + l), in1=std,
                                               op0=ALU.mult, op1=ALU.mult).then_inc(head_scaled, 1)
                rotate(0)
                rotate(1)
                c = FIRST[f"pu{l}"]
                lo(c)
                dve.wait_ge(pu_in, 2 * l + 1)
                v.memset(small[:, 16:17], 0.0).then_inc(drained, 1)
                rotate(2)
                rotate(3)
                lo(c + 1)
                dve.wait_ge(pu_in, 2 * l + 2)
                v.memset(small[:, 16:17], 0.0).then_inc(drained, 1)
                rotate(4)
                dve.wait_ge(swapped, l + 1)
                v.tensor_copy(tile(kA, 1), bank(4)).then_inc(qk_ready, 1)

                def scores_a(n, s, q):
                    return v.tensor_reduce(small[:, 4 + q:5 + q], bank(n % 2), AX.X, ALU.max)

                attention("A", STEPS[f"A{l}"], 32, T, pA, scores_a, y_rest("A", l, 0))
                for g in range(4):
                    dve.wait_ge(pool_hi, 4 * l + g + 1)
                    v.scalar_tensor_tensor(out=tile(yl, 4 + g), in0=bank(2 + g), scalar=col("pool_scale", 4 * l + g),
                                           in1=tile(yh, 4 + g).bitcast(F32), op0=ALU.mult, op1=ALU.subtract).then_inc(pool_lo, 1)
                cleared = ch.mark(v.memset(mg[:, :], 0.0))
                c = FIRST[f"merge{l}"]
                d = DRAINS[f"merge{l}"]
                with dve.Fori(0, 3) as n:
                    for g in range(2):
                        for j in range(2):
                            lo(c + 3 * g + j, n, 6)
                            if g or j:
                                pass
                            for m in range(2):
                                ins = v.tensor_scalar(tile(gates, 2 * j + m), bank(4 + 2 * j + m),
                                                      col("b_gate", n * 8 + (24 * l + 4 * g + 2 * j + m)), None, ALU.add)
                            ins.then_inc(drained, 1)
                        lo(c + 3 * g + 2, n, 6)
                        dve.wait_ge(gate_sig, n * 4 + (12 * l + 2 * g + 2))
                        v.tensor_tensor(gates[:, :], gates[:, :], bank(0, 4), ALU.mult).then_inc(drained, 1)
                        dve.wait_ge(drained, n * 6 + (2 + d + 3 * g + 3))
                        ch.wait(cleared)
                        v.tensor_tensor(tile(mg, 4 * g, 4), tile(mg, 4 * g, 4), gates[:, :], ALU.add).then_inc(merged, 1)
                        dve.wait_ge(merged, n * 2 + (6 * l + g + 1))
                split_lo(f"mg{l}", mg, yh, yl)
                out_rows(l)
                pre(2 * l + 1)
                ffn(l)
                pre(2 * l + 2)
            last = [0, 0]

            def add_tapped(j):
                for m in range(2):
                    ch.wait(last[m])
                    dve.wait_ge(tapped, 2 * j + m + 1)
                    v.tensor_tensor(tile(vb, 2 * j + m), tile(vb, 2 * j + m), bank(4 + m), ALU.add).then_inc(convolved, 1)

            c = FIRST["cm_in"]
            v.memset(ub[:, :].rearrange("p (t w) -> p t w", t=KT)[:, :, 0:TAPS - 1], 0.0)
            for j in range(4):
                lo(c + 2 * j)
                for m in range(2):
                    t = 2 * j + m
                    ins = v.tensor_scalar(ub[:, t * UW + TAPS - 1:(t + 1) * UW], bank(2 * (c % 2) + m), col("cm_b_in_2", t), None,
                                          ALU.add)
                ins.then_inc(drained, 1)
                lo(c + 2 * j + 1)
                dve.wait_ge(drained, 2 + DRAINS["cm_in"] + 2 * j + 1)
                for m in range(2):
                    t = 2 * j + m
                    dve.wait_ge(u_sig, t + 1)
                    u = ub[:, t * UW + TAPS - 1:(t + 1) * UW]
                    ins = v.tensor_tensor(u, u, tmp[m], ALU.mult)
                    ins.then_inc(u_ready, 1)
                v.memset(small[:, 16:17], 0.0).then_inc(drained, 1)
                if j:
                    add_tapped(j - 1)
                dve.wait_ge(u_ready, 2 * j + 2)
                last = [0, 0]
                for k in range(TAPS - PE_TAPS):
                    for m in range(2):
                        t = 2 * j + m
                        u = ub[:, t * UW + k:t * UW + k + T]
                        if k == 0:
                            last[m] = ch.mark(v.tensor_scalar(tile(vb, t), u, col("cm_dw_2", 8 * k + t), col("cm_dw_b_2", t),
                                                              ALU.mult, ALU.add))
                            continue
                        ch.wait(last[m])
                        last[m] = ch.mark(v.scalar_tensor_tensor(out=tile(vb, t), in0=u, scalar=col("cm_dw_2", 8 * k + t),
                                                                 in1=tile(vb, t), op0=ALU.mult, op1=ALU.add))
            add_tapped(3)
            dve.wait_ge(summed, NORM["ln_mean"] + 1)
            for t in range(KT):
                v.tensor_tensor(tile(vb, t), tile(vb, t), bank(7), ALU.subtract).then_inc(centred, 1)
            rs = rstd("ln_var")
            for t in range(KT):
                v.tensor_tensor(tile(vb, t), tile(vb, t), rs, ALU.mult).then_inc(ln_scaled, 1)
            split_lo("ln", vb, uh, ul)
            out_rows(2)
            pre(5)
            ffn(2)
            pre(6)
            c = FIRST["d_qkv"]
            for hp in range(4):
                for g in range(3):
                    for j, dst in enumerate((kD, vD, qD)):
                        lo(c)
                        src = bank(2 * (c % 2), 2)
                        if j == 1:
                            ins = v.tensor_copy(vD[:, :].rearrange("p (b g n) -> p b g n", b=4, g=3)[:, :, g, :],
                                                src.rearrange("p (b n) -> p b n", b=4))
                        else:
                            ins = v.tensor_copy(tile(dst, 2 * g, 2), src)
                        ins.then_inc(drained, 1)
                        c += 1
                n0 = STEPS["D"] + 8 * hp

                def scores_d(n, s, q, n0=n0):
                    m, b = steps_of("D")[n]
                    if n >= SLOTS:
                        dve.wait_ge(turned, n0 + n - SLOTS + 1)
                    ch.link(v.tensor_tensor(pD[:, s * 768:s * 768 + T], bank(2 * (n % 2)), dmask[:, (3 - b) * P:(7 - b) * P], ALU.add))
                    ch.link(v.tensor_tensor(pD[:, s * 768 + T:s * 768 + 768], bank(2 * (n % 2) + 1)[:, 0:256], dmask[:, 7 * P:9 * P], ALU.add))
                    return v.tensor_reduce(small[:, 4 + q:5 + q], pD[:, s * 768:s * 768 + 768], AX.X, ALU.max)

                def head_out(m, n0=n0, hp=hp):
                    dve.wait_ge(weighted, n0 + 4 * m + 4)
                    v.tensor_copy(tile(yD, 2 * hp + m), bank(6 + m)).then_inc(y_lo, 1)

                dve.wait_ge(tables, 16 * (5 + 8 + 1))
                attention("D", n0, 8, 768, pD, scores_d, head_out)
            split_lo("y", yD, qh, ql)
            out_rows(3)
            pre(7)
            ffn(3)
            for n in range(8):
                dve.wait_ge(init_turn, 11 + n + 1)
                v.tensor_copy(xrow[:, n * T:(n + 1) * T], bank(n % 4)).then_inc(init_out, 1)

        @block.tensor
        def _(pe):
            te = nc.tensor

            def mm3(out, wh, wl, xh, xl, first, last):
                te.matmul(out, wh, xh, start=first, stop=False)
                te.matmul(out, wh, xl, start=False, stop=False)
                return te.matmul(out, wl, xh, start=False, stop=last)

            def start(c, i=None, per=0, d=None):
                if i is None:
                    pe.wait_ge(w_lo, c + 1)
                    pe.wait_ge(drained, d + 1)
                else:
                    pe.wait_ge(w_lo, i * per + (c + 1))
                    pe.wait_ge(drained, i * per + (d + 1))

            def rows_out(c, bufs, split, bank0=None, tiles=2):
                s = c % 2
                b0 = 2 * s if bank0 is None else bank0
                order = ([(m, k) for m in range(tiles) for k in range(KT)] if split is None else
                         [(m, k) for k in range(KT) for m in range(tiles)])
                for m, k in order:
                    if split is not None and m == 0:
                        pe.wait_ge(h_lo, SPLIT[split] + k + 1)
                    wh, wl = (w[s][:, k * CW + m * P:k * CW + (m + 1) * P] for w in (whi, wlo))
                    ins = mm3(bank(b0 + m), wh, wl, tile(bufs[0], k), tile(bufs[1], k), k == 0, k == KT - 1)
                return ins

            def tokens_out(c, bufs, c0, n, at):
                s = c % 2
                for b in range(4):
                    o = ps[:, at * T + b * n:at * T + (b + 1) * n]
                    for k in range(KT):
                        xs = [u[:, k * T + b * P:k * T + (b + 1) * P] for u in bufs]
                        wh, wl = (w[s][:, k * CW + c0:k * CW + c0 + n] for w in (whi, wlo))
                        te.matmul(o, xs[0], wh, start=k == 0, stop=False)
                        te.matmul(o, xs[0], wl, start=False, stop=False)
                        ins = te.matmul(o, xs[1], wh, start=False, stop=k == KT - 1)
                return ins

            def keep_warm(n=1):
                for _ in range(n):
                    te.matmul(bank(5), meanm, base[:, 0:T], start=True, stop=True)

            def norm(name, wait=None):
                n, b0 = SQUARES[name] // 8, MEAN_BANK(name)
                pe.wait_ge(sq_added, n + 1)
                for b in range(4):
                    ins = te.matmul(bank(b0)[:, b:b + 1], sq[:, b * P:(b + 1) * P], meanm[:, 0:1], start=b == 0, stop=b == 3)
                ins.then_inc(summed, 1)
                keep_warm(1)
                pe.wait_ge(diagonal, n + 1)
                te.matmul(bank(b0), meanm, std, start=True, stop=True).then_inc(spread, 1)

            def out_product(f, bufs, split):
                c, d = FIRST[f"out{f}"], DRAINS[f"out{f}"]
                for j in range(4):
                    start(c + j, d=d + j)
                    rows_out(c + j, bufs, split if j == 0 else None, bank0=2 * (j % 2)).then_inc(w_used, 1)
                for t in range(6, KT):
                    pe.wait_ge(squared, SQUARES[f"post{2 * f}"] + t + 1)
                    keep_warm()
                norm(f"post{2 * f}")

            def pre(h):
                for t in range(KT):
                    if h:
                        pe.wait_ge(squared, SQUARES[f"pre{h}"] + t + 1)
                        keep_warm()
                norm(f"pre{h}")

            def ffn(f):
                c, m0 = FIRST[f"up{f}"], FT * f
                pe.wait_ge(drained, 2 + DRAINS[f"up{f}"])
                with pe.Fori(0, FT // 2) as i:
                    for s in range(2):
                        pe.wait_ge(w_lo, i * 2 + (c + s + 1))
                        pe.wait_ge(conv_done, i * 4 + (2 * m0 + 2 * s + 2))
                        rows_out(c + s, (hh, hl), None if s else f"pre{2 * f + 1}", bank0=2 * s).then_inc(w_used, 1)
                pe.wait_ge(conv_done, 4 + 2 * m0 + 2 * FT)
                c = FIRST[f"down{f}"]
                for half in range(2):
                    for j in range(6):
                        cc = c + 6 * half + j
                        pe.wait_ge(w_lo, cc + 1)
                        for k in range(min(4, FT - 4 * j)):
                            n = 4 * j + k
                            if half == 0:
                                pe.wait_ge(mid_lo, 2 + m0 + n + 1)
                            for t in range(4):
                                at = k * 512 + t * P
                                ins = mm3(bank(4 * (1 - half) + t), whi[cc % 2][:, at:at + P], wlo[cc % 2][:, at:at + P],
                                          tile(midh, n), tile(midl, n), n == 0, n == FT - 1)
                        ins.then_inc(w_used, 1)
                        if half == 1 and j == 1:
                            pe.wait_ge(drained, 2 + DRAINS[f"down{f}"] + 6)
                for t in range(4, KT):
                    pe.wait_ge(squared, SQUARES[f"post{2 * f + 1}"] + t + 1)
                    keep_warm()
                norm(f"post{2 * f + 1}")

            def attention(kind, n0, count, scores, pbuf, weigh):
                blocks, width = (6, 768) if kind == "D" else (4, T)
                scores(0, n0)
                scores(1, n0 + 1)
                for n in range(count + 1):
                    if n < count:
                        g = n0 + n
                        pe.wait_ge(probs if kind == "A" else maxed, g + 1)
                        if n + 2 < count:
                            scores(n + 2, g + 2)
                        pe.wait_ge(scaled, g + 1)
                        back = 1 if kind == "D" else 2
                        if n >= back:
                            pe.wait_ge(pt_ready, g - back + 1)
                        o = bank(4, 2) if kind == "D" else bank(2 + g % 2)
                        for j in range(blocks):
                            at = (g % SLOTS) * width + j * P
                            ins = te.transpose(o[:, j * P:(j + 1) * P], pbuf[:, at:at + P], ident)
                        ins.then_inc(turned, 1)
                    if n:
                        pe.wait_ge(pt_ready, n0 + n)
                        weigh(n - 1, n0 + n - 1)

            def weigh_pair(kind, l, vbuf):
                def weigh(n, g):
                    h, b = steps_of(kind)[n]
                    hp, r = h // 2, 64 * (h % 2)
                    if n % 8 == 0 and hp >= 2:
                        pe.wait_ge(y_lo, PAIRS[f"{kind}{l}"] + hp - 1)
                    for k in range(4):
                        at = k * 512 + h * 64 if kind == "C" else k * P + 64 * (h // 4)
                        ins = te.matmul(bank(4 + hp % 2)[r:r + 64, b * P:(b + 1) * P], vbuf[:, at:at + 64],
                                        scratch[:, (g % 2) * T + k * P:(g % 2) * T + (k + 1) * P], start=k == 0, stop=k == 3)
                    ins.then_inc(weighted, 1)
                return weigh

            pe.wait_ge(init_in, 16 * len(param_loads))
            pe.wait_ge(tables, 16 * 5)
            for r in range(3):
                for j in range(min(4, ROW_TILES - 4 * r)):
                    n = 4 * r + j
                    k = min(P, ROWS_ALL - n * P)
                    ins = te.transpose(bank(r)[:, j * P:j * P + k], prow[0:k, n * P:(n + 1) * P], ident[0:k, 0:k])
                ins.then_inc(init_turn, 1)
            for t in range(KT):
                if t >= 3:
                    pe.wait_ge(init_out, 3 + t - 3 + 1)
                for b in range(4):
                    ins = te.transpose(bank(3 + t % 3)[:, b * P:(b + 1) * P], xrow[:, b * D + t * P:b * D + (t + 1) * P], ident)
                ins.then_inc(init_turn, 1)
            pre(0)
            for l in range(2):
                c, d = FIRST[f"c_qkv{l}"], DRAINS[f"c_qkv{l}"]
                for j in range(6):
                    start(c + j, d=d + j)
                    if j == 0:
                        pe.wait_ge(drained, 2 + d)
                    if j < 4:
                        rows_out(c + j, (hh, hl), f"pre{2 * l}" if j == 0 else None).then_inc(w_used, 1)
                    else:
                        tokens_out(c + j, (hh, hl), 0, CW, 2 * ((c + j) % 2)).then_inc(w_used, 1)
                pe.wait_ge(drained, 2 + d + 6)

                def scores_c(n, g):
                    h, b = steps_of("C")[n]
                    r, t = 64 * (h % 2), h // 2
                    te.matmul(bank(g % 2), qC[r:r + 64, t * T + b * P:t * T + (b + 1) * P], kC[r:r + 64, t * T:(t + 1) * T],
                              start=True, stop=True).then_inc(scored, 1)

                attention("C", STEPS[f"C{l}"], 32, scores_c, pC, weigh_pair("C", l, vC))

                def head_mean(t, l=l):
                    n = 5 * l + t
                    pe.wait_ge(head_sq, n + 1)
                    if t:
                        pe.wait_ge(head_std, n)
                    te.matmul(bank(6), headm, tmp[n % 2], start=True, stop=True).then_inc(head_sum, 1)

                def rotate(t, l=l):
                    n = 5 * l + t
                    pe.wait_ge(head_scaled, n + 1)
                    if t >= 2:
                        pe.wait_ge(qk_ready, 6 * l + t - 1)
                    te.matmul(bank(5 + 2 * (n % 2)), rotm, tile(qA, t) if t < 4 else tile(kA, t - 4), start=True,
                              stop=True).then_inc(head_rot, 1)

                pe.wait_ge(y_lo, PAIRS[f"C{l}"] + 4)
                c, d = FIRST[f"a_qkv{l}"], DRAINS[f"a_qkv{l}"]
                for j in range(3):
                    start(c + j, d=d + j)
                    if j < 2:
                        rows_out(c + j, (hh, hl), None).then_inc(w_used, 1)
                    else:
                        rows_out(c + j, (hh, hl), None, tiles=1)
                        tokens_out(c + j, (hh, hl), P, P, 4).then_inc(w_used, 1)
                    if j == 1:
                        head_mean(0)
                        head_mean(1)
                for t in range(2, 5):
                    head_mean(t)
                rotate(0)
                rotate(1)
                c, d = FIRST[f"pu{l}"], DRAINS[f"pu{l}"]
                start(c, d=d)
                rows_out(c, (hh, hl), None).then_inc(w_used, 1)
                rotate(2)
                rotate(3)
                start(c + 1, d=d + 1)
                rows_out(c + 1, (hh, hl), None).then_inc(w_used, 1)
                rotate(4)
                pe.wait_ge(qk_ready, 6 * l + 5)
                te.matmul(bank(4), swapm, tile(kA, 0), start=True, stop=True).then_inc(swapped, 1)
                pe.wait_ge(qk_ready, 6 * l + 6)
                pe.wait_ge(drained, 2 + d + 2)

                def scores_a(n, g):
                    h, b = steps_of("A")[n]
                    r, t, kv = 64 * (h % 2), h // 2, int(h % 2 != h // 4)
                    te.matmul(bank(g % 2), qA[r:r + 64, t * T + b * P:t * T + (b + 1) * P], kA[r:r + 64, kv * T:(kv + 1) * T],
                              start=True, stop=True).then_inc(scored, 1)

                attention("A", STEPS[f"A{l}"], 32, scores_a, pA, weigh_pair("A", l, vA))
                pe.wait_ge(y_lo, PAIRS[f"A{l}"] + 4)
                W = T + 2 * PAD
                for g in range(4):
                    pe.wait_ge(pooled, 4 * l + g + 1)
                    te.matmul(bank(2 + g), pw[:, g * P:(g + 1) * P], pu[:, g * W + PAD:g * W + PAD + T], start=True,
                              stop=True).then_inc(pool_out, 1)
                pe.wait_ge(pool_lo, 4 * l + 4)
                c, d = FIRST[f"merge{l}"], DRAINS[f"merge{l}"]
                with pe.Fori(0, 3) as n:
                    for g in range(2):
                        for j in range(2):
                            start(c + 3 * g + j, n, 6, d + 3 * g + j)
                            rows_out(c + 3 * g + j, (hh, hl), None, bank0=4 + 2 * j).then_inc(w_used, 1)
                        cc = c + 3 * g + 2
                        start(cc, n, 6, d + 3 * g + 2)
                        for t in range(4):
                            for k in range(4):
                                at = k * 512 + t * P
                                ins = mm3(bank(t), whi[cc % 2][:, at:at + P], wlo[cc % 2][:, at:at + P],
                                          tile(yh, n * 4 + k), tile(yl, n * 4 + k), k == 0, k == 3)
                        ins.then_inc(w_used, 1)
                out_product(l, (yh, yl), f"mg{l}")
                pre(2 * l + 1)
                ffn(l)
                pre(2 * l + 2)
            c, d = FIRST["cm_in"], DRAINS["cm_in"]
            def taps(j):
                for m in range(2):
                    t = 2 * j + m
                    pe.wait_ge(taps_in, t + 1)
                    pe.wait_ge(u_ready, t + 1)
                    if j:
                        pe.wait_ge(convolved, t - 1)
                    for i in range(PE_TAPS):
                        at, u0 = ((t % 4) * PE_TAPS + i) * P, t * UW + TAPS - PE_TAPS + i
                        ins = te.matmul(bank(4 + m), tapd[:, at:at + P], ub[:, u0:u0 + T], start=i == 0, stop=i == PE_TAPS - 1)
                    ins.then_inc(tapped, 1)

            def ln_mean(j):
                for t in (2 * j, 2 * j + 1):
                    pe.wait_ge(convolved, t + 1)
                    ins = te.matmul(bank(7), meanm, tile(vb, t), start=t == 0, stop=t == KT - 1)
                if j == 3:
                    ins.then_inc(summed, 1)

            for j in range(4):
                for i in range(2):
                    start(c + 2 * j + i, d=d + 2 * j + i)
                    if j == i == 0:
                        pe.wait_ge(drained, 2 + d)
                    rows_out(c + 2 * j + i, (hh, hl), "pre4" if j == i == 0 else None).then_inc(w_used, 1)
                if j:
                    taps(j - 1)
                if j > 1:
                    ln_mean(j - 2)
            taps(3)
            ln_mean(2)
            ln_mean(3)
            for t in range(KT):
                pe.wait_ge(squared, SQUARES["ln_var"] + t + 1)
                keep_warm()
            norm("ln_var")
            pe.wait_ge(drained, 2 + d + 8)
            out_product(2, (uh, ul), "ln")
            pre(5)
            ffn(2)
            pre(6)
            c, d = FIRST["d_qkv"], DRAINS["d_qkv"]
            for hp in range(4):
                for g in range(3):
                    for j in range(3):
                        start(c, d=d)
                        if hp == g == j == 0:
                            pe.wait_ge(drained, 2 + d)
                        if j == 1:
                            tokens_out(c, (hh, hl), 0, CW, 2 * (c % 2)).then_inc(w_used, 1)
                        else:
                            bufs, split = ((hh, hl), "pre6") if j == 0 else ((qh, ql), "hq")
                            rows_out(c, bufs, split if hp == g == 0 else None).then_inc(w_used, 1)
                        c, d = c + 1, d + 1
                pe.wait_ge(drained, 2 + d)

                def scores_d(n, g, hp=hp):
                    m, b = steps_of("D")[n]

                    def at(buf, i):
                        return buf[:, (2 * i + m) * T + b * P:(2 * i + m) * T + (b + 1) * P]
                    te.matmul(bank(2 * (g % 2)), at(qD, 0), kD[:, m * T:(m + 1) * T], start=True, stop=True)
                    te.matmul(bank(2 * (g % 2) + 1)[:, 0:P], at(qD, 1), at(kD, 1), start=True, stop=True)
                    te.matmul(bank(2 * (g % 2) + 1)[:, P:2 * P], at(qD, 2), at(kD, 2), start=True, stop=True).then_inc(scored, 1)

                def weigh_d(n, g, hp=hp):
                    m, b = steps_of("D")[n]
                    if hp and b == 0:
                        pe.wait_ge(y_lo, PAIRS["D"] + 2 * hp - 1 + m)
                    keys = [(k, 0) for k in range(4)] + [(b, 1), (b, 2)]
                    for j, (k, i) in enumerate(keys):
                        at = k * 768 + i * CW + m * P
                        ins = te.matmul(bank(6 + m)[:, b * P:(b + 1) * P], vD[:, at:at + P],
                                        scratch[:, (g % 2) * 768 + j * P:(g % 2) * 768 + (j + 1) * P], start=j == 0, stop=j == 5)
                    ins.then_inc(weighted, 1)

                attention("D", STEPS["D"] + 8 * hp, 8, scores_d, pD, weigh_d)
            out_product(3, (qh, ql), "y")
            pre(7)
            ffn(3)
            pe.wait_ge(x_new, 8 * KT)
            for n in range(8):
                b, half = n // 2, n % 2
                if n >= 4:
                    pe.wait_ge(init_out, 11 + n - 3)
                for j in range(4):
                    t = 4 * half + j
                    ins = te.transpose(bank(n % 4)[:, j * P:(j + 1) * P], x[:, t * T + b * P:t * T + (b + 1) * P], ident)
                ins.then_inc(init_turn, 1)


def kernel(**inputs):
    import numpy as _np
    import concourse.bacc as _bacc
    from concourse import mybir as _mybir
    from concourse.bass_utils import run_bass_kernel_spmd as _run

    nc = _bacc.Bacc("TRN2", target_bir_lowering=False, num_devices=1)
    arrays = {n: _np.ascontiguousarray(a) for n, a in inputs.items() if n != "rpb"}
    arrays["rpbp"] = _np.pad(_np.ascontiguousarray(inputs["rpb"]).reshape(1, -1), ((0, 0), (RPB_PAD, RPB_PAD)))
    arrays.update(host_constants())
    maps, aps = {}, {}
    for n, a in arrays.items():
        maps[f"in_{n}_dram"] = a
        aps[n] = nc.dram_tensor(f"in_{n}_dram", a.shape, _mybir.dt.from_np(a.dtype), kind="ExternalInput").ap()
    out = nc.dram_tensor("out_0_dram", (1, T, D), F32, kind="ExternalOutput").ap()
    build(nc, aps, out)
    r = _run(nc, [maps], core_ids=[0])
    return r.results[0]["out_0_dram"]
```

```python
from contextlib import ExitStack

import numpy as np

import concourse.bass as bass
from concourse import mybir

F32 = mybir.dt.float32
F32R = mybir.dt.float32r
ALU = mybir.AluOpType
ACT = mybir.ActivationFunctionType
AX = mybir.AxisListType

P = 128
T = 512
D = 1024
KT = D // P
D_IN = 5888
FF = 2816
FT = FF // P
EPS = 1e-6
NEG = -1e30
CH = 2048
CW = CH // KT
POOL_WINDOWS = (2, 4, 8, 16)
PAD = 8
TAPS = 31
PE_TAPS = 10
GRID = 64
NA_COLS = 16
RPB_PAD = 64
E2C = 14 * GRID
SD = 128 ** -0.5

QA, KA, VA, PU, QC, KC, VC, GL = 0, 512, 640, 768, 1280, 1792, 2304, 2816

PLAN = []
for _l in range(2):
    PLAN += [(f"c_qkv{_l}", 6), (f"a_qkv{_l}", 3), (f"pu{_l}", 2), (f"merge{_l}", 18), (f"out{_l}", 4),
             (f"up{_l}", FT), (f"down{_l}", 12)]
PLAN += [("cm_in", 8), ("out2", 4), (f"up2", FT), ("down2", 12), ("d_qkv", 36), ("out3", 4), ("up3", FT), ("down3", 12)]
FIRST, DRAINS = {}, {}
_c = _d = 0
for _name, _n in PLAN:
    FIRST[_name], DRAINS[_name] = _c, _d
    _c += _n
    _d += 0 if _name.startswith("up") else _n
CHUNKS = _c

ROWS = {}
_r = 0
for _name, _n in [("norm_mix_pre", 16), ("norm_mix_post", 16), ("norm_ffn_pre", 16), ("norm_ffn_post", 16),
                  ("b_gate", 48), ("pool_scale", 8), ("qkg", 4), ("conv_w", 264), ("conv_b", 88),
                  ("mix_pre_g_2", 16), ("mix_post_g_2", 16), ("ffn_pre_g_2", 16), ("ffn_post_g_2", 16),
                  ("cm_b_in_2", 16), ("cm_dw_2", 248), ("cm_dw_b_2", 8), ("cm_ln_g_2", 8), ("cm_ln_b_2", 8),
                  ("cm_b_out_2", 8), ("kv_norm_g_2", 8), ("ffn_dw_2", 264), ("ffn_dw_b_2", 88)]:
    ROWS[_name] = (_r, _n)
    _r += _n
ROWS_ALL = _r
ROW_TILES = -(-ROWS_ALL // P)

STEPS = {"C0": 0, "A0": 32, "C1": 64, "A1": 96, "D": 128}
POOL_STEPS = (16, 20, 24, 28)
SLOTS = 3
PAIRS = {"C0": 0, "A0": 4, "C1": 8, "A1": 12, "D": 16}
NORMS = ["pre0"]
for _h in range(8):
    if _h == 4:
        NORMS += ["ln_mean", "ln_var"]
    NORMS += [f"post{_h}"] + ([f"pre{_h + 1}"] if _h < 7 else [])
NORM = {n: i for i, n in enumerate(NORMS)}
SQUARES = {n: 8 * i for i, n in enumerate(n for n in NORMS if n != "ln_mean")}
SPLITS = ["pre0", "mg0", "pre1", "pre2", "mg1", "pre3", "pre4", "ln", "pre5", "pre6", "hq", "y", "pre7"]
SPLIT = {n: 8 * i for i, n in enumerate(SPLITS)}
SCALED = {n: 8 * i for i, n in enumerate(n for n in SPLITS if n[0] in "ph")}


def host_constants():
    ident = np.eye(P, dtype=np.float32)
    head = np.kron(np.eye(2), np.full((64, 64), 1 / 64)).astype(np.float32)
    mean = np.full((P, P), 1 / D, np.float32)
    rot = np.zeros((P, P), np.float32)
    for m in range(P):
        rot[m + 16 if m % 32 < 16 else m - 16, m] = -1.0 if m % 32 < 16 else 1.0
    t = np.arange(T)
    freqs = np.float32(10000.0) ** (-np.arange(0, 32, 2, dtype=np.float32) / np.float32(32))
    p = np.arange(P)
    pos = np.where((p % 64 < 32)[:, None], (t // GRID)[None], (t % GRID)[None]).astype(np.float32)
    ang = pos * freqs[p % 16][:, None].astype(np.float32)
    cos, sin = np.cos(ang).astype(np.float32), np.sin(ang).astype(np.float32)
    col = np.arange(GRID)
    start = np.clip(col - NA_COLS // 2, 0, GRID - NA_COLS)
    inside = (col[None] >= start[:, None]) & (col[None] < start[:, None] + NA_COLS)
    cmask = np.tile(np.where(inside, 0, NEG).astype(np.float32)[::-1], (2, 1))
    edge = np.ones((len(POOL_WINDOWS), 2 * PAD), np.float32)
    for g, w in enumerate(POOL_WINDOWS):
        count = np.clip(t + w - w // 2, 0, T) - np.clip(t - w // 2, 0, T)
        edge[g] = np.float32(w) / np.concatenate([count[:PAD], count[-PAD:]]).astype(np.float32)
    edge = np.tile(edge.reshape(1, -1), (P, 1))
    l, m = np.arange(P)[:, None], np.arange(P)[None]
    band = [np.where((4 * (l - m) + d >= 0) & (4 * (l - m) + d <= 128), 0, NEG) for d in range(3, -4, -1)]
    causal = np.where(l >= m, 0, NEG)
    strided = np.where((l >= m) & ((l - m) % 4 == 0), 0, NEG)
    dmask = np.concatenate(band + [causal, strided], axis=1).astype(np.float32)
    return {"c_base": np.concatenate([ident, head, mean, rot, np.roll(ident, 64, axis=1)], axis=1), "c_rope": np.concatenate([cos, sin], axis=1),
            "c_cmask": cmask, "c_edge": edge, "c_dmask": dmask}


class Chain:

    def __init__(self, eng, sem):
        self.eng, self.sem, self.n, self.shift = eng, sem, 0, 0

    def mark(self, ins):
        ins.then_inc(self.sem, 1)
        self.n += 1
        return self.n

    def wait(self, value):
        self.eng.wait_ge(self.sem, value + self.shift)

    def link(self, ins):
        self.wait(self.mark(ins))


def build(nc, A, out):
    with ExitStack() as ctx:
        def sb(name, cols, dt=F32, stack=ctx):
            return stack.enter_context(nc.sbuf_tensor("t_" + name, [P, cols], dt))

        def sem(name):
            return ctx.enter_context(nc.semaphore(name))

        wraw = [sb(f"wraw{s}", CH) for s in range(2)]
        whi = [sb(f"whi{s}", CH, F32R) for s in range(2)]
        wlo = [sb(f"wlo{s}", CH, F32R) for s in range(2)]
        x = sb("x", KT * T)
        base = sb("base", 5 * P)
        pvec = sb("pvec", ROW_TILES * P)
        scratch = sb("scratch", 3 * T)
        small = sb("small", 32)
        ident, headm, meanm, rotm, swapm = (base[:, i * P:(i + 1) * P] for i in range(5))
        tmp = [scratch[:, 0:T], scratch[:, T:2 * T]]
        std = scratch[:, 2 * T:3 * T]
        trio = [tmp[0], tmp[1], std]
        roots, rroots = small[:, 20:24], small[:, 24:28]
        epsc = small[:, 31:32]
        with ExitStack() as s:
            hh, hl = sb("hh", KT * T, F32R, s), sb("hl", KT * T, F32R, s)
        hbufs = ctx.enter_context(ExitStack())
        mix, sq = sb("mix", KT * T, stack=hbufs), sb("sq", KT * T, stack=hbufs)

        with ExitStack() as s:
            prow, xrow = sb("prow", ROW_TILES * P, stack=s), sb("xrow", 4 * D, stack=s)
        with ExitStack() as s:
            yh, yl = sb("yh", 12 * T, F32R, s), sb("yl", 12 * T, F32R, s)
            with ExitStack() as u:
                qC, kC, vC = sb("qC", 4 * T, stack=u), sb("kC", 4 * T, stack=u), sb("vC", 4 * T, stack=u)
                e2 = [sb(f"e2{i}", 2 * E2C, stack=u) for i in range(2)]
                pC = sb("pC", SLOTS * T, stack=u)
                cmask = sb("cmask", GRID, stack=u)
            with ExitStack() as u:
                qA, kA, vA = sb("qA", 4 * T, stack=u), sb("kA", 2 * T, stack=u), sb("vA", T, stack=u)
                rope = sb("rope", 2 * T, stack=u)
                pA = sb("pA", SLOTS * T, stack=u)
                pw = sb("pw", 4 * P, stack=u)
                pu = sb("pu", 4 * (T + 2 * PAD), stack=u)
                win = [sb(f"win{i}", T + 2 * PAD, stack=u) for i in range(2)]
                edge = sb("edge", len(POOL_WINDOWS) * 2 * PAD, stack=u)
            with ExitStack() as u:
                gates, mg = sb("gates", 4 * T, stack=u), sb("mg", KT * T, stack=u)
        with ExitStack() as s:
            midh, midl = sb("midh", FT * T, F32R, s), sb("midl", FT * T, F32R, s)
            accv, accg = sb("accv", 2 * T, stack=s), sb("accg", 2 * T, stack=s)
        with ExitStack() as s:
            uh, ul = sb("uh", KT * T, F32R, s), sb("ul", KT * T, F32R, s)
            UW = T + TAPS - 1
            ub, vb = sb("ub", KT * UW, stack=s), sb("vb", KT * T, stack=s)
            tapd = sb("tapd", 4 * PE_TAPS * P, stack=s)
        with ExitStack() as s:
            qh, ql = sb("qh", KT * T, F32R, s), sb("ql", KT * T, F32R, s)
            yD = sb("yD", KT * T, stack=s)
            qD, kD, vD = (sb(n, 6 * T, stack=s) for n in ("qD", "kD", "vD"))
            pD = sb("pD", SLOTS * 768, stack=s)
            dmask = sb("dmask", 9 * P, stack=s)

        ps = ctx.enter_context(nc.psum_tensor("ps", [P, 8 * T], F32))

        def bank(b, n=1):
            return ps[:, b * T:(b + n) * T]

        w_loaded = [sem("w_loaded0"), sem("w_loaded1")]
        w_hi, w_lo, w_used = sem("w_hi"), sem("w_lo"), sem("w_used")
        drained = sem("drained")
        tile_done = sem("tile_done")
        conv_done = sem("conv_done")
        mid_lo = sem("mid_lo")
        affine, acted, product, mid_hi = sem("affine"), sem("acted"), sem("product"), sem("mid_hi")
        init_in = [sem("init_in0"), sem("init_in1")]
        init_turn, init_out, out_copied = sem("init_turn"), sem("init_out"), sem("out_copied")
        stored = sem("stored")
        squared, summed, rooted, x_tmp, x_new = (sem(n) for n in ("squared", "summed", "rooted", "x_tmp", "x_new"))
        diagonal, spread, sq_added = sem("diagonal"), sem("spread"), sem("sq_added")
        h_tmp, h_hi, h_lo = sem("h_tmp"), sem("h_hi"), sem("h_lo")
        gate_sig, head_sq, head_sum, head_std, head_scaled, head_rot = (
            sem(n) for n in ("gate_sig", "head_sq", "head_sum", "head_std", "head_scaled", "head_rot"))
        qk_ready, swapped = sem("qk_ready"), sem("swapped")
        scored, maxed, probs, scaled, turned, pt_ready, weighted, y_hi, y_lo = (
            sem(n) for n in ("scored", "maxed", "probs", "scaled", "turned", "pt_ready", "weighted", "y_hi", "y_lo"))
        e2_loaded = [sem("e2_loaded0"), sem("e2_loaded1")]
        e2_ready, tables = sem("e2_ready"), sem("tables")
        pu_in, pooled, pool_out = sem("pu_in"), sem("pooled"), sem("pool_out")
        u_ready, taps_in, tapped, u_sig, convolved, centred, ln_scaled = sem("u_ready"), sem("taps_in"), sem("tapped"), sem("u_sig"), sem("convolved"), sem("centred"), sem("ln_scaled")
        pool_hi, pool_lo, merged = sem("pool_hi"), sem("pool_lo"), sem("merged")
        dve_self, act_self, pool_self = sem("dve_self"), sem("act_self"), sem("pool_self")

        def col(name, i=0):
            if isinstance(i, int):
                return pvec[:, ROWS[name][0] + i:ROWS[name][0] + i + 1]
            return pvec[:, bass.ds(i + ROWS[name][0], 1)]

        def tile(buf, t, n=1):
            if isinstance(t, int):
                return buf[:, t * T:(t + n) * T]
            return buf[:, bass.ds(t * T, n * T)]

        def MEAN_BANK(name):
            return 7 if name[:4] == "post" else 6

        def permuted(ap):
            return ap.rearrange("p (l b) -> p b l", b=4)

        def by4(ap):
            return ap.rearrange("p (b l) -> p b l", b=4)

        def out_bank(f, j):
            return 4 if f < 2 and j == 0 else 2 * (j % 2)

        def backward(ap):
            return by4(ap)[:, :, ::-1]

        D_ORDER = [(kD, vD, qD), (kD, vD, qD), (kD, qD, vD)]
        FFN = [("w_up", "w_down", 0, "conv_w", "conv_b"), ("w_up", "w_down", 1, "conv_w", "conv_b"),
               ("ffn_w_in_2", "ffn_w_out_2", 0, "ffn_dw_2", "ffn_dw_b_2"),
               ("ffn_w_in_2", "ffn_w_out_2", 1, "ffn_dw_2", "ffn_dw_b_2")]
        POST = [("norm_mix_post", 0), ("norm_ffn_post", 0), ("norm_mix_post", 1), ("norm_ffn_post", 1),
                ("mix_post_g_2", 0), ("ffn_post_g_2", 0), ("mix_post_g_2", 1), ("ffn_post_g_2", 1)]
        PRE = [("norm_mix_pre", 0), ("norm_ffn_pre", 0), ("norm_mix_pre", 1), ("norm_ffn_pre", 1),
               ("mix_pre_g_2", 0), ("ffn_pre_g_2", 0), ("kv_norm_g_2", 0), ("ffn_pre_g_2", 1)]

        param_loads = []
        for name, (r0, n) in ROWS.items():
            if name == "qkg":
                for i, a in enumerate((A["qk_norm_q"], A["qk_norm_k"])):
                    for l in range(2):
                        for half in range(2):
                            r, c0 = r0 + 2 * i + l, 64 * half
                            at0 = (r // P) * P + c0
                            param_loads.append((prow[r % P:r % P + 1, at0:at0 + 64], a[l:l + 1, :]))
                continue
            flat = A[name]
            if len(flat.shape) == 3:
                flat = flat.rearrange("a b c -> (a b) c")
            flat = (flat.rearrange("a (n p) -> (a n) p", p=P) if len(flat.shape) == 2 else
                    flat.rearrange("(n p) -> n p", p=P))
            done = 0
            while done < n:
                r = r0 + done
                k = min(n - done, P - r % P)
                param_loads.append((prow[r % P:r % P + k, (r // P) * P:(r // P + 1) * P], flat[done:done + k, :]))
                done += k

        def steps_of(kind):
            if kind[0] == "D":
                return [(m, b) for m in range(2) for b in range(4)]
            return [(2 * hp + s, b) for hp in range(4) for s in range(2) for b in range(4)]

        block = ctx.enter_context(nc.Block())

        def half_layer_tail(sp, load, at, rows, f, w_out):
            c = FIRST[f"out{f}"]
            for j in range(4):
                load(at(c + j), w_out[:, :, CW * j:CW * (j + 1)])
            up, down, l = FFN[f][:3]
            w = rows(A[up], l)
            c = FIRST[f"up{f}"]
            with sp.Fori(0, FT // 2) as i:
                for s in range(2):
                    load(at(c + s, i, 2), w[:, :, bass.ds(i * CW + FF * s, CW)])
            w = rows(A[down], l)
            c = FIRST[f"down{f}"]
            for half in range(2):
                for j in range(6):
                    k = min(4, FT - 4 * j)
                    load(at(c + 6 * half + j), w[:, 4 * j:4 * j + k, 512 * half:512 * half + 512], k * 512)

        @block.sync
        def _(sp):
            def load(c, src, cols=CH):
                c, slot, turn = c
                if not isinstance(c, int) or c >= 2:
                    sp.wait_ge(w_lo, c - 1)
                sp.dma_start(wraw[slot][:, 0:cols].rearrange("p (k n) -> p k n", n=src.shape[-1]),
                             src).then_inc(w_loaded[slot], 16)

            def at(c, i=None, per=0):
                if i is None:
                    return c, c % 2, c // 2
                return i * per + c, c % 2, i * (per // 2) + c // 2

            def rows(w, l):
                return w[l].rearrange("(k p) n -> p k n", p=P)

            for dst, src in param_loads[0::2]:
                sp.dma_start(dst, src).then_inc(init_in[0], 16)

            for l in range(2):
                w = rows(A["w_in"], l)
                c = FIRST[f"c_qkv{l}"]
                for j, n0 in enumerate([QC, QC + CW, KC, KC + CW, VC, VC + CW]):
                    load(at(c + j), w[:, :, n0:n0 + CW])
                c = FIRST[f"a_qkv{l}"]
                for j in range(2):
                    load(at(c + j), w[:, :, QA + CW * j:QA + CW * (j + 1)])
                load(at(c + 2), w[:, :, KA:KA + CW])
                c = FIRST[f"pu{l}"]
                for j in range(2):
                    load(at(c + j), w[:, :, PU + CW * j:PU + CW * (j + 1)])
                c = FIRST[f"merge{l}"]
                wb = A["w_branch"][l].rearrange("b (k p) n -> p (b k) n", p=P)
                with sp.Fori(0, 3) as n:
                    for g in range(2):
                        for j in range(2):
                            load(at(c + 3 * g + j, n, 6), w[:, :, bass.ds(n * D + (GL + 512 * g + CW * j), CW)])
                        load(at(c + 3 * g + 2, n, 6), wb[:, bass.ds(n * 4, 4), 512 * g:512 * g + 512])
                half_layer_tail(sp, load, at, rows, l, rows(A["w_out"], l))
            c = FIRST["cm_in"]
            w = rows(A["cm_w_in_2"], 0)
            for j in range(4):
                load(at(c + 2 * j), w[:, :, CW * j:CW * (j + 1)])
                load(at(c + 2 * j + 1), w[:, :, D + CW * j:D + CW * (j + 1)])
            half_layer_tail(sp, load, at, rows, 2, rows(A["cm_w_out_2"], 0))
            c = FIRST["d_qkv"]
            wkv = A["w_kv_2"].rearrange("(k p) n -> p k n", p=P)
            wq = rows(A["w_q_2"], 0)
            for hp in range(4):
                for g in range(3):
                    n0 = D * g + CW * hp
                    for dst in D_ORDER[g]:
                        w, w0 = (wq, 0) if dst is qD else (wkv, 3 * D if dst is vD else 0)
                        load(at(c), w[:, :, w0 + n0:w0 + n0 + CW])
                        c += 1
            half_layer_tail(sp, load, at, rows, 3, rows(A["w_o_2"], 0))
            for n in range(8):
                half, b = divmod(n, 4)
                if n < 6:
                    sp.wait_ge(out_copied, n + 1)
                else:
                    sp.wait_ge(init_out, KT + 3 + n - 5)
                sp.dma_start(out[0, b * P:(b + 1) * P, half * T:(half + 1) * T],
                             xrow[:, b * D + half * T:b * D + (half + 1) * T]).then_inc(stored, 16)
            sp.wait_ge(stored, 16 * 8)

        @block.gpsimd
        def _(pool):
            ch = Chain(pool, pool_self)
            gp = nc.gpsimd

            nt = [0]

            def const(buf, src):
                pool.dma_start(buf, src).then_inc(tables, 16)
                nt[0] += 16
                return nt[0]

            const(base[:, :], A["c_base"])
            for b in range(4):
                const(xrow[:, b * D:(b + 1) * D], A["x"][0, b * P:(b + 1) * P, :])
            ch.mark(gp.memset(epsc, EPS))

            def add_squares(name):
                n = None
                for t in range(1, KT - 1):
                    pool.wait_ge(squared, SQUARES[name] + t + 1)
                    if n:
                        ch.wait(n)
                    ins = gp.tensor_tensor(tile(sq, 0), tile(sq, 0), tile(sq, t), ALU.add)
                    if t < KT - 2:
                        n = ch.mark(ins)
                ins.then_inc(sq_added, 1)

            add_squares("pre0")
            for l in range(2):
                if l == 0:
                    pool.wait_ge(init_out, 3 + 8)
                else:
                    pool.wait_ge(w_used, FIRST[f"c_qkv{l}"])
                    pool.wait_ge(mid_lo, 2 + FT * l)
                pool.wait_ge(tables, nt[0])
                pool.wait_ge(tables, const(cmask[:, :], A["c_cmask"]))
                for hp in range(4):
                    if hp >= 2:
                        pool.wait_ge(maxed, STEPS[f"C{l}"] + 8 * (hp - 1))
                    for s in range(2):
                        for half in range(2):
                            src = bass.AP(tensor=A["rpbp"].tensor, ap=[[1, GRID], [31, 14], [1, GRID]],
                                          offset=RPB_PAD + ((l * 8 + 2 * hp + s) * 15 + half) * 31 + 15 - 63)
                            pool.dma_start(e2[hp % 2][64 * half:64 * half + 64, s * E2C:(s + 1) * E2C].rearrange(
                                "p (r k) -> p r k", k=GRID), src).then_inc(e2_loaded[hp % 2], 16)
                    pool.wait_ge(e2_loaded[hp % 2], 64 * (2 * l + hp // 2 + 1))
                    v = e2[hp % 2][:, :].rearrange("p (r k) -> p r k", k=GRID)
                    m = cmask[:, :].rearrange("p (o k) -> p o k", o=1).broadcast_to([P, 28, GRID])
                    gp.tensor_tensor(v, v, m, ALU.add).then_inc(e2_ready, 1)
                pool.wait_ge(y_lo, PAIRS[f"C{l}"] + 4)
                const(rope[:, :], A["c_rope"])
                const(pw[:, :].rearrange("p (g d) -> p g d", g=4), A["w_pool"][l].rearrange("g c d -> c g d"))
                k = const(edge[:, :], A["c_edge"])
                W = T + 2 * PAD
                for g in range(4):
                    for a, b in ((0, PAD), (T + PAD, W)):
                        n = ch.mark(gp.memset(pu[:, g * W + a:g * W + b], 0.0))
                pool.wait_ge(tables, k)
                for g, w in enumerate(POOL_WINDOWS):
                    pool.wait_ge(pu_in, 2 * l + g // 2 + 1)
                    if g:
                        pool.wait_ge(pooled, 4 * l + g)
                    ch.wait(n)
                    u = pu[:, g * W:(g + 1) * W]
                    n = ch.mark(gp.tensor_tensor(win[0][:, 1:W], u[:, 0:W - 1], u[:, 1:W], ALU.add))
                    have, cur, lo = 2, 0, 1
                    while have < w:
                        ch.wait(n)
                        s = have // 2
                        lo += s
                        hi = W - lo + 1
                        n = ch.mark(gp.tensor_tensor(win[1 - cur][:, lo:hi], win[cur][:, lo - s:hi - s],
                                                     win[cur][:, lo + s:hi + s], ALU.add))
                        have, cur = 2 * have, 1 - cur
                    ch.wait(n)
                    e = edge[:, g * 2 * PAD:(g + 1) * 2 * PAD]
                    ch.mark(gp.tensor_tensor(win[cur][:, PAD:2 * PAD], win[cur][:, PAD:2 * PAD], e[:, 0:PAD], ALU.mult))
                    n = ch.mark(gp.tensor_tensor(win[cur][:, T:T + PAD], win[cur][:, T:T + PAD], e[:, PAD:2 * PAD], ALU.mult))
                    ch.wait(n)
                    mean = win[cur][:, PAD:PAD + T]
                    ch.link(gp.tensor_scalar(mean, mean, 1.0 / w, None, ALU.mult))
                    gp.tensor_tensor(u[:, PAD:PAD + T], mean, u[:, PAD:PAD + T], ALU.subtract).then_inc(pooled, 1)
                for name in (f"post{2 * l}", f"pre{2 * l + 1}", f"post{2 * l + 1}", f"pre{2 * l + 2}"):
                    add_squares(name)
            for name in ("ln_var", "post4", "pre5", "post5", "pre6"):
                add_squares(name)
            pool.wait_ge(w_used, FIRST["d_qkv"])
            pool.wait_ge(mid_lo, 2 + 3 * FT)
            const(dmask[:, :], A["c_dmask"])
            for name in ("post6", "pre7", "post7"):
                add_squares(name)

        @block.scalar
        def _(act):
            ch = Chain(act, act_self)
            sc = nc.scalar

            def hi(c, i=None, per=0):
                cc, slot = (c, c % 2) if i is None else (i * per + c, c % 2)
                act.wait_ge(w_used, cc + 1)
                if isinstance(cc, int) and cc + 2 >= CHUNKS:
                    return
                act.wait_ge(w_loaded[slot], (cc // 2 + 2) * 16 if i is None else i * (per * 8) + (c // 2 + 2) * 16)
                sc.activation(whi[slot][:, :], wraw[slot][:, :], ACT.Copy).then_inc(w_hi, 1)

            def split_hi(name, src, dst, ready, n=KT):
                for t in range(n):
                    ready(t)
                    sc.activation(dst(t), src(t), ACT.Copy).then_inc(h_hi, 1)

            def root(name):
                m = NORM[name]
                if m == 0:
                    act.wait_ge(pool_self, 1)
                sc.activation(small[:, 19:20], epsc, ACT.Sqrt)
                act.wait_ge(summed, m + 1)
                sc.activation(roots, bank(MEAN_BANK(name))[:, 0:4], ACT.Sqrt, bias=epsc).then_inc(rooted, 1)

            def h_split(name, dsth, view=lambda a: a):
                for t in range(KT):
                    act.wait_ge(h_tmp, SCALED[name] + t + 1)
                    sc.activation(tile(dsth, t), trio[t % 3], ACT.Copy).then_inc(h_hi, 1)

            def squares_of_x(name):
                for t in range(KT):
                    if name == "pre0":
                        act.wait_ge(init_out, t + 1)
                    else:
                        act.wait_ge(x_new, KT * (int(name[3:]) - 1) + t + 1)
                    sc.activation(tile(sq, t), tile(x, t), ACT.Square).then_inc(squared, 1)

            def pre(h, second=None):
                name = f"pre{h}"
                squares_of_x(name)
                for c in range(2 if h == 0 else 0):
                    act.wait_ge(w_loaded[c], 16)
                    sc.activation(whi[c][:, :], wraw[c][:, :], ACT.Copy).then_inc(w_hi, 1)
                root(name)
                h_split(name, hh)
                if second:
                    h_split("hq", qh)

            def attention(kind, n0, count, width, pbuf, from_psum, extra):
                for n in range(count + 3):
                    if n < count:
                        s = (n0 + n) % SLOTS
                        act.wait_ge(maxed, n0 + n + 1)
                        if n >= SLOTS:
                            act.wait_ge(turned, n0 + n - SLOTS + 1)
                        q = (n0 + n) % 4
                        src = from_psum((n0 + n) % 2) if from_psum else pbuf[:, s * width:(s + 1) * width]
                        sc.activation(pbuf[:, s * width:(s + 1) * width], src, ACT.Exp, bias=small[:, q:q + 1],
                                      scale={"A": 0.125, "C": 1.0, "D": SD}[kind],
                                      accum_out=small[:, 8 + q:9 + q]).then_inc(probs, 1)
                    if n in extra:
                        extra[n]()
                    if 1 <= n <= count:
                        m = n0 + n - 1
                        act.wait_ge(turned, m + 1)
                        if n >= 3:
                            act.wait_ge(weighted, m - 1)
                        src = bank(4, 2)[:, 0:768] if kind == "D" else bank(2 + m % 2)
                        sc.activation(scratch[:, (m % 2) * width:(m % 2) * width + width], src,
                                      ACT.Copy).then_inc(pt_ready, 1)
                    if kind != "D" and n >= 10 and (n - 10) % 8 == 0:
                        y_round(n0, (n - 10) // 8, 8 if kind == "C" else 0)

            def y_round(n0, hp, t0):
                act.wait_ge(weighted, n0 + 8 * hp + 8)
                src, dst = bank(4 + hp % 2), tile(yh, t0 + hp)
                if t0:
                    src, dst = backward(src), by4(dst)
                sc.activation(dst, src, ACT.Copy).then_inc(y_hi, 1)

            def out_rows(f, extra_bias=None, view=lambda a: a):
                c = FIRST[f"out{f}"]
                for j in range(4):
                    if j < 3:
                        hi(c + j)
                    for m in range(2):
                        t = 2 * j + m
                        if j == 3:
                            act.wait_ge(*((tile_done, 7 * f + 1) if m == 0 else (w_used, c + 4)))
                        b = {"bias": col(extra_bias, t)} if extra_bias else {}
                        sc.activation(view(tile(sq, t)), by4(bank(out_bank(f, j) + m)) if f == 3 else bank(out_bank(f, j) + m),
                                      ACT.Square, **b).then_inc(squared, 1)
                root(f"post{2 * f}")
                hi(c + 3)

            def ffn(f):
                fn = ACT.Gelu_apprx_tanh if f < 2 else ACT.Silu
                _, _, l, cw, cb = FFN[f]
                centre = 1 if f < 2 else 2
                c = FIRST[f"up{f}"]
                m0 = FT * f
                with act.Fori(0, FT // 2) as i:
                    for s, acc in enumerate((accv, accg)):
                        hi(c + s, i, 2)
                        for m in range(2):
                            if s == 0:
                                act.wait_ge(mid_lo, i * 2 + (m0 + m + 1))
                            r = i * 2 + (s * FT + m)
                            sc.activation(tile(acc, m), bank(2 * s + m), ACT.Identity,
                                          bias=col(cb, r + 2 * FT * l),
                                          scale=col(cw, r + 2 * FT * (3 * l + centre))).then_inc(affine, 1)
                    for m in range(2):
                        act.wait_ge(conv_done, i * 4 + (4 + 2 * m0 + 2 + m + 1))
                        sc.activation(tile(accg, m), tile(accg, m), fn).then_inc(acted, 1)
                    for m in range(2):
                        act.wait_ge(product, i * 2 + (m0 + m + 1))
                        sc.activation(tile(midh, i * 2 + m), tile(accv, m), ACT.Copy).then_inc(mid_hi, 1)
                c = FIRST[f"down{f}"]
                for half in range(2):
                    for j in range(5):
                        hi(c + 6 * half + j)
                    for t in range(4):
                        act.wait_ge(*((tile_done, 7 * f + 3 * half + t + 2) if t < 3 else (w_used, c + 6 * half + 6)))
                        sc.activation(tile(sq, 4 * half + t), bank(4 * (1 - half) + t), ACT.Square).then_inc(squared, 1)
                    if half == 0:
                        hi(c + 5)
                root(f"post{2 * f + 1}")
                hi(c + 11)

            for dst, src in param_loads[1::2]:
                act.dma_start(dst, src).then_inc(init_in[1], 16)
            pre(0)
            for l in range(2):
                c = FIRST[f"c_qkv{l}"]
                for j in range(5):
                    hi(c + j)
                attention("C", STEPS[f"C{l}"], 32, T, pC, None, {1: lambda c=c: hi(c + 5)})
                c = FIRST[f"a_qkv{l}"]
                for j in range(3):
                    hi(c + j)
                    for m in range(2 if j < 2 else 1):
                        t = 5 * l + 2 * j + m
                        if t >= 2:
                            act.wait_ge(head_sum, t - 1)
                        sc.activation(tmp[t % 2], bank(2 * (j % 2) + m), ACT.Square).then_inc(head_sq, 1)
                    for m in range(2 if j < 2 else 1):
                        t = 5 * l + 2 * j + m
                        act.wait_ge(head_sum, t + 1)
                        if t >= 1:
                            act.wait_ge(head_scaled, t)
                        sc.activation(std, bank(6), ACT.Sqrt, bias=epsc).then_inc(head_std, 1)
                c = FIRST[f"pu{l}"]
                W = T + 2 * PAD
                for j in range(2):
                    hi(c + j)
                    sc.activation(pu[:, 2 * j * W:2 * (j + 1) * W].rearrange("p (m w) -> p m w", m=2)[:, :, PAD:PAD + T],
                                  bank(2 * ((j + 1) % 2), 2).rearrange("p (m w) -> p m w", m=2), ACT.Copy).then_inc(pu_in, 1)

                def pooled_hi(g, l=l):
                    act.wait_ge(pool_out, 4 * l + g + 1)
                    sc.activation(tile(yh, 4 + g), bank(6 + g % 2), ACT.Copy, scale=col("pool_scale", 4 * l + g)).then_inc(pool_hi, 1)

                attention("A", STEPS[f"A{l}"], 32, T, pA, lambda s: bank(s),
                          {n + 1: lambda g=g: pooled_hi(g) for g, n in enumerate(POOL_STEPS)})
                c = FIRST[f"merge{l}"]
                d = DRAINS[f"merge{l}"]

                def gate(n, g, j, c=c, d=d):
                    hi(c + 3 * g + j, n, 6)
                    act.wait_ge(drained, n * 6 + (2 + d + 3 * g + j + 1))
                    sc.activation(tile(gates, 2 * j, 2), tile(gates, 2 * j, 2), ACT.Sigmoid).then_inc(gate_sig, 1)

                with act.Fori(0, 2) as n:
                    for g in range(2):
                        for j in range(2):
                            gate(n, g, j)
                        hi(c + 3 * g + 2, n, 6)
                for g in range(2):
                    for j in range(2):
                        gate(2, g, j)
                        if g == 1 and j == 0:
                            for t in range(4):
                                act.wait_ge(merged, 9 * l + 5)
                                sc.activation(tile(yh, t), tile(mg, t), ACT.Copy).then_inc(h_hi, 1)
                    if g == 0:
                        hi(c + 14)
                for t in range(4, KT):
                    act.wait_ge(merged, 9 * l + 5 + t - 3)
                    sc.activation(tile(yh, t), tile(mg, t), ACT.Copy).then_inc(h_hi, 1)
                hi(c + 17)
                out_rows(l)
                pre(2 * l + 1)
                ffn(l)
                pre(2 * l + 2)
            def tap_diagonals(j):
                if j >= 2:
                    act.wait_ge(tapped, 2 * (j - 1))
                for m in range(2):
                    t = 2 * j + m
                    for i in range(PE_TAPS):
                        at = ((t % 4) * PE_TAPS + i) * P
                        ins = sc.activation(tapd[:, at:at + P], ident, ACT.Copy, scale=col("cm_dw_2", 8 * (TAPS - PE_TAPS + i) + t))
                    ins.then_inc(taps_in, 1)

            c = FIRST["cm_in"]
            for j in range(4):
                hi(c + 2 * j)
                hi(c + 2 * j + 1)
                for m in range(2):
                    act.wait_ge(drained, 2 + DRAINS["cm_in"] + 2 * j)
                    sc.activation(tmp[m], bank(2 * ((c + 1) % 2) + m), ACT.Sigmoid, bias=col("cm_b_in_2", 8 + 2 * j + m)).then_inc(u_sig, 1)
                tap_diagonals(j)
            for t in range(KT):
                act.wait_ge(centred, t + 1)
                sc.activation(tile(sq, t), tile(vb, t), ACT.Square).then_inc(squared, 1)
            root("ln_var")
            for t in range(KT):
                act.wait_ge(ln_scaled, t + 1)
                ch.link(sc.activation(tile(vb, t), tile(vb, t), ACT.Silu, scale=col("cm_ln_g_2", t), bias=col("cm_ln_b_2", t)))
                sc.activation(tile(uh, t), tile(vb, t), ACT.Copy).then_inc(h_hi, 1)
            out_rows(2, "cm_b_out_2")
            pre(5)
            ffn(2)
            pre(6, second=True)
            c = FIRST["d_qkv"]
            for hp in range(4):
                for j in range(8):
                    hi(c + 9 * hp + j)
                attention("D", STEPS["D"] + 8 * hp, 8, 768, pD, None, {1: lambda c=c + 9 * hp + 8: hi(c)})
            for t in range(KT):
                act.wait_ge(y_lo, PAIRS["D"] + t + 1)
                sc.activation(tile(qh, t), tile(yD, t), ACT.Copy).then_inc(h_hi, 1)
            out_rows(3, view=permuted)
            pre(7)
            ffn(3)
            for n in range(6):
                half, b = divmod(n, 4)
                act.wait_ge(init_turn, 11 + n + 1)
                sc.activation(xrow[:, b * D + half * T:b * D + (half + 1) * T], bank(b if half == 0 else 4 + b),
                              ACT.Copy).then_inc(out_copied, 1)

        @block.vector
        def _(dve):
            ch = Chain(dve, dve_self)
            v = nc.vector

            def lo(c, i=None, per=0):
                cc, slot = (c, c % 2) if i is None else (i * per + c, c % 2)
                dve.wait_ge(w_used, cc + 1)
                if isinstance(cc, int) and cc + 2 >= CHUNKS:
                    return
                dve.wait_ge(w_hi, cc + 3)
                v.tensor_tensor(wlo[slot][:, :], wraw[slot][:, :], whi[slot][:, :].bitcast(F32), ALU.subtract).then_inc(w_lo, 1)

            def split_lo(name, src, dsth, dstl, t0=0, t1=KT):
                for t in range(t0, t1):
                    dve.wait_ge(h_hi, SPLIT[name] + t + 1)
                    v.tensor_tensor(tile(dstl, t), tile(src, t), tile(dsth, t).bitcast(F32), ALU.subtract).then_inc(h_lo, 1)

            def rstd(name):
                n = SQUARES[name] // 8 + 1
                dve.wait_ge(rooted, n)
                ch.link(v.reciprocal(rroots, roots))
                for b in range(4):
                    ins = v.tensor_scalar(std[:, b * P:(b + 1) * P], ident, rroots[:, b:b + 1], float(D), ALU.mult, ALU.mult)
                ins.then_inc(diagonal, 1)
                dve.wait_ge(spread, n)
                return bank(MEAN_BANK(name))

            def post(h):
                rs = rstd(f"post{h}")
                name, l = POST[h]
                for t in range(KT + 1):
                    if t < KT:
                        if t >= 3:
                            dve.wait_ge(x_new, KT * h + t - 2)
                        v.scalar_tensor_tensor(out=trio[t % 3], in0=tile(mix, t), scalar=col(name, KT * l + t), in1=rs,
                                               op0=ALU.mult, op1=ALU.mult).then_inc(x_tmp, 1)
                    if t:
                        dve.wait_ge(x_tmp, KT * h + t)
                        v.tensor_tensor(tile(x, t - 1), tile(x, t - 1), trio[(t - 1) % 3], ALU.add).then_inc(x_new, 1)

            def h_split(name, gain, l, rs, dsth, dstl, permute):
                for t in range(KT + 1):
                    if t < KT:
                        if t >= 3 or name == "hq":
                            dve.wait_ge(h_lo, SPLIT[name] + max(t - 2, 0))
                        a, r, o = tile(x, t), rs, trio[t % 3]
                        if permute:
                            a, r, o = permuted(a), permuted(r), by4(o)
                        v.scalar_tensor_tensor(out=o, in0=a, scalar=col(gain, KT * l + t), in1=r,
                                               op0=ALU.mult, op1=ALU.mult).then_inc(h_tmp, 1)
                    if t >= 1:
                        dve.wait_ge(h_hi, SPLIT[name] + t)
                        v.tensor_tensor(tile(dstl, t - 1), trio[(t - 1) % 3], tile(dsth, t - 1).bitcast(F32),
                                        ALU.subtract).then_inc(h_lo, 1)

            def pre(h):
                rs = rstd(f"pre{h}")
                h_split(f"pre{h}", *PRE[h], rs, hh, hl, h == 6)
                if h == 6:
                    h_split("hq", "mix_pre_g_2", 1, rs, qh, ql, True)

            def attention(kind, n0, count, width, pbuf, scores_in, pair_out, extra):
                per = 4 if kind == "D" else 8

                def divide(g):
                    q, s = g % 4, g % SLOTS
                    dve.wait_ge(probs, g + 1)
                    ch.link(v.reciprocal(small[:, 12 + q:13 + q], small[:, 8 + q:9 + q]))
                    p = pbuf[:, s * width:s * width + width]
                    v.tensor_scalar(p, p, small[:, 12 + q:13 + q], None, ALU.mult).then_inc(scaled, 1)

                for n in range(count + 4):
                    if n < count:
                        g, q, s = n0 + n, (n0 + n) % 4, (n0 + n) % SLOTS
                        dve.wait_ge(scored, g + 1)
                        m = ch.mark(scores_in(n, s, q))
                        ch.wait(m)
                        v.tensor_scalar(small[:, q:q + 1], small[:, 4 + q:5 + q], {"A": -0.125, "C": -1.0, "D": -SD}[kind],
                                        None, ALU.mult).then_inc(maxed, 1)
                    if 1 <= n < count + 1 and not (n == 2 and 1 in extra):
                        divide(n0 + n - 1)
                    if n == 1 and n in extra:
                        divide(n0 + 1)
                    if n in extra:
                        extra[n]()
                    if n >= per + 3 and (n - 3) % per == 0:
                        pair_out((n - 3) // per - 1)

            def y_rest(kind, l, t0):
                def rest(hp):
                    dve.wait_ge(y_hi, PAIRS[f"{kind}{l}"] + hp + 1)
                    src, h, dst = bank(4 + hp % 2), tile(yh, t0 + hp).bitcast(F32), tile(yl, t0 + hp)
                    if t0:
                        src, h, dst = backward(src), by4(h), by4(dst)
                    v.tensor_tensor(dst, src, h, ALU.subtract).then_inc(y_lo, 1)
                return rest

            def ffn(f):
                c = FIRST[f"up{f}"]
                m0 = FT * f
                _, _, l, cw, cb = FFN[f]
                taps = [(0, (1, T), (0, T - 1)), (2, (0, T - 1), (1, T))] if f < 2 else \
                       [(1, (1, T), (0, T - 1)), (0, (2, T), (0, T - 2))]
                per = 4
                with dve.Fori(0, FT // 2) as i:
                    start = ch.n
                    ch.shift = i * per
                    for s, acc in enumerate((accv, accg)):
                        lo(c + s, i, 2)
                        first = []
                        for n, (k, (o0, o1), (i0, i1)) in enumerate(taps):
                            for m in range(2):
                                r = i * 2 + (s * FT + m + 2 * FT * (3 * l + k))
                                if n == 0:
                                    dve.wait_ge(affine, i * 4 + (2 * m0 + 2 * s + m + 1))
                                else:
                                    ch.wait(first[m])
                                ins = v.scalar_tensor_tensor(
                                    out=tile(acc, m)[:, o0:o1], in0=bank(2 * s + m)[:, i0:i1], scalar=col(cw, r),
                                    in1=tile(acc, m)[:, o0:o1], op0=ALU.mult, op1=ALU.add)
                                if n == 0:
                                    first.append(ch.mark(ins))
                                else:
                                    ins.then_inc(conv_done, 1)
                    for m in range(2):
                        dve.wait_ge(acted, i * 2 + (m0 + m + 1))
                        v.tensor_tensor(tile(accv, m), tile(accg, m), tile(accv, m), ALU.mult).then_inc(product, 1)
                    for m in range(2):
                        dve.wait_ge(mid_hi, i * 2 + (m0 + m + 1))
                        v.tensor_tensor(tile(midl, i * 2 + m), tile(accv, m), tile(midh, i * 2 + m).bitcast(F32),
                                        ALU.subtract).then_inc(mid_lo, 1)
                    assert ch.n - start == per
                ch.shift = 0
                ch.n += per * (FT // 2 - 1)
                c = FIRST[f"down{f}"]
                for half in range(2):
                    for j in range(5):
                        lo(c + 6 * half + j)
                    if half == 0:
                        lo(c + 5)
                    for t in range(4):
                        dve.wait_ge(squared, SQUARES[f"post{2 * f + 1}"] + 4 * half + t + 1)
                        ins = v.tensor_copy(tile(mix, 4 * half + t), bank(4 * (1 - half) + t))
                    ins.then_inc(drained, 6)
                post(2 * f + 1)
                lo(c + 11)

            def out_rows(f):
                c = FIRST[f"out{f}"]
                for j in range(4):
                    if j < 3:
                        lo(c + j)
                    for m in range(2):
                        t, b = 2 * j + m, bank(out_bank(f, j) + m)
                        dve.wait_ge(squared, SQUARES[f"post{2 * f}"] + t + 1)
                        if f == 2:
                            ins = v.tensor_scalar(tile(mix, t), b, col("cm_b_out_2", t), None, ALU.add)
                        elif f == 3:
                            ins = v.tensor_copy(permuted(tile(mix, t)), by4(b))
                        else:
                            ins = v.tensor_copy(tile(mix, t), b)
                    ins.then_inc(drained, 1)
                post(2 * f)
                lo(c + 3)

            v.memset(small[:, 16:17], 0.0).then_inc(drained, 2)
            v.memset(small[:, 17:18], 0.0).then_inc(conv_done, 4)
            v.memset(small[:, 18:19], 0.0).then_inc(mid_lo, 2)
            for t in range(KT):
                dve.wait_ge(init_turn, t + 1)
                v.tensor_copy(tile(x, t), bank(t % 4)).then_inc(init_out, 1)
            for r in range(3):
                n = min(4 * P, ROWS_ALL - 4 * r * P)
                dve.wait_ge(init_turn, KT + r + 1)
                v.tensor_copy(pvec[:, 4 * r * P:4 * r * P + n], bank((4, 0, 7)[r])[:, 0:n]).then_inc(init_out, 1)
            dve.wait_ge(init_out, KT + 3)
            for c in range(2):
                dve.wait_ge(w_hi, c + 1)
                v.tensor_tensor(wlo[c][:, :], wraw[c][:, :], whi[c][:, :].bitcast(F32), ALU.subtract).then_inc(w_lo, 1)
            pre(0)
            for l in range(2):
                c = FIRST[f"c_qkv{l}"]

                def qkv_out(j, c=c):
                    lo(c + j)
                    src = bank(2 * ((c + j) % 2) if j < 4 else (6, 4)[j - 4], 2)
                    if j < 2:
                        ins = v.tensor_scalar(tile(qC, 2 * j, 2).rearrange("p (b q) -> p b q", q=P),
                                              src.rearrange("p (b q) -> p b q", q=P)[:, :, ::-1], 0.125, None, ALU.mult)
                    elif j < 4:
                        ins = v.tensor_copy(tile(kC, 2 * j - 4, 2), src)
                    else:
                        ins = v.tensor_copy(vC[:, :].rearrange("p (b n) -> p b n", b=4)[:, :, CW * (j - 4):CW * (j - 3)],
                                            src.rearrange("p (b n) -> p b n", b=4))
                    ins.then_inc(drained, 1)

                for j in range(5):
                    qkv_out(j)

                def scores_c(n, s, q, l=l):
                    h, b = steps_of("C")[n]
                    hp = h // 2
                    dve.wait_ge(e2_ready, 4 * l + hp + 1)
                    if n >= SLOTS:
                        dve.wait_ge(turned, STEPS[f"C{l}"] + n - SLOTS + 1)
                    off = (h % 2) * E2C + (6 - 2 * b) * GRID
                    return v.tensor_tensor_reduce(pC[:, s * T:(s + 1) * T], bank(n % 2), e2[hp % 2][:, off:off + T], 1.0,
                                                  2 * NEG, ALU.add, ALU.max, small[:, 4 + q:5 + q])

                attention("C", STEPS[f"C{l}"], 32, T, pC, scores_c, y_rest("C", l, 8), {1: lambda f=qkv_out: f(5)})

                def rotate(t):
                    dst = tile(qA, t) if t < 4 else tile(kA, t - 4)
                    n = 5 * l + t
                    dve.wait_ge(head_rot, n + 1)
                    dve.wait_ge(tables, 16 * (5 + 4 * (l + 1)))
                    o = pA[:, (n % 2) * T:(n % 2) * T + T]
                    v.tensor_tensor(o, bank(5 + 2 * (n % 2)), rope[:, T:2 * T], ALU.mult)
                    ch.link(v.tensor_tensor(dst, dst, rope[:, 0:T], ALU.mult))
                    v.tensor_tensor(dst, dst, o, ALU.add).then_inc(qk_ready, 1)

                c = FIRST[f"a_qkv{l}"]
                for j in range(3):
                    lo(c + j)
                    s = j % 2
                    dve.wait_ge(head_sq, 5 * l + min(2 * j + 2, 5))
                    if j < 2:
                        ins = v.tensor_copy(tile(qA, 2 * j, 2), bank(2 * s, 2))
                    else:
                        v.tensor_copy(tile(kA, 0), bank(2 * s))
                        ins = v.tensor_copy(vA[:, :], bank(4))
                    ins.then_inc(drained, 1)
                    for m in range(2 if j < 2 else 1):
                        t = 2 * j + m
                        n = 5 * l + t
                        dst = tile(qA, t) if t < 4 else tile(kA, t - 4)
                        dve.wait_ge(head_std, n + 1)
                        ch.link(v.reciprocal(std, std))
                        v.scalar_tensor_tensor(out=dst, in0=dst, scalar=col("qkg", l if t < 4 else 2 + l), in1=std,
                                               op0=ALU.mult, op1=ALU.mult).then_inc(head_scaled, 1)
                rotate(0)
                rotate(1)
                c = FIRST[f"pu{l}"]
                lo(c)
                dve.wait_ge(pu_in, 2 * l + 1)
                v.memset(small[:, 16:17], 0.0).then_inc(drained, 1)
                rotate(2)
                rotate(3)
                lo(c + 1)
                dve.wait_ge(pu_in, 2 * l + 2)
                v.memset(small[:, 16:17], 0.0).then_inc(drained, 1)
                rotate(4)
                dve.wait_ge(swapped, l + 1)
                v.tensor_copy(tile(kA, 1), bank(4)).then_inc(qk_ready, 1)

                def scores_a(n, s, q):
                    return v.tensor_reduce(small[:, 4 + q:5 + q], bank(n % 2), AX.X, ALU.max)

                def pooled_lo(g, l=l):
                    dve.wait_ge(pool_hi, 4 * l + g + 1)
                    v.scalar_tensor_tensor(out=tile(yl, 4 + g), in0=bank(6 + g % 2), scalar=col("pool_scale", 4 * l + g),
                                           in1=tile(yh, 4 + g).bitcast(F32), op0=ALU.mult, op1=ALU.subtract).then_inc(pool_lo, 1)

                attention("A", STEPS[f"A{l}"], 32, T, pA, scores_a, y_rest("A", l, 0),
                          {n + 2: lambda g=g: pooled_lo(g) for g, n in enumerate(POOL_STEPS)})
                cleared = ch.mark(v.memset(mg[:, :], 0.0))
                c = FIRST[f"merge{l}"]
                d = DRAINS[f"merge{l}"]

                def gate(n, g, j, l=l, c=c):
                    lo(c + 3 * g + j, n, 6)
                    for m in range(2):
                        ins = v.tensor_scalar(tile(gates, 2 * j + m), bank(4 + 2 * j + m),
                                              col("b_gate", n * 8 + (24 * l + 4 * g + 2 * j + m)), None, ALU.add)
                    ins.then_inc(drained, 1)

                def weighted_sum(n, g, l=l, c=c, d=d):
                    lo(c + 3 * g + 2, n, 6)
                    dve.wait_ge(gate_sig, n * 4 + (12 * l + 2 * g + 2))
                    v.tensor_tensor(gates[:, :], gates[:, :], bank(0, 4), ALU.mult).then_inc(drained, 1)
                    dve.wait_ge(drained, n * 6 + (2 + d + 3 * g + 3))
                    ch.wait(cleared)
                    v.tensor_tensor(tile(mg, 4 * g, 4), tile(mg, 4 * g, 4), gates[:, :], ALU.add).then_inc(merged, 1)
                    dve.wait_ge(merged, n * 2 + (9 * l + g + 1))

                with dve.Fori(0, 2) as n:
                    for g in range(2):
                        for j in range(2):
                            gate(n, g, j)
                        weighted_sum(n, g)
                for j in range(2):
                    gate(2, 0, j)
                weighted_sum(2, 0)
                gate(2, 1, 0)
                split_lo(f"mg{l}", mg, yh, yl, 0, 4)
                gate(2, 1, 1)
                dve.wait_ge(w_used, c + 18)
                dve.wait_ge(gate_sig, 12 * (l + 1))
                done = []
                for m in range(5):
                    if m < 4:
                        ins = v.tensor_tensor(tile(gates, m), tile(gates, m), bank(m), ALU.mult)
                        done.append(ch.mark(ins))
                    if m:
                        ch.wait(done[m - 1])
                        v.tensor_tensor(tile(mg, 3 + m), tile(mg, 3 + m), tile(gates, m - 1), ALU.add).then_inc(merged, 1)
                v.memset(small[:, 16:17], 0.0).then_inc(drained, 1)
                split_lo(f"mg{l}", mg, yh, yl, 4, KT)
                lo(c + 17)
                out_rows(l)
                pre(2 * l + 1)
                ffn(l)
                pre(2 * l + 2)
            last = [0, 0]

            def add_tapped(j):
                for m in range(2):
                    ch.wait(last[m])
                    dve.wait_ge(tapped, 2 * j + m + 1)
                    v.tensor_tensor(tile(vb, 2 * j + m), tile(vb, 2 * j + m), bank(4 + m), ALU.add).then_inc(convolved, 1)

            c = FIRST["cm_in"]
            v.memset(ub[:, :].rearrange("p (t w) -> p t w", t=KT)[:, :, 0:TAPS - 1], 0.0)
            for j in range(4):
                lo(c + 2 * j)
                for m in range(2):
                    t = 2 * j + m
                    ins = v.tensor_scalar(ub[:, t * UW + TAPS - 1:(t + 1) * UW], bank(2 * (c % 2) + m), col("cm_b_in_2", t), None,
                                          ALU.add)
                ins.then_inc(drained, 1)
                lo(c + 2 * j + 1)
                dve.wait_ge(drained, 2 + DRAINS["cm_in"] + 2 * j + 1)
                for m in range(2):
                    t = 2 * j + m
                    dve.wait_ge(u_sig, t + 1)
                    u = ub[:, t * UW + TAPS - 1:(t + 1) * UW]
                    ins = v.tensor_tensor(u, u, tmp[m], ALU.mult)
                    ins.then_inc(u_ready, 1)
                v.memset(small[:, 16:17], 0.0).then_inc(drained, 1)
                if j:
                    add_tapped(j - 1)
                dve.wait_ge(u_ready, 2 * j + 2)
                last = [0, 0]
                for k in range(TAPS - PE_TAPS):
                    for m in range(2):
                        t = 2 * j + m
                        u = ub[:, t * UW + k:t * UW + k + T]
                        if k == 0:
                            last[m] = ch.mark(v.tensor_scalar(tile(vb, t), u, col("cm_dw_2", 8 * k + t), col("cm_dw_b_2", t),
                                                              ALU.mult, ALU.add))
                            continue
                        ch.wait(last[m])
                        last[m] = ch.mark(v.scalar_tensor_tensor(out=tile(vb, t), in0=u, scalar=col("cm_dw_2", 8 * k + t),
                                                                 in1=tile(vb, t), op0=ALU.mult, op1=ALU.add))
            add_tapped(3)
            dve.wait_ge(summed, NORM["ln_mean"] + 1)
            for t in range(KT):
                v.tensor_tensor(tile(vb, t), tile(vb, t), bank(7), ALU.subtract).then_inc(centred, 1)
            rs = rstd("ln_var")
            for t in range(KT):
                v.tensor_tensor(tile(vb, t), tile(vb, t), rs, ALU.mult).then_inc(ln_scaled, 1)
            split_lo("ln", vb, uh, ul)
            out_rows(2)
            pre(5)
            ffn(2)
            pre(6)
            c = FIRST["d_qkv"]
            for hp in range(4):

                def qkv_out(g, j, dst, c):
                    lo(c)
                    src = bank(6 if g == 2 and dst is vD else 2 * (c % 2), 2)
                    if dst is vD:
                        ins = v.tensor_copy(vD[:, :].rearrange("p (b g n) -> p b g n", b=4, g=3)[:, :, g, :],
                                            src.rearrange("p (b n) -> p b n", b=4))
                    else:
                        ins = v.tensor_copy(tile(dst, 2 * g, 2), src)
                    ins.then_inc(drained, 1)

                for g in range(3):
                    for j, dst in enumerate(D_ORDER[g]):
                        if (g, j) != (2, 2):
                            qkv_out(g, j, dst, c)
                            c += 1
                c += 1
                n0 = STEPS["D"] + 8 * hp

                def scores_d(n, s, q, n0=n0):
                    m, b = steps_of("D")[n]
                    if n >= SLOTS:
                        dve.wait_ge(turned, n0 + n - SLOTS + 1)
                    ch.link(v.tensor_tensor(pD[:, s * 768:s * 768 + T], bank(2 * (n % 2)), dmask[:, (3 - b) * P:(7 - b) * P], ALU.add))
                    ch.link(v.tensor_tensor(pD[:, s * 768 + T:s * 768 + 768], bank(2 * (n % 2) + 1)[:, 0:256], dmask[:, 7 * P:9 * P], ALU.add))
                    return v.tensor_reduce(small[:, 4 + q:5 + q], pD[:, s * 768:s * 768 + 768], AX.X, ALU.max)

                def head_out(m, n0=n0, hp=hp):
                    dve.wait_ge(weighted, n0 + 4 * m + 4)
                    v.tensor_copy(tile(yD, 2 * hp + m), bank(6 + m)).then_inc(y_lo, 1)

                dve.wait_ge(tables, 16 * (5 + 8 + 1))
                attention("D", n0, 8, 768, pD, scores_d, head_out,
                          {1: lambda f=qkv_out, c=c - 1: f(2, 2, vD, c)})
            split_lo("y", yD, qh, ql)
            out_rows(3)
            pre(7)
            ffn(3)
            for b in (2, 3):
                dve.wait_ge(init_turn, 11 + 4 + b + 1)
                v.tensor_copy(xrow[:, b * D + T:b * D + 2 * T], bank((4, 5, 6, 0)[b])).then_inc(init_out, 1)

        @block.tensor
        def _(pe):
            te = nc.tensor

            def mm3(out, wh, wl, xh, xl, first, last):
                te.matmul(out, wh, xh, start=first, stop=False)
                te.matmul(out, wh, xl, start=False, stop=False)
                return te.matmul(out, wl, xh, start=False, stop=last)

            def start(c, i=None, per=0, d=None):
                if i is None:
                    pe.wait_ge(w_lo, c + 1)
                    pe.wait_ge(drained, d + 1)
                else:
                    pe.wait_ge(w_lo, i * per + (c + 1))
                    pe.wait_ge(drained, i * per + (d + 1))

            def rows_out(c, bufs, split, bank0=None, tiles=2, signal=None):
                s = c % 2
                b0 = 2 * s if bank0 is None else bank0
                order = ([(m, k) for m in range(tiles) for k in range(KT)] if split is None else
                         [(m, k) for k in range(KT) for m in range(tiles)])
                for m, k in order:
                    if split is not None and m == 0:
                        pe.wait_ge(h_lo, SPLIT[split] + k + 1)
                    wh, wl = (w[s][:, k * CW + m * P:k * CW + (m + 1) * P] for w in (whi, wlo))
                    ins = mm3(bank(b0 + m), wh, wl, tile(bufs[0], k), tile(bufs[1], k), k == 0, k == KT - 1)
                    if signal and m == 0 and k == KT - 1:
                        ins.then_inc(signal, 1)
                return ins

            def tokens_out(c, bufs, c0, n, at, halfway=None):
                s = c % 2
                for b in range(4):
                    if b == 2 and halfway:
                        halfway()
                    o = ps[:, at * T + b * n:at * T + (b + 1) * n]
                    for k in range(KT):
                        xs = [u[:, k * T + b * P:k * T + (b + 1) * P] for u in bufs]
                        wh, wl = (w[s][:, k * CW + c0:k * CW + c0 + n] for w in (whi, wlo))
                        te.matmul(o, xs[0], wh, start=k == 0, stop=False)
                        te.matmul(o, xs[0], wl, start=False, stop=False)
                        ins = te.matmul(o, xs[1], wh, start=False, stop=k == KT - 1)
                return ins

            def keep_warm(n=1):
                for _ in range(n):
                    te.matmul(bank(5), meanm, base[:, 0:T], start=True, stop=True)

            def norm(name, wait=None):
                n, b0 = SQUARES[name] // 8, MEAN_BANK(name)
                for t in (0, KT - 1):
                    pe.wait_ge(*((squared, SQUARES[name] + KT) if t else (sq_added, n + 1)))
                    for b in range(4):
                        at = t * T + b * P
                        ins = te.matmul(bank(b0)[:, b:b + 1], sq[:, at:at + P], meanm[:, 0:1], start=t == b == 0,
                                        stop=t > 0 and b == 3)
                ins.then_inc(summed, 1)
                keep_warm(1)
                pe.wait_ge(diagonal, n + 1)
                te.matmul(bank(b0), meanm, std, start=True, stop=True).then_inc(spread, 1)
                keep_warm(2)

            def out_product(f, bufs, split):
                c, d = FIRST[f"out{f}"], DRAINS[f"out{f}"]
                for j in range(4):
                    start(c + j, d=d + j)
                    rows_out(c + j, bufs, split if j == 0 else None, bank0=out_bank(f, j),
                             signal=tile_done if j == 3 else None).then_inc(w_used, 1)
                keep_warm()
                norm(f"post{2 * f}")

            def pre(h):
                for t in range(KT):
                    if h and t < KT - 1:
                        pe.wait_ge(squared, SQUARES[f"pre{h}"] + t + 1)
                        keep_warm()
                norm(f"pre{h}")

            def ffn(f):
                c, m0 = FIRST[f"up{f}"], FT * f
                pe.wait_ge(drained, 2 + DRAINS[f"up{f}"])
                with pe.Fori(0, FT // 2) as i:
                    for s in range(2):
                        pe.wait_ge(w_lo, i * 2 + (c + s + 1))
                        pe.wait_ge(conv_done, i * 4 + (2 * m0 + 2 * s + 2))
                        rows_out(c + s, (hh, hl), None if s else f"pre{2 * f + 1}", bank0=2 * s).then_inc(w_used, 1)
                c = FIRST[f"down{f}"]
                for half in range(2):
                    if half:
                        pe.wait_ge(conv_done, 4 + 2 * m0 + 2 * FT)
                    for j in range(6):
                        cc = c + 6 * half + j
                        pe.wait_ge(w_lo, cc + 1)
                        ks = range(min(4, FT - 4 * j))
                        if half == 0:
                            order = [(k, t) for k in ks for t in range(4)]
                        else:
                            order = [(k, t) for t in range(4) for k in ks]
                        if half == 0 and j == 5:
                            for k in ks:
                                pe.wait_ge(mid_lo, 2 + m0 + 4 * j + k + 1)
                            order = [(k, t) for t in range(4) for k in ks]
                        for k, t in order:
                            n, at = 4 * j + k, k * 512 + t * P
                            if half == 0 and t == 0:
                                pe.wait_ge(mid_lo, 2 + m0 + n + 1)
                            ins = mm3(bank(4 * (1 - half) + t), whi[cc % 2][:, at:at + P], wlo[cc % 2][:, at:at + P],
                                      tile(midh, n), tile(midl, n), n == 0, n == FT - 1)
                            if n == FT - 1 and t < 3:
                                ins.then_inc(tile_done, 1)
                        ins.then_inc(w_used, 1)
                        if half == 1 and j == 1:
                            pe.wait_ge(drained, 2 + DRAINS[f"down{f}"] + 6)
                keep_warm()
                norm(f"post{2 * f + 1}")

            def attention(kind, n0, count, scores, pbuf, weigh, v_drained=None, behind=None, extra={}):
                blocks, width = (6, 768) if kind == "D" else (4, T)
                for n in range(count + 1):
                    if n < count:
                        g = n0 + n
                        pe.wait_ge(probs if kind == "A" else maxed, g + 1)
                        if n + 2 < count:
                            scores(n + 2, g + 2)
                        pe.wait_ge(scaled, g + 1)
                        back = 1 if kind == "D" else 2
                        if n >= back:
                            pe.wait_ge(pt_ready, g - back + 1)
                        o = bank(4, 2) if kind == "D" else bank(2 + g % 2)
                        for j in range(blocks):
                            at = (g % SLOTS) * width + j * P
                            ins = te.transpose(o[:, j * P:(j + 1) * P], pbuf[:, at:at + P], ident)
                        ins.then_inc(turned, 1)
                    if n in extra:
                        extra[n]()
                    if n == count and behind:
                        behind()
                    if n == 1 and v_drained:
                        pe.wait_ge(drained, v_drained)
                    if n:
                        pe.wait_ge(pt_ready, n0 + n)
                        weigh(n - 1, n0 + n - 1)

            def weigh_pair(kind, l, vbuf):
                def weigh(n, g):
                    h, b = steps_of(kind)[n]
                    hp, r = h // 2, 64 * (h % 2)
                    if n % 8 == 0 and hp >= 2:
                        pe.wait_ge(y_lo, PAIRS[f"{kind}{l}"] + hp - 1)
                    for k in range(4):
                        at = k * 512 + h * 64 if kind == "C" else k * P + 64 * (h // 4)
                        ins = te.matmul(bank(4 + hp % 2)[r:r + 64, b * P:(b + 1) * P], vbuf[:, at:at + 64],
                                        scratch[:, (g % 2) * T + k * P:(g % 2) * T + (k + 1) * P], start=k == 0, stop=k == 3)
                    ins.then_inc(weighted, 1)
                return weigh

            pe.wait_ge(tables, 16 * 5)
            for t in range(KT):
                if t >= 4:
                    pe.wait_ge(init_out, t - 3)
                for b in range(4):
                    ins = te.transpose(bank(t % 4)[:, b * P:(b + 1) * P], xrow[:, b * D + t * P:b * D + (t + 1) * P], ident)
                ins.then_inc(init_turn, 1)
            for i in range(2):
                pe.wait_ge(init_in[i], 16 * len(param_loads[i::2]))
            pe.wait_ge(init_out, 5)
            for r in range(3):
                for j in range(min(4, ROW_TILES - 4 * r)):
                    n = 4 * r + j
                    k = min(P, ROWS_ALL - n * P)
                    ins = te.transpose(bank((4, 0, 7)[r])[:, j * P:j * P + k], prow[0:k, n * P:(n + 1) * P], ident[0:k, 0:k])
                ins.then_inc(init_turn, 1)
            pre(0)
            for l in range(2):
                c, d = FIRST[f"c_qkv{l}"], DRAINS[f"c_qkv{l}"]
                for j in range(5):
                    start(c + j, d=d + j)
                    if j == 0:
                        pe.wait_ge(drained, 2 + d)
                    if j < 4:
                        rows_out(c + j, (hh, hl), f"pre{2 * l}" if j == 0 else None).then_inc(w_used, 1)
                    else:
                        tokens_out(c + j, (hh, hl), 0, CW, 6).then_inc(w_used, 1)

                def scores_c(n, g):
                    h, b = steps_of("C")[n]
                    r, t = 64 * (h % 2), h // 2
                    te.matmul(bank(g % 2), qC[r:r + 64, t * T + b * P:t * T + (b + 1) * P], kC[r:r + 64, t * T:(t + 1) * T],
                              start=True, stop=True).then_inc(scored, 1)

                pe.wait_ge(drained, 2 + d + 4)
                for n in range(2):
                    scores_c(n, STEPS[f"C{l}"] + n)
                start(c + 5, d=d + 5)
                tokens_out(c + 5, (hh, hl), 0, CW, 4).then_inc(w_used, 1)

                def first_a(c=FIRST[f"a_qkv{l}"], d=DRAINS[f"a_qkv{l}"]):
                    start(c, d=d)
                    rows_out(c, (hh, hl), None, bank0=0).then_inc(w_used, 1)

                attention("C", STEPS[f"C{l}"], 32, scores_c, pC, weigh_pair("C", l, vC), v_drained=2 + d + 6, behind=first_a)

                def head_mean(t, l=l):
                    n = 5 * l + t
                    pe.wait_ge(head_sq, n + 1)
                    if t:
                        pe.wait_ge(head_std, n)
                    te.matmul(bank(6), headm, tmp[n % 2], start=True, stop=True).then_inc(head_sum, 1)

                def rotate(t, l=l):
                    n = 5 * l + t
                    pe.wait_ge(head_scaled, n + 1)
                    if t >= 2:
                        pe.wait_ge(qk_ready, 6 * l + t - 1)
                    te.matmul(bank(5 + 2 * (n % 2)), rotm, tile(qA, t) if t < 4 else tile(kA, t - 4), start=True,
                              stop=True).then_inc(head_rot, 1)

                c, d = FIRST[f"a_qkv{l}"], DRAINS[f"a_qkv{l}"]
                for j in range(1, 3):
                    start(c + j, d=d + j)
                    if j < 2:
                        rows_out(c + j, (hh, hl), None, bank0=2).then_inc(w_used, 1)
                    else:
                        pe.wait_ge(y_lo, PAIRS[f"C{l}"] + 4)
                        rows_out(c + j, (hh, hl), None, tiles=1, bank0=0)
                        tokens_out(c + j, (hh, hl), P, P, 4).then_inc(w_used, 1)
                    if j == 1:
                        head_mean(0)
                        head_mean(1)
                for t in range(2, 5):
                    head_mean(t)
                rotate(0)
                rotate(1)
                c, d = FIRST[f"pu{l}"], DRAINS[f"pu{l}"]
                start(c, d=d)
                rows_out(c, (hh, hl), None, bank0=2).then_inc(w_used, 1)
                rotate(2)
                rotate(3)
                start(c + 1, d=d + 1)
                rows_out(c + 1, (hh, hl), None, bank0=0).then_inc(w_used, 1)
                rotate(4)
                pe.wait_ge(qk_ready, 6 * l + 5)
                te.matmul(bank(4), swapm, tile(kA, 0), start=True, stop=True).then_inc(swapped, 1)
                pe.wait_ge(qk_ready, 6 * l + 6)
                pe.wait_ge(drained, 2 + d + 2)

                def scores_a(n, g):
                    h, b = steps_of("A")[n]
                    r, t, kv = 64 * (h % 2), h // 2, int(h % 2 != h // 4)
                    te.matmul(bank(g % 2), qA[r:r + 64, t * T + b * P:t * T + (b + 1) * P], kA[r:r + 64, kv * T:(kv + 1) * T],
                              start=True, stop=True).then_inc(scored, 1)

                def pooled_out(g, l=l):
                    W = T + 2 * PAD
                    pe.wait_ge(pooled, 4 * l + g + 1)
                    if g >= 2:
                        pe.wait_ge(pool_lo, 4 * l + g - 1)
                    te.matmul(bank(6 + g % 2), pw[:, g * P:(g + 1) * P], pu[:, g * W + PAD:g * W + PAD + T], start=True,
                              stop=True).then_inc(pool_out, 1)

                for n in range(2):
                    scores_a(n, STEPS[f"A{l}"] + n)
                attention("A", STEPS[f"A{l}"], 32, scores_a, pA, weigh_pair("A", l, vA),
                          extra={n: lambda g=g: pooled_out(g) for g, n in enumerate(POOL_STEPS)})
                pe.wait_ge(y_lo, PAIRS[f"A{l}"] + 4)
                pe.wait_ge(pool_lo, 4 * l + 4)
                c, d = FIRST[f"merge{l}"], DRAINS[f"merge{l}"]
                with pe.Fori(0, 3) as n:
                    for g in range(2):
                        for j in range(2):
                            start(c + 3 * g + j, n, 6, d + 3 * g + j)
                            rows_out(c + 3 * g + j, (hh, hl), None, bank0=4 + 2 * j).then_inc(w_used, 1)
                        cc = c + 3 * g + 2
                        start(cc, n, 6, d + 3 * g + 2)
                        for t in range(4):
                            for k in range(4):
                                at = k * 512 + t * P
                                ins = mm3(bank(t), whi[cc % 2][:, at:at + P], wlo[cc % 2][:, at:at + P],
                                          tile(yh, n * 4 + k), tile(yl, n * 4 + k), k == 0, k == 3)
                        ins.then_inc(w_used, 1)
                out_product(l, (yh, yl), f"mg{l}")
                pre(2 * l + 1)
                ffn(l)
                pre(2 * l + 2)
            c, d = FIRST["cm_in"], DRAINS["cm_in"]
            def taps(j):
                for m in range(2):
                    t = 2 * j + m
                    pe.wait_ge(taps_in, t + 1)
                    pe.wait_ge(u_ready, t + 1)
                    if j:
                        pe.wait_ge(convolved, t - 1)
                    for i in range(PE_TAPS):
                        at, u0 = ((t % 4) * PE_TAPS + i) * P, t * UW + TAPS - PE_TAPS + i
                        ins = te.matmul(bank(4 + m), tapd[:, at:at + P], ub[:, u0:u0 + T], start=i == 0, stop=i == PE_TAPS - 1)
                    ins.then_inc(tapped, 1)

            def ln_mean(j):
                for t in (2 * j, 2 * j + 1):
                    pe.wait_ge(convolved, t + 1)
                    ins = te.matmul(bank(7), meanm, tile(vb, t), start=t == 0, stop=t == KT - 1)
                if j == 3:
                    ins.then_inc(summed, 1)

            for j in range(4):
                for i in range(2):
                    start(c + 2 * j + i, d=d + 2 * j + i)
                    if j == i == 0:
                        pe.wait_ge(drained, 2 + d)
                    rows_out(c + 2 * j + i, (hh, hl), "pre4" if j == i == 0 else None).then_inc(w_used, 1)
                if j:
                    taps(j - 1)
                if j > 1:
                    ln_mean(j - 2)
            taps(3)
            ln_mean(2)
            ln_mean(3)
            for t in range(KT):
                pe.wait_ge(squared, SQUARES["ln_var"] + t + 1)
                keep_warm()
            norm("ln_var")
            pe.wait_ge(drained, 2 + d + 8)
            out_product(2, (uh, ul), "ln")
            pre(5)
            ffn(2)
            pre(6)
            c, d = FIRST["d_qkv"], DRAINS["d_qkv"]

            def d_chunk(hp, g, j, halfway=None):
                i = 9 * hp + 3 * g + j
                cc, dst = c + i, D_ORDER[g][j]
                start(cc, d=d + i)
                if i == 0:
                    pe.wait_ge(drained, 2 + d)
                if dst is vD:
                    if g == 2:
                        if hp:
                            pe.wait_ge(y_lo, PAIRS["D"] + 2 * hp)
                    tokens_out(cc, (hh, hl), 0, CW, 6 if g == 2 else 2 * (cc % 2), halfway).then_inc(w_used, 1)
                else:
                    bufs, split = ((qh, ql), "hq") if dst is qD else ((hh, hl), "pre6")
                    rows_out(cc, bufs, split if hp == g == 0 else None).then_inc(w_used, 1)

            for hp in range(4):
                def scores_d(n, g, hp=hp):
                    m, b = steps_of("D")[n]

                    def at(buf, i):
                        return buf[:, (2 * i + m) * T + b * P:(2 * i + m) * T + (b + 1) * P]
                    te.matmul(bank(2 * (g % 2)), at(qD, 0), kD[:, m * T:(m + 1) * T], start=True, stop=True)
                    te.matmul(bank(2 * (g % 2) + 1)[:, 0:P], at(qD, 1), at(kD, 1), start=True, stop=True)
                    te.matmul(bank(2 * (g % 2) + 1)[:, P:2 * P], at(qD, 2), at(kD, 2), start=True, stop=True).then_inc(scored, 1)

                def weigh_d(n, g, hp=hp):
                    m, b = steps_of("D")[n]
                    if hp and b == 0:
                        pe.wait_ge(y_lo, PAIRS["D"] + 2 * hp - 1 + m)
                    keys = [(k, 0) for k in range(4)] + [(b, 1), (b, 2)]
                    for j, (k, i) in enumerate(keys):
                        at = k * 768 + i * CW + m * P
                        ins = te.matmul(bank(6 + m)[:, b * P:(b + 1) * P], vD[:, at:at + P],
                                        scratch[:, (g % 2) * 768 + j * P:(g % 2) * 768 + (j + 1) * P], start=j == 0, stop=j == 5)
                    ins.then_inc(weighted, 1)

                def first_scores(hp=hp, scores=scores_d):
                    pe.wait_ge(drained, 2 + d + 9 * hp + 8)
                    for n in range(2):
                        scores(n, STEPS["D"] + 8 * hp + n)

                for g in range(3):
                    for j in range(3):
                        if hp == 0 or g or j:
                            d_chunk(hp, g, j, first_scores if (g, j) == (2, 2) else None)
                attention("D", STEPS["D"] + 8 * hp, 8, scores_d, pD, weigh_d, v_drained=2 + d + 9 * hp + 9,
                          behind=(lambda hp=hp: d_chunk(hp + 1, 0, 0)) if hp < 3 else None)
            out_product(3, (qh, ql), "y")
            pre(7)
            ffn(3)
            for t in range(KT):
                pe.wait_ge(x_new, 7 * KT + t + 1)
                half, j = divmod(t, 4)
                for b in range(4):
                    bk = b if half == 0 else (4, 5, 6, 0)[b]
                    if (t, b) == (4, 3):
                        pe.wait_ge(out_copied, 1)
                    ins = te.transpose(bank(bk)[:, j * P:(j + 1) * P], x[:, t * T + b * P:t * T + (b + 1) * P], ident)
                    if j == 3:
                        ins.then_inc(init_turn, 1)


def kernel(**inputs):
    import numpy as _np
    import concourse.bacc as _bacc
    from concourse import mybir as _mybir
    from concourse.bass_utils import run_bass_kernel_spmd as _run

    nc = _bacc.Bacc("TRN2", target_bir_lowering=False, num_devices=1)
    arrays = {n: _np.ascontiguousarray(a) for n, a in inputs.items() if n != "rpb"}
    arrays["rpbp"] = _np.pad(_np.ascontiguousarray(inputs["rpb"]).reshape(1, -1), ((0, 0), (RPB_PAD, RPB_PAD)))
    arrays.update(host_constants())
    maps, aps = {}, {}
    for n, a in arrays.items():
        maps[f"in_{n}_dram"] = a
        aps[n] = nc.dram_tensor(f"in_{n}_dram", a.shape, _mybir.dt.from_np(a.dtype), kind="ExternalInput").ap()
    out = nc.dram_tensor("out_0_dram", (1, T, D), F32, kind="ExternalOutput").ap()
    build(nc, aps, out)
    r = _run(nc, [maps], core_ids=[0])
    return r.results[0]["out_0_dram"]
```
